# Optimizing a Trainium2 kernel written in Bass

```python
import math
import jax, jax.numpy as jnp
from jax import lax
import numpy as np

D_MODEL = 1024
BATCH = 1
SEQ = 512
DEPTH = 2

DA_HEADS = 4
DA_QK_DIM = 64
DA_V_DIM = 2 * DA_QK_DIM
DA_ROT_DIM = DA_QK_DIM // 4
ROPE_THETA = 500000.0
Q_BLOCK = 128
RET_HEADS = 4
RET_QK_DIM = 32
RET_V_DIM = 2 * RET_QK_DIM
RET_THETA = 10000.0
RET_CHUNK = 128
POOL_GROUPS = 4
POOL_DIM = 64
POOL_WINDOWS = (2, 4, 8, 16)
DA_WIDTH = DA_HEADS * DA_V_DIM
RET_WIDTH = RET_HEADS * RET_V_DIM
POOL_WIDTH = POOL_GROUPS * POOL_DIM
MIX_WIDTH = DA_WIDTH + RET_WIDTH + POOL_WIDTH
SPLIT_SIZES = (DA_HEADS * 2 * DA_QK_DIM, DA_HEADS * 2 * DA_QK_DIM, DA_WIDTH,
               RET_HEADS * RET_QK_DIM, RET_HEADS * RET_QK_DIM, RET_WIDTH, RET_WIDTH,
               POOL_WIDTH)
IN_WIDTH = 2560
D_FF = 2816
CONV_WIDTH = 3
EPS = 1e-6


def rms_norm(x, g):
    xf = x.astype(jnp.float32)
    y = xf * lax.rsqrt(jnp.mean(xf * xf, axis=-1, keepdims=True) + EPS)
    return (y * g).astype(x.dtype)

def rotary(x, pos, rot_dim, theta):
    inv = jnp.float32(theta) ** (-jnp.arange(0, rot_dim, 2, dtype=jnp.float32) / rot_dim)
    ang = pos[:, None] * inv[None, :]
    cos = jnp.cos(ang).astype(x.dtype)
    sin = jnp.sin(ang).astype(x.dtype)
    half = rot_dim // 2
    x1, x2, xp = x[..., :half], x[..., half:rot_dim], x[..., rot_dim:]
    return jnp.concatenate([x1 * cos - x2 * sin, x2 * cos + x1 * sin, xp], axis=-1)

def diff_attention(q, k, v, lq1, lk1, lq2, lk2, subln_g, lam_init):
    B, S, _ = q.shape
    pos = jnp.arange(S, dtype=jnp.float32)
    q = q.reshape(B, S, DA_HEADS, 2, DA_QK_DIM).transpose(0, 2, 3, 1, 4)
    k = k.reshape(B, S, DA_HEADS, 2, DA_QK_DIM).transpose(0, 2, 3, 1, 4)
    q = rotary(q, pos, DA_ROT_DIM, ROPE_THETA)
    k = rotary(k, pos, DA_ROT_DIM, ROPE_THETA)
    v = v.reshape(B, S, DA_HEADS, DA_V_DIM).transpose(0, 2, 1, 3)
    lam = (jnp.exp(jnp.sum(lq1.astype(jnp.float32) * lk1.astype(jnp.float32)))
           - jnp.exp(jnp.sum(lq2.astype(jnp.float32) * lk2.astype(jnp.float32))) + lam_init)
    scale = DA_QK_DIM ** -0.5
    nb = S // Q_BLOCK
    qb = q.reshape(B, DA_HEADS, 2, nb, Q_BLOCK, DA_QK_DIM).transpose(3, 0, 1, 2, 4, 5)
    kpos = jnp.arange(S)

    def block(args):
        q_blk, i = args
        s = jnp.einsum('bhmqd,bhmkd->bhmqk', q_blk, k).astype(jnp.float32) * scale
        qpos = i * Q_BLOCK + jnp.arange(Q_BLOCK)
        mask = kpos[None, :] <= qpos[:, None]
        p = jax.nn.softmax(jnp.where(mask, s, -jnp.inf), axis=-1)
        a = p[:, :, 0] - lam * p[:, :, 1]
        return jnp.einsum('bhqk,bhkd->bhqd', a.astype(v.dtype), v)

    o = lax.map(block, (qb, jnp.arange(nb)))
    o = o.transpose(1, 0, 3, 2, 4).reshape(B, S, DA_HEADS, DA_V_DIM)
    o = rms_norm(o, subln_g) * (1.0 - lam_init)
    return o.reshape(B, S, DA_WIDTH)

def retention(q, k, v, g, ret_g):
    B, S, _ = q.shape
    H, dk, dv, C = RET_HEADS, RET_QK_DIM, RET_V_DIM, RET_CHUNK
    pos = jnp.arange(S, dtype=jnp.float32)
    q = rotary(q.reshape(B, S, H, dk).transpose(0, 2, 1, 3), pos, dk, RET_THETA)
    k = rotary(k.reshape(B, S, H, dk).transpose(0, 2, 1, 3), pos, dk, RET_THETA) * (dk ** -0.5)
    v = v.reshape(B, S, H, dv).transpose(0, 2, 1, 3)
    log_g = jnp.log(1.0 - 2.0 ** (-5.0 - jnp.arange(H, dtype=jnp.float32)))
    idx = jnp.arange(C, dtype=jnp.float32)
    diff = idx[:, None] - idx[None, :]
    decay = jnp.where(diff >= 0, jnp.exp(jnp.maximum(diff, 0.0) * log_g[:, None, None]), 0.0)
    xi = jnp.exp((idx + 1.0) * log_g[:, None])[..., None]
    zeta = jnp.exp((C - 1.0 - idx) * log_g[:, None])[..., None]
    chunk_decay = jnp.exp(C * log_g)[:, None, None]
    nc = S // C

    def to_chunks(t):
        return t.reshape(B, H, nc, C, t.shape[-1]).transpose(2, 0, 1, 3, 4).astype(jnp.float32)

    def step(state, inp):
        qi, ki, vi = inp
        inner = jnp.einsum('bhqd,bhkd->bhqk', qi, ki) * decay
        o = (jnp.einsum('bhqk,bhkv->bhqv', inner, vi)
             + jnp.einsum('bhqd,bhdv->bhqv', qi * xi, state))
        state = state * chunk_decay + jnp.einsum('bhkd,bhkv->bhdv', ki * zeta, vi)
        return state, o

    state0 = jnp.zeros((B, H, dk, dv), jnp.float32)
    _, o = lax.scan(step, state0, (to_chunks(q), to_chunks(k), to_chunks(v)))
    o = o.transpose(1, 0, 3, 2, 4).reshape(B, S, H, dv)
    mu = jnp.mean(o, axis=-1, keepdims=True)
    var = jnp.mean(jnp.square(o - mu), axis=-1, keepdims=True)
    o = (o - mu) * lax.rsqrt(var + EPS) * ret_g.reshape(H, dv)
    return jax.nn.silu(g) * o.reshape(B, S, RET_WIDTH).astype(g.dtype)

def pool_mixer(u, pool_w, pool_scale):
    B, S, _ = u.shape
    ug = u.reshape(B, S, POOL_GROUPS, POOL_DIM).astype(jnp.float32)
    c = jnp.cumsum(ug, axis=1)
    t = jnp.arange(S, dtype=jnp.float32)
    means = []
    for gi, w in enumerate(POOL_WINDOWS):
        cg = c[:, :, gi]
        shifted = jnp.pad(cg, ((0, 0), (w, 0), (0, 0)))[:, :S]
        means.append((cg - shifted) / jnp.minimum(t + 1.0, float(w))[:, None])
    pooled = (jnp.stack(means, axis=2) - ug).astype(u.dtype)
    y = jnp.einsum('bsgp,gpq->bsgq', pooled, pool_w)
    return y.reshape(B, S, POOL_WIDTH) * pool_scale

def conv_mlp(h, w_up, conv_w, conv_b, w_down):
    S = h.shape[1]
    u = h @ w_up
    up = jnp.pad(u, ((0, 0), (CONV_WIDTH - 1, 0), (0, 0)))
    uc = conv_b + sum(conv_w[j] * up[:, j:j + S] for j in range(CONV_WIDTH))
    gate, val = jnp.split(uc, 2, axis=-1)
    return (jax.nn.gelu(gate, approximate=True) * val) @ w_down

def first_inputs(seed: int = 0) -> dict:
    key = jax.random.key(seed)
    ks = jax.random.split(key, 24)
    f32 = jnp.float32

    def nrm(k, shape, scale):
        return jax.random.normal(k, shape, f32) * scale

    def gain(k, shape):
        return 1.0 + 0.05 * jax.random.normal(k, shape, f32)

    L = DEPTH
    return {
        "x": nrm(ks[0], (BATCH, SEQ, D_MODEL), 1.0),
        "norm_mix_pre": gain(ks[1], (L, D_MODEL)),
        "norm_mix_post": gain(ks[2], (L, D_MODEL)),
        "w_in": nrm(ks[3], (L, D_MODEL, IN_WIDTH), D_MODEL ** -0.5),
        "lambda_q1": nrm(ks[4], (L, DA_QK_DIM), 0.1),
        "lambda_k1": nrm(ks[5], (L, DA_QK_DIM), 0.1),
        "lambda_q2": nrm(ks[6], (L, DA_QK_DIM), 0.1),
        "lambda_k2": nrm(ks[7], (L, DA_QK_DIM), 0.1),
        "diff_subln": gain(ks[8], (L, DA_V_DIM)),
        "ret_norm": gain(ks[9], (L, RET_WIDTH)),
        "pool_w": nrm(ks[10], (L, POOL_GROUPS, POOL_DIM, POOL_DIM), POOL_DIM ** -0.5),
        "pool_scale": 0.5 + 0.1 * jax.random.normal(ks[11], (L, POOL_WIDTH), f32),
        "w_out": nrm(ks[12], (L, MIX_WIDTH, D_MODEL), MIX_WIDTH ** -0.5),
        "norm_mlp_pre": gain(ks[13], (L, D_MODEL)),
        "norm_mlp_post": gain(ks[14], (L, D_MODEL)),
        "w_up": nrm(ks[15], (L, D_MODEL, 2 * D_FF), D_MODEL ** -0.5),
        "conv_w": nrm(ks[16], (L, CONV_WIDTH, 2 * D_FF), CONV_WIDTH ** -0.5),
        "conv_b": nrm(ks[17], (L, 2 * D_FF), 0.02),
        "w_down": nrm(ks[18], (L, D_FF, D_MODEL), D_FF ** -0.5),
    }

def first_block(x, norm_mix_pre, norm_mix_post, w_in, lambda_q1, lambda_k1, lambda_q2, lambda_k2,
              diff_subln, ret_norm, pool_w, pool_scale, w_out, norm_mlp_pre, norm_mlp_post,
              w_up, conv_w, conv_b, w_down):
    split_points = []
    acc = 0
    for s in SPLIT_SIZES[:-1]:
        acc += s
        split_points.append(acc)
    for l in range(DEPTH):
        lam_init = 0.8 - 0.6 * math.exp(-0.3 * l)
        h = rms_norm(x, norm_mix_pre[l])
        proj = h @ w_in[l]
        q_da, k_da, v_da, q_r, k_r, v_r, g_r, u_pool = jnp.split(proj, split_points, axis=-1)
        o_da = diff_attention(q_da, k_da, v_da, lambda_q1[l], lambda_k1[l], lambda_q2[l],
                              lambda_k2[l], diff_subln[l], lam_init)
        o_ret = retention(q_r, k_r, v_r, g_r, ret_norm[l])
        o_pool = pool_mixer(u_pool, pool_w[l], pool_scale[l])
        mix = jnp.concatenate([o_da, o_ret, o_pool], axis=-1) @ w_out[l]
        x = x + rms_norm(mix, norm_mix_post[l])
        h = rms_norm(x, norm_mlp_pre[l])
        y = conv_mlp(h, w_up[l], conv_w[l], conv_b[l], w_down[l])
        x = x + rms_norm(y, norm_mlp_post[l])
    return x


HEAD_DIM = 64
N_HEADS_TOTAL = D_MODEL // HEAD_DIM
N_SB_HEADS = N_HEADS_TOTAL // 4
DIL_GROUPS = ((128, 1), (512, 4), (2048, 16))
N_DIL_GROUPS = len(DIL_GROUPS)
HEADS_PER_GROUP = (N_HEADS_TOTAL - N_SB_HEADS) // N_DIL_GROUPS
N_DIL_HEADS = HEADS_PER_GROUP * N_DIL_GROUPS
D_DIL = N_DIL_HEADS * HEAD_DIM
D_DIL_OUT = HEADS_PER_GROUP * HEAD_DIM
D_SB = N_SB_HEADS * HEAD_DIM
D_IN = 3 * D_DIL + 3 * D_SB + 2 * D_MODEL
D_FF_2 = 128 * ((8 * D_MODEL // 3 + 127) // 128)
ROPE_DIM = HEAD_DIM // 4
RMS_EPS = 1e-6


def rms_norm_2(x, gain):
    xf = x.astype(jnp.float32)
    xf = xf * lax.rsqrt(jnp.mean(xf * xf, axis=-1, keepdims=True) + RMS_EPS)
    return (xf * gain.astype(jnp.float32)).astype(x.dtype)

def swiglu(x, w_gate, w_up, w_down):
    return (jax.nn.silu(x @ w_gate) * (x @ w_up)) @ w_down

def rope_tables(seq_len):
    pos = jnp.arange(seq_len, dtype=jnp.float32)
    inv_freq = ROPE_THETA ** (-jnp.arange(0, ROPE_DIM, 2, dtype=jnp.float32) / ROPE_DIM)
    ang = pos[:, None] * inv_freq[None, :]
    return jnp.cos(ang), jnp.sin(ang)

def apply_partial_rope(x, cos, sin):
    half = ROPE_DIM // 2
    x1 = x[..., :half]
    x2 = x[..., half:ROPE_DIM]
    c = cos.astype(x.dtype)
    s = sin.astype(x.dtype)
    return jnp.concatenate([x1 * c - x2 * s, x2 * c + x1 * s, x[..., ROPE_DIM:]], axis=-1)

def dilated_window_attention(q, k, v, window, dilation):
    B, H, T, dh = q.shape
    span = window // dilation
    unit = span * dilation
    t_pad = -(-T // unit) * unit
    n_sub = t_pad // dilation
    n_blk = n_sub // span

    def to_blocks(a):
        a = jnp.pad(a, ((0, 0), (0, 0), (0, t_pad - T), (0, 0)))
        a = a.reshape(B, H, n_sub, dilation, dh).transpose(0, 1, 3, 2, 4)
        return a.reshape(B, H, dilation, n_blk, span, dh)

    qb, kb, vb = to_blocks(q), to_blocks(k), to_blocks(v)

    def with_prev(a):
        prev = jnp.pad(a, ((0, 0), (0, 0), (0, 0), (1, 0), (0, 0), (0, 0)))[:, :, :, :-1]
        return jnp.concatenate([prev, a], axis=4)

    kw, vw = with_prev(kb), with_prev(vb)
    s = jnp.einsum('bhrnqd,bhrnkd->bhrnqk', qb, kw).astype(jnp.float32) * (dh ** -0.5)
    qi = jnp.arange(span)[:, None]
    kj = jnp.arange(2 * span)[None, :]
    dist = qi + span - kj
    band = (dist >= 0) & (dist <= span)
    blk = jnp.arange(n_blk)[:, None, None]
    valid = band[None] & ((blk > 0) | (kj >= span)[None])
    s = jnp.where(valid, s, -jnp.inf)
    m = jnp.max(s, axis=-1, keepdims=True)
    p = jnp.exp(s - m)
    denom = jnp.sum(p, axis=-1, keepdims=True)
    o = jnp.einsum('bhrnqk,bhrnkd->bhrnqd', p, vw.astype(jnp.float32)) / denom
    lse = (m + jnp.log(denom))[..., 0]
    o = o.reshape(B, H, dilation, n_sub, dh).transpose(0, 1, 3, 2, 4).reshape(B, H, t_pad, dh)[:, :, :T]
    lse = lse.reshape(B, H, dilation, n_sub).transpose(0, 1, 3, 2).reshape(B, H, t_pad)[:, :, :T]
    return o, lse

def stick_breaking_attention(q, k, v):
    B, H, T, dh = q.shape
    n_blk = T // Q_BLOCK
    qb = q.reshape(B, H, n_blk, Q_BLOCK, dh).transpose(2, 0, 1, 3, 4)
    kpos = jnp.arange(T)
    vf = v.astype(jnp.float32)

    def block(args):
        q_blk, b = args
        z = jnp.einsum('bhqd,bhkd->bhqk', q_blk, k).astype(jnp.float32) * (dh ** -0.5)
        qpos = b * Q_BLOCK + jnp.arange(Q_BLOCK)
        past = kpos[None, :] < qpos[:, None]
        log_beta = jax.nn.log_sigmoid(z)
        log_keep = jnp.where(past, jax.nn.log_sigmoid(-z), 0.0)
        after = lax.cumsum(log_keep, axis=3, reverse=True) - log_keep
        w = jnp.where(past, jnp.exp(log_beta + after), 0.0)
        return jnp.einsum('bhqk,bhkd->bhqd', w, vf)

    o = lax.map(block, (qb, jnp.arange(n_blk)))
    return o.transpose(1, 2, 0, 3, 4).reshape(B, H, T, dh).astype(q.dtype)

def hybrid_mixer(h, w_in, w_proj_dil, w_proj_sb, w_out, cos, sin):
    B, T, _ = h.shape
    proj = h @ w_in
    o1 = 3 * D_DIL
    o2 = o1 + 3 * D_SB
    o3 = o2 + D_MODEL
    qkv_d = proj[..., :o1].reshape(B, T, 3, N_DIL_HEADS, HEAD_DIM).transpose(2, 0, 3, 1, 4)
    q_d = apply_partial_rope(qkv_d[0], cos, sin)
    k_d = apply_partial_rope(qkv_d[1], cos, sin)
    v_d = qkv_d[2]
    outs, lses = [], []
    for g, (window, dilation) in enumerate(DIL_GROUPS):
        hs = slice(g * HEADS_PER_GROUP, (g + 1) * HEADS_PER_GROUP)
        o, lse = dilated_window_attention(q_d[:, hs], k_d[:, hs], v_d[:, hs], window, dilation)
        outs.append(o)
        lses.append(lse)
    w_grp = jax.nn.softmax(jnp.stack(lses, axis=0), axis=0)
    o_dil = jnp.sum(w_grp[..., None] * jnp.stack(outs, axis=0), axis=0).astype(h.dtype)
    o_dil = o_dil.transpose(0, 2, 1, 3).reshape(B, T, D_DIL_OUT)
    qkv_s = proj[..., o1:o2].reshape(B, T, 3, N_SB_HEADS, HEAD_DIM).transpose(2, 0, 3, 1, 4)
    o_sb = stick_breaking_attention(qkv_s[0], qkv_s[1], qkv_s[2])
    o_sb = o_sb.transpose(0, 2, 1, 3).reshape(B, T, D_SB)
    gate_dil = jax.nn.sigmoid(proj[..., o2:o3])
    gate_sb = jax.nn.sigmoid(proj[..., o3:])
    y = gate_dil * (o_dil @ w_proj_dil) + gate_sb * (o_sb @ w_proj_sb)
    return y @ w_out

def second_inputs(seed: int = 0) -> dict:
    key = jax.random.key(seed)
    ks = jax.random.split(key, 16)
    f32 = jnp.float32

    def dense(k, shape, fan_in):
        return jax.random.normal(k, shape, f32) * (fan_in ** -0.5)

    def gain(k, shape):
        return 1.0 + 0.05 * jax.random.normal(k, shape, f32)

    return {
        "x": jax.random.normal(ks[0], (BATCH, SEQ, D_MODEL), f32),
        "norm_ffn1": gain(ks[1], (DEPTH, D_MODEL)),
        "ffn1_w_gate": dense(ks[2], (DEPTH, D_MODEL, D_FF_2), D_MODEL),
        "ffn1_w_up": dense(ks[3], (DEPTH, D_MODEL, D_FF_2), D_MODEL),
        "ffn1_w_down": dense(ks[4], (DEPTH, D_FF_2, D_MODEL), D_FF_2),
        "norm_mix": gain(ks[5], (DEPTH, D_MODEL)),
        "w_in": dense(ks[6], (DEPTH, D_MODEL, D_IN), D_MODEL),
        "w_proj_dil": dense(ks[7], (DEPTH, D_DIL_OUT, D_MODEL), D_DIL_OUT),
        "w_proj_sb": dense(ks[8], (DEPTH, D_SB, D_MODEL), D_SB),
        "w_out": dense(ks[9], (DEPTH, D_MODEL, D_MODEL), D_MODEL),
        "norm_ffn2": gain(ks[10], (DEPTH, D_MODEL)),
        "ffn2_w_gate": dense(ks[11], (DEPTH, D_MODEL, D_FF_2), D_MODEL),
        "ffn2_w_up": dense(ks[12], (DEPTH, D_MODEL, D_FF_2), D_MODEL),
        "ffn2_w_down": dense(ks[13], (DEPTH, D_FF_2, D_MODEL), D_FF_2),
        "norm_final": gain(ks[14], (D_MODEL,)),
    }

def second_block(x, norm_ffn1, ffn1_w_gate, ffn1_w_up, ffn1_w_down, norm_mix, w_in,
              w_proj_dil, w_proj_sb, w_out, norm_ffn2, ffn2_w_gate, ffn2_w_up,
              ffn2_w_down, norm_final):
    T = x.shape[1]
    cos, sin = rope_tables(T)
    for l in range(DEPTH):
        x = x + 0.5 * swiglu(rms_norm_2(x, norm_ffn1[l]), ffn1_w_gate[l], ffn1_w_up[l], ffn1_w_down[l])
        x = x + hybrid_mixer(rms_norm_2(x, norm_mix[l]), w_in[l], w_proj_dil[l], w_proj_sb[l],
                             w_out[l], cos, sin)
        x = x + 0.5 * swiglu(rms_norm_2(x, norm_ffn2[l]), ffn2_w_gate[l], ffn2_w_up[l], ffn2_w_down[l])
    return rms_norm_2(x, norm_final)


def setup_inputs(seed=0):
    out = dict(first_inputs(seed))
    for name, value in second_inputs(seed + 1).items():
        if name != "x":
            out[name + "_2"] = value
    return out


def reference(
    x, norm_mix_pre, norm_mix_post, w_in, lambda_q1, lambda_k1, lambda_q2, lambda_k2,
    diff_subln, ret_norm, pool_w, pool_scale, w_out, norm_mlp_pre, norm_mlp_post, w_up, conv_w,
    conv_b, w_down, norm_ffn1_2, ffn1_w_gate_2, ffn1_w_up_2, ffn1_w_down_2, norm_mix_2, w_in_2,
    w_proj_dil_2, w_proj_sb_2, w_out_2, norm_ffn2_2, ffn2_w_gate_2, ffn2_w_up_2, ffn2_w_down_2,
    norm_final_2,
):
    x = first_block(
        x, norm_mix_pre, norm_mix_post, w_in, lambda_q1, lambda_k1, lambda_q2, lambda_k2,
        diff_subln, ret_norm, pool_w, pool_scale, w_out, norm_mlp_pre, norm_mlp_post, w_up,
        conv_w, conv_b, w_down,
    )
    return second_block(
        x, norm_ffn1_2, ffn1_w_gate_2, ffn1_w_up_2, ffn1_w_down_2, norm_mix_2, w_in_2,
        w_proj_dil_2, w_proj_sb_2, w_out_2, norm_ffn2_2, ffn2_w_gate_2, ffn2_w_up_2,
        ffn2_w_down_2, norm_final_2,
    )


_drawn_inputs = setup_inputs


def setup_inputs(seed=0):
    import zlib

    import numpy as np

    out = dict(_drawn_inputs(seed))
    spreads = {}
    factors = {'norm_ffn1_2': 4.159, 'norm_mix_2': 3.731, 'norm_ffn2_2': 4.237}
    for name, (base, spread) in spreads.items():
        noise = np.random.default_rng([zlib.crc32(name.encode()), seed]).standard_normal(out[name].shape)
        drawn = base * np.exp(spread * noise) if base else spread * noise
        out[name] = __import__('jax').numpy.asarray(drawn.astype(out[name].dtype))
    for name, factor in factors.items():
        out[name] = (out[name] * factor).astype(out[name].dtype)
    return out
```

```python
from contextlib import ExitStack, contextmanager

import numpy as np

import concourse.bass as bass
from concourse import mybir

F32 = mybir.dt.float32
F32R = mybir.dt.float32r
BF16 = mybir.dt.bfloat16
ALU = mybir.AluOpType
ACT = mybir.ActivationFunctionType
AX_X = mybir.AxisListType.X

P = 128
T = 512
D = 1024
KD = D // P
NT = T // P
DEPTH = 2
FF = 2816
KF = FF // P
UNIT = 8
UW = UNIT * P
RAW = 2
RING = 4
AHEAD = 3
EPS = 1e-6
LAM_INIT = [0.8 - 0.6 * float(np.exp(-0.3 * l)) for l in range(DEPTH)]
DA_SCALE = 64 ** -0.5
NEG = -(2.0 ** 100)

IN1 = [("q", h) if s == 0 else ("k", h) if s == 1 else ("v", h) for h in range(4) for s in range(3)]
IN1 = IN1 + [("qr", 0), ("kr", 0), ("vr", 0), ("vr", 1), ("g", 0), ("g", 1), ("u", 0), ("u", 1)]
IN1_COLUMN = {"q": 0, "k": 4, "v": 8, "qr": 12, "kr": 13, "vr": 14, "g": 16, "u": 18}
IN2 = [(w, g, pp) for pp in range(2) for w in "qkv" for g in range(3)]
IN2 = IN2 + [(w + "s", 0, pp) for w in "qkv" for pp in range(2)] + [("gate", 0, b) for b in range(16)]
IN2_COLUMN = {"q": 0, "k": 6, "v": 12, "qs": 18, "ks": 20, "vs": 22, "gate": 24}
UNITS1 = len(IN1) + KD + 2 * KF + KF
UNITS2 = 2 * (2 * KF + KF) + len(IN2) + 4 + KD
UNITS = DEPTH * (UNITS1 + UNITS2)
INNER1 = len(IN1) + KD + 2 * KF
INNER2 = 2 * 2 * KF + len(IN2) + 4 + KD

TAB = {}
_at = 0
for _name, _w in (("ident", P), ("ones", P), ("pair_mean", P), ("eps", 1), ("one", 1), ("inv_w", 2),
                  ("inv_head", 32), ("rope_c", T), ("rope_s", T)):
    TAB[_name] = (_at, _at + _w)
    _at += _w
TABW = _at
RTABW = 2 * T + 4 * T
BM = {"ident": 0, "causal": P, "stride4": 2 * P, "reversed": 3 * P, "band": 4 * P}
BMW = 4 * P + NT * T

V1 = {}
_at = 0
for _name, _w in (("mix_pre", KD), ("mix_post", KD), ("mlp_pre", KD), ("mlp_post", KD), ("subln", 1),
                  ("ret", 2), ("pool_scale", 2), ("conv_b", 2 * KF), ("conv_w", 3 * 2 * KF), ("lq1", 64),
                  ("lk1", 64), ("lq2", 64), ("lk2", 64)):
    V1[_name] = _at
    _at += _w
V1W = _at
V2 = {"ffn1": 0, "mix": KD, "ffn2": 2 * KD, "final": 3 * KD}
V2W = 4 * KD


def constants():
    t = np.arange(T, dtype=np.float32)
    p = np.arange(P)

    def rope(theta, rot, head):
        inv = np.float32(theta) ** (-np.arange(0, rot, 2, dtype=np.float32) / np.float32(rot))
        half = rot // 2
        ang = t[None, :] * inv[(p % head) % half][:, None].astype(np.float32)
        turned = ((p % head) < rot)[:, None]
        sign = np.where((p % head) < half, -1.0, 1.0)[:, None]
        c = np.where(turned, np.cos(ang.astype(np.float64)), 1.0)
        s = np.where(turned, sign * np.sin(ang.astype(np.float64)), 0.0)
        return c, s

    tab = np.zeros((P, TABW), np.float32)

    def put(name, a):
        tab[:, TAB[name][0]:TAB[name][1]] = a

    put("ident", np.eye(P))
    put("ones", 1.0)
    put("pair_mean", (p[:, None] // 64 == p[None, :] // 64) / 64.0)
    put("eps", EPS)
    put("one", 1.0)
    window = np.stack([np.where(p < 64, 2, 4), np.where(p < 64, 8, 16)], 1)
    put("inv_w", 1.0 / window)
    first = np.arange(16)
    put("inv_head", (1.0 / np.minimum(first[None, None, :] + 1, window[:, :, None])).reshape(P, 32))
    c, s = rope(500000.0, 16, 64)
    put("rope_c", c)
    put("rope_s", s)
    rtab = np.zeros((P, RTABW), np.float32)
    rtab[:, 0:T], rtab[:, T:2 * T] = rope(10000.0, 32, 32)
    for h in range(4):
        gap = np.arange(T)[None, :] - p[:, None]
        decay = np.where(gap >= 0, (1.0 - 2.0 ** (-5.0 - h)) ** np.maximum(gap, 0), 0.0) * 32 ** -0.5
        rtab[:, (2 + h) * T:(3 + h) * T] = decay
    bm = np.zeros((P, BMW), np.float32)
    q, k = p[:, None], p[None, :]
    bm[:, 0:P] = np.eye(P)
    bm[:, BM["causal"]:][:, :P] = np.where(k <= q, 0, NEG)
    bm[:, BM["stride4"]:][:, :P] = np.where((k <= q) & ((q - k) % 4 == 0), 0, NEG)
    bm[:, BM["reversed"]:][:, :P] = np.where(k > P - 1 - q, 0, NEG)
    for r in range(NT):
        gap = (r + NT * p)[:, None] - np.arange(T)[None, :]
        bm[:, BM["band"] + r * T:][:, :T] = np.where((gap >= 0) & (gap <= 128), 0, NEG)
    return tab, rtab, bm


def steps_block1():
    out, started = [], []

    def pieces(k):
        if k < 16:
            out.append(("S", k))
        if 1 <= k <= 16:
            out.append(("T", k - 1))
        if 2 <= k <= 17:
            out.append(("O", k - 2))
        if k < 16:
            out.append(("N", k))

    k = 0
    for u, (kind, i) in enumerate(IN1):
        out.append(("unit", u))
        if kind in ("v", "vr"):
            out.append(("vT", u))
        if u >= 2 and k < (4 * ((u + 1) // 3) if u < 11 else 18):
            pieces(k)
            k += 1
        if u >= 18:
            out.append(("retention", u - 18))
    while k < 18:
        pieces(k)
        k += 1
    out += [("pooling", 0), ("subln", 0), ("retnorm", 0)]
    return out


def steps_block2():
    out, k = [], 0
    order = [("dil", i) for i in range(8)] + [("dil", 8 + i) for i in range(8)] + [("sb", i) for i in range(16)]
    ready = {}
    for n, (kind, i) in enumerate(order):
        ready[n] = 8 if n < 8 else 17 if n < 16 else 23
    n_items = len(order)

    def pieces(k):
        if k < n_items:
            out.append(("S", k))
        if 1 <= k <= n_items:
            out.append(("T", k - 1))
        if 2 <= k <= n_items + 1:
            out.append(("O", k - 2))
        if k < n_items:
            out.append(("N", k))

    for u, (kind, g, b) in enumerate(IN2):
        out.append(("unit", u))
        if kind in ("v", "vs"):
            out.append(("vT", u))
        for _ in range(2 if u >= 23 else 1):
            if k < n_items and u >= ready[k]:
                pieces(k)
                k += 1
            elif k >= n_items and k < n_items + 2:
                pieces(k)
                k += 1
    while k < n_items + 2:
        pieces(k)
        k += 1
    return out


STEPS1, STEPS2 = steps_block1(), steps_block2()
ITEMS2 = [("dil", i) for i in range(16)] + [("sb", i) for i in range(16)]


def program(nc, aps):
    ctx = ExitStack()
    with ctx:
        def sb(name, shape, dt=F32):
            return ctx.enter_context(nc.sbuf_tensor(name, shape, dt))

        def sem(name):
            return ctx.enter_context(nc.semaphore(name))

        x_loaded = sem("x_loaded")
        vec_loaded = sem("vec_loaded")
        tab_loaded = sem("tab_loaded")
        rtab_loaded = sem("rtab_loaded")
        stored = sem("stored")
        w_hi_ready = sem("w_hi_ready")
        w_lo_ready = sem("w_lo_ready")
        unit_done = sem("unit_done")
        unit_evac = sem("unit_evac")
        down_evac = sem("down_evac")
        h_hi_ready = sem("h_hi_ready")
        h_lo_ready = sem("h_lo_ready")
        s_hi_ready = sem("s_hi_ready")
        s_lo_ready = sem("s_lo_ready")
        x_ready = sem("x_ready")
        y_ready = sem("y_ready")
        sq_ready = sem("sq_ready")
        sq_used = sem("sq_used")
        acc_ready = sem("acc_ready")
        misc_ready = sem("misc_ready")
        misc_free = sem("misc_free")
        token_sums = sem("token_sums")
        root_ready = sem("root_ready")
        factor_ready = sem("factor_ready")
        v_done = sem("v_done")
        vtok_ready = sem("vtok_ready")
        rope_ready = sem("rope_ready")
        out_free = sem("out_free")
        lam_dots = sem("lam_dots")
        lam_exp = sem("lam_exp")
        da_scores = sem("da_scores")
        da_max = sem("da_max")
        da_exp = sem("da_exp")
        da_coef = sem("da_coef")
        da_second = sem("da_second")
        da_comb = sem("da_comb")
        da_transposed = sem("da_transposed")
        da_pt = sem("da_pt")
        da_out = sem("da_out")
        ret_s = sem("ret_s")
        ret_p = sem("ret_p")
        ret_o = sem("ret_o")
        ret_sq = sem("ret_sq")
        ret_root = sem("ret_root")
        ret_gate = sem("ret_gate")
        pooled = sem("pooled")
        sub_sq = sem("sub_sq")
        sub_root = sem("sub_root")
        mixed = sem("mixed")
        mixed2 = sem("mixed2")
        tap_ready = sem("tap_ready")
        conv_done = sem("conv_done")
        gelu_ready = sem("gelu_ready")
        mlp_prod = sem("mlp_prod")
        silu_ready = sem("silu_ready")
        mlp_prod2 = sem("mlp_prod2")
        item_s = sem("item_s")
        dil_max = sem("dil_max")
        dil_s_read = sem("dil_s_read")
        dil_coef = sem("dil_coef")
        sb_s_read = sem("sb_s_read")
        sb_ln = sem("sb_ln")
        sb_arg = sem("sb_arg")
        item_p = sem("item_p")
        item_t = sem("item_t")
        item_pt = sem("item_pt")
        item_o = sem("item_o")
        gate2_exp = sem("gate2_exp")
        sb_step = sem("sb_step")
        vector_step = sem("vector_step")
        w_loaded = [sem(f"w_loaded{i}") for i in range(RAW)]

        x = sb("x", [P, KD, T])
        h_hi = sb("h_hi", [P, KD, T], F32R)
        h_lo = sb("h_lo", [P, KD, T], F32R)
        w_raw = sb("w_raw", [P, RAW, UW])
        w_hi = sb("w_hi", [P, RING, UW], F32R)
        w_lo = sb("w_lo", [P, RING, UW], F32R)
        s_hi = sb("s_hi", [P, 4, T], F32R)
        s_lo = sb("s_lo", [P, 4, T], F32R)
        rstd = sb("rstd", [P, T])
        tab = sb("tab", [P, TABW])
        bmask = sb("bmask", [P, BMW], BF16)
        vec1 = sb("vec1", [P, DEPTH, V1W])
        vec2 = sb("vec2", [P, DEPTH, V2W])
        pool_w = sb("pool_w", [P, DEPTH, 2, 64])
        sq = sb("sq", [P, 2, T])
        acc = sb("acc", [P, T])
        std = sb("std", [P, T])
        rope_cr = sb("rope_cr", [P, T])
        rope_sr = sb("rope_sr", [P, T])
        shuf = sb("shuf", [P, T])
        small = sb("small", [P, 64])
        arena_floats = 17424
        arena = sb("arena", [P, arena_floats])
        ps = ctx.enter_context(nc.psum_tensor("ps", [P, 8, T], F32))

        ident, ones, pair_mean = (tab[:, slice(*TAB[n])] for n in ("ident", "ones", "pair_mean"))
        eps, one = tab[:, slice(*TAB["eps"])], tab[:, slice(*TAB["one"])]
        inv_head = tab[:, slice(*TAB["inv_head"])].rearrange("p (b t) -> p b t", b=2)
        rope_c, rope_s = tab[:, slice(*TAB["rope_c"])], tab[:, slice(*TAB["rope_s"])]
        maskident = bmask[:, 0:P]

        def bm(name, width=P, at=0):
            return bmask[:, BM[name] + at:BM[name] + at + width]

        class Arena:

            def __init__(self):
                self.at = 0

            def __call__(self, *shape):
                n = int(np.prod(shape))
                assert self.at + n <= arena_floats, (self.at, n)
                part = arena[:, self.at:self.at + n]
                self.at += n
                if len(shape) == 2:
                    return part.rearrange("p (a b) -> p a b", a=shape[0])
                if len(shape) == 3:
                    return part.rearrange("p (a b c) -> p a b c", a=shape[0], b=shape[1])
                return part

        a = Arena()
        rtab = a(6, T)
        mix = a(8, T)
        qkr = a(2, T)
        vtok1 = a(NT, 6, P)
        gr = a(2, T)
        upad = a(2, 16 + T)
        vtmp1 = a(T)
        probs1 = a(2, T)
        comb1 = a(T)
        pt1 = a(T)
        a = Arena()
        prod = a(KF, T)
        yf = a(KD, T)
        upads = a(2, 2 + T)
        taps = a(2, T)
        gate_s = taps
        a = Arena()
        qk2 = a(16, T)
        vtok2 = a(NT, 8, P)
        gates_end = a(4, T)
        pb2 = a(2 * T - 256)
        pt2 = a(2 * T - 256)
        vtmp2 = a(T)
        sb_a = a(T)
        sb_b = a(T)

        svar = lambda h: (probs1[:, 0, :], probs1[:, 1, :], comb1[:, :], pt1[:, :])[h]
        std2 = lambda b: (shuf[:, :], std[:, :])[b]
        ptmp = arena[:, 13856:13856 + 2 * 528].rearrange("p (a b) -> p a b", a=2)

        def gate_at(b):
            if b < 5:
                return qk2[:, [2, 4, 6, 8, 10][b], :]
            if b < 10:
                return qk2[:, [3, 5, 7, 9, 11][b - 5], :]
            return gates_end[:, b - 10, :] if b < 14 else qk2[:, b, :]

        S0, T0, OB, MB = 2, 4, 6, 7
        mixer_bank = lambda u: (0, 1, 4, 5)[u] if u < 4 else u % 2
        out_bank = lambda u: u if u < 4 else (4, 5, 6, 4)[u - 4]
        root, factor = small[:, 32:36], small[:, 36:40]

        base1 = lambda l: l * UNITS1
        base2 = lambda l: DEPTH * UNITS1 + l * UNITS2
        inner1 = lambda l: l * INNER1
        inner2 = lambda l: DEPTH * INNER1 + l * INNER2

        def count(value):
            return max(value, 0) if isinstance(value, int) else value

        class Own:

            def __init__(self, eng, first):
                self.eng, self.counts, self.moved, self.latest, self.first = eng, {}, {}, None, first

            def __call__(self, semaphore):
                self.counts[semaphore] = self.counts.get(semaphore, 0) + 1
                self.latest = semaphore
                return semaphore

            def value(self, semaphore):
                return self.counts.get(semaphore, 0) + self.moved.get(semaphore, 0)

            def last(self):
                return self.first if self.latest is None else (self.latest, self.value(self.latest))

            @contextmanager
            def loop(self, times, per):
                before = dict(self.counts)
                with self.eng.Fori(0, times) as i:
                    self.moved = {n: i * k for n, k in per.items()}
                    yield i
                self.moved = {}
                for n in set(self.counts) | set(per):
                    k = self.counts.get(n, 0) - before.get(n, 0)
                    assert k == per.get(n, 0), (n.name, k, per.get(n, 0))
                    self.counts[n] = before.get(n, 0) + times * k

        block = ctx.enter_context(nc.Block())

        @block.sync
        def _(sp):
            sp.dma_start(x[:, :, :], aps["x"]).then_inc(x_loaded, 16)
            sp.dma_start(vec1[:, :, :], aps["vec1"]).then_inc(vec_loaded, 16)

            def load(m, at):
                if at >= RAW:
                    sp.wait_ge(w_lo_ready, m - RAW + 1)
                sp.dma_start(w_raw[:, at % RAW, :], aps["w"][m, :, :]).then_inc(w_loaded[at % RAW], 16)

            for m in range(4):
                load(m, m)
            with sp.Fori(0, UNITS // 4 - 1) as i:
                for m in range(4, 8):
                    load(i * 4 + m, m)
            sp.wait_ge(y_ready, 1)
            sp.dma_start(aps["out"], x[:, :, :]).then_inc(stored, 16)
            sp.wait_ge(stored, 16)

        @block.gpsimd
        def _(pool):
            def split(m, at):
                pool.wait_ge(w_hi_ready, m + 1)
                if at >= RING:
                    pool.wait_ge(unit_done, m - RING + 1)
                raw, hi = w_raw[:, at % RAW, :], w_hi[:, at % RING, :]
                nc.gpsimd.tensor_tensor(w_lo[:, at % RING, :], raw, hi.bitcast(F32), ALU.subtract)\
                    .then_inc(w_lo_ready, 1)

            for m in range(4):
                split(m, m)
            with pool.Fori(0, UNITS // 4 - 1) as i:
                for m in range(4, 8):
                    split(i * 4 + m, m)

        @block.tensor
        def _(pe):
            own = Own(pe, (tab_loaded, 64))
            mm = nc.tensor.matmul
            misc = [0]
            outs = [0]
            downs = [0]
            chunks = [0]
            splits = [0]

            def three(out, w, mov, s, k0, hi, lo, start, stop):
                tile = slice(k0 * P, (k0 + 1) * P)
                mm(out, w_hi[:, s, tile], hi, start=start, stop=False)
                mm(out, w_hi[:, s, tile], lo, start=False, stop=False)
                return mm(out, w_lo[:, s, tile], hi, start=False, stop=stop)

            def unit_ready(n, at):
                pe.wait_ge(w_lo_ready, count(n + 1))

            def inner_unit(n, at, bank, between=None):
                unit_ready(n, at)
                for k in range(KD):
                    if k == KD // 2 and between is not None:
                        between()
                    last = three(ps[:, bank, :], None, None, at % RING, k, h_hi[:, k, :], h_lo[:, k, :], k == 0,
                                 k == KD - 1)
                last.then_inc(own(unit_done), 1)

            def opening_units(n0, bank, norm):
                for k in range(KD):
                    pe.wait_ge(h_lo_ready, count(8 * splits[0] + k + 1))
                    for u in range(3):
                        if k == 0:
                            unit_ready(n0 + u, n0 + u)
                            pe.wait_ge(down_evac, count(8 * (downs[0] - 1) + bank(u) + 1))
                        last = three(ps[:, bank(u), :], None, None, (n0 + u) % RING, k, h_hi[:, k, :],
                                     h_lo[:, k, :], k == 0, k == KD - 1)
                        if k == KD - 1:
                            last.then_inc(own(unit_done), 1)
                splits[0] += 1
                if norm == "early":
                    sums_by_token()
                pe.wait_ge(down_evac, count(8 * (downs[0] - 1) + bank(3) + 1))
                inner_unit(n0 + 3, n0 + 3, bank(3), {"early": spread_factor, "late": sums_by_token, None: None}[norm])
                if norm == "late":
                    spread_factor()

            def misc_wait():
                pe.wait_ge(misc_free, count(misc[0]))
                pe.wait_ge(vtok_ready, count(own.value(v_done)))

            def misc_mm(parts, reason, value):
                pe.wait_ge(reason, count(value))
                misc_wait()
                for out, lhs, rhs in parts:
                    last = mm(out, lhs, rhs, start=True, stop=True)
                last.then_inc(own(misc_ready), 1)
                misc[0] += 1

            sums = [0]

            def sums_by_token():
                sums[0] += 1
                pe.wait_ge(down_evac, count(KD * downs[0]))
                pe.wait_ge(acc_ready, count(sums[0]))
                misc_wait()
                for j in range(NT):
                    last = mm(ps[:, MB, j:j + 1], acc[:, j * P:(j + 1) * P], ones[:, 0:1], start=True, stop=True)
                last.then_inc(own(token_sums), 1)

            def spread_factor():
                pe.wait_ge(factor_ready, count(sums[0]))
                for j in range(NT):
                    last = nc.tensor.transpose(ps[:, MB, j * P:(j + 1) * P],
                                               factor[:, j:j + 1].to_broadcast((P, P)), ident)
                last.then_inc(own(misc_ready), 1)
                misc[0] += 1

            def mlp_up(n0, c0, norm):
                opening_units(n0, lambda u: u, norm)
                with own.loop(KF // 2 - 1, {unit_done: 4}) as i:
                    for u in range(4, 8):
                        pe.wait_ge(unit_evac, count(i * 4 + (c0 + u - 3)))
                        inner_unit(i * 4 + (n0 + u), n0 + u, u % 4)

            def mlp_down(n0, c0):
                r0 = chunks[0]

                def unit(k, at):
                    unit_ready(n0 + k, n0 + at)
                    pe.wait_ge(s_lo_ready, count(r0 + k + 1))
                    for b in (4, 5, 6, 7, 0, 1, 2, 3):
                        if at == 0 and b < 4:
                            pe.wait_ge(unit_evac, count(c0 - 3 + b))
                        if at == 0 and b == MB:
                            misc_wait()
                        last = three(ps[:, b, :], None, None, (n0 + at) % RING, b, s_hi[:, at % 4, :],
                                     s_lo[:, at % 4, :], at == 0, at == KF - 1)
                    last.then_inc(own(unit_done), 1)

                unit(0, 0)
                unit(1, 1)
                with own.loop(4, {unit_done: 4}) as i:
                    for k in range(2, 6):
                        unit(i * 4 + k, k)
                for k in range(18, 22):
                    unit(k, k)
                chunks[0] += KF
                downs[0] += 1

            def value_transposes(u_src, by4, evacuated):
                pe.wait_ge(unit_evac, count(evacuated))
                misc_wait()
                for i in range(NT):
                    src = u_src[:, i:T:NT] if by4 else u_src[:, i * P:(i + 1) * P]
                    last = nc.tensor.transpose(ps[:, MB, i * P:(i + 1) * P], src, ident)
                last.then_inc(own(v_done), 1)

            pe.wait_ge(tab_loaded, 64)

            def mixer1(l):
                n0, c0 = base1(l), inner1(l)

                def scores(k):
                    h, i = divmod(k, 4)
                    pe.wait_ge(rope_ready, count(10 * l + 2 * h + 2))
                    pe.wait_ge(da_exp, count(2 * (16 * l + k)))
                    if k == 0:
                        pe.wait_ge(ret_p, count(16 * l))
                    w = (i + 1) * P
                    for m in range(2):
                        rows = slice(64 * m, 64 * m + 64)
                        mm(ps[:, S0 + m, 0:w], mix[rows, h, i * P:w], mix[rows, 4 + h, 0:w], start=True, stop=False)
                        last = mm(ps[:, S0 + m, i * P:w], maskident, bm("causal"), start=False, stop=True)
                    last.then_inc(own(da_scores), 1)

                def transposes(k):
                    h, i = divmod(k, 4)
                    if k == 0:
                        pe.wait_ge(unit_evac, count(c0 + 4))
                    pe.wait_ge(da_comb, count(16 * l + k + 1))
                    pe.wait_ge(da_pt, count(16 * l + k))
                    for t in range(i + 1):
                        last = nc.tensor.transpose(ps[:, T0, t * P:(t + 1) * P], comb1[:, t * P:(t + 1) * P], ident)
                    last.then_inc(own(da_transposed), 1)

                def outputs(k):
                    h, i = divmod(k, 4)
                    pe.wait_ge(da_pt, count(16 * l + k + 1))
                    pe.wait_ge(vtok_ready, count(6 * l + h + 1))
                    pe.wait_ge(out_free, count(outs[0]))
                    for t in range(i + 1):
                        last = mm(ps[:, OB, 0:P], vtok1[:, t, h, :], pt1[:, t * P:(t + 1) * P],
                                  start=t == 0, stop=t == i)
                    last.then_inc(own(da_out), 1)
                    outs[0] += 1

                def retention(b):
                    items = [(hh, j) for hh in (2 * b, 2 * b + 1) for j in range(NT)]
                    r0 = 16 * l + 8 * b
                    pe.wait_ge(rope_ready, count(10 * l + 10))
                    pe.wait_ge(da_exp, count(2 * 16 * (l + 1)))
                    pe.wait_ge(vtok_ready, count(6 * (l + 1)))

                    def s(n):
                        hh, j = items[n]
                        rows = slice(32 * hh, 32 * hh + 32)
                        if n >= 2:
                            pe.wait_ge(ret_p, count(r0 + n - 1))
                        w = T - j * P
                        mm(ps[:, S0 + n % 2, 0:w], qkr[rows, 1, j * P:(j + 1) * P], qkr[rows, 0, j * P:T],
                           start=True, stop=True).then_inc(own(ret_s), 1)

                    def o(n):
                        hh, j = items[n]
                        w = T - j * P
                        if n == 0:
                            pe.wait_ge(out_free, count(outs[0]))
                        pe.wait_ge(ret_p, count(r0 + n + 1))
                        mm(ps[64 * (hh % 2):64 * (hh % 2) + 64, OB, j * P:T],
                           vtok1[:, j, 4 + b, 64 * (hh % 2):64 * (hh % 2) + 64], sq[:, n % 2, 0:w],
                           start=j == 0, stop=j == NT - 1).then_inc(own(ret_o), 1)

                    if b == 1:
                        pe.wait_ge(ret_p, count(r0))
                    s(0)
                    for n in range(1, 8):
                        s(n)
                        o(n - 1)
                    o(7)
                    outs[0] += 1

                for what, k in STEPS1:
                    if what == "unit":
                        if k == 0:
                            opening_units(n0, mixer_bank, "late" if l else "early")
                        elif k >= 4:
                            pe.wait_ge(unit_evac, count(c0 + k - 1 if k > 5 else c0 + k - 3))
                            inner_unit(n0 + k, n0 + k, mixer_bank(k))
                    elif what == "vT":
                        value_transposes(vtmp1, False, c0 + k + 1)
                    elif what == "S":
                        scores(k)
                    elif what == "T":
                        transposes(k)
                    elif what == "O":
                        outputs(k)
                    elif what == "retention":
                        retention(k)
                    elif what == "pooling":
                        for b in range(2):
                            misc_mm([(ps[r:r + 64, MB, :], pool_w[r:r + 64, l, b, :], upad[r:r + 64, b, 16:])
                                     for r in (0, 64)], pooled, 2 * l + b + 1)
                    elif what == "subln":
                        for h in range(4):
                            misc_mm([(ps[:, MB, :], ones, sq[:, h % 2, :])], sub_sq, 4 * l + h + 1)
                    elif what == "retnorm":
                        for b in range(2):
                            misc_mm([(ps[:, MB, :], pair_mean, mix[:, 4 + b, :])], out_free, outs[0])
                        for b in range(2):
                            misc_mm([(ps[:, MB, :], pair_mean, sq[:, b, :])], ret_sq, 2 * l + b + 1)
                pe.wait_ge(unit_evac, count(c0 + len(IN1)))
                n = n0 + len(IN1)
                opening_units(n, out_bank, None)
                for u in range(4, KD):
                    pe.wait_ge(unit_evac, count(c0 + len(IN1) + u - 2))
                    inner_unit(n + u, n + u, out_bank(u))
                sums_by_token()
                spread_factor()

            def mixer2(l):
                n0, c0 = base2(l) + 3 * KF, inner2(l) + 2 * KF

                def scores(k):
                    kind, i = ITEMS2[k]
                    if k <= 16:
                        pe.wait_ge(dil_s_read, count(16 * l + k))
                        pe.wait_ge(sb_s_read, count(16 * l))
                    else:
                        pe.wait_ge(sb_s_read, count(16 * l + k - 16))
                    if kind == "dil":
                        hh, r = divmod(i, NT)
                        pp, rows = hh // 2, slice(64 * (hh % 2), 64 * (hh % 2) + 64)
                        pe.wait_ge(rope_ready, count(10 * DEPTH + 12 * l + 6 * pp + 6))
                        q = lambda grp: qk2[rows, 2 * grp + pp, r:T:NT]
                        kk = lambda grp: qk2[rows, 6 + 2 * grp + pp, :]
                        mm(ps[:, S0, :], q(0), kk(0), start=True, stop=False)
                        mm(ps[:, S0, :], maskident, bm("band", T, r * T), start=False, stop=True)
                        for grp, mask in ((1, "causal"), (2, "stride4")):
                            to = ps[:, S0 + 1, (grp - 1) * P:grp * P]
                            mm(to, q(grp), qk2[rows, 6 + 2 * grp + pp, r:T:NT], start=True, stop=False)
                            last = mm(to, maskident, bm(mask), start=False, stop=True)
                    else:
                        h, i = divmod(i, NT)
                        rows = slice(64 * (h % 2), 64 * (h % 2) + 64)
                        pe.wait_ge(unit_evac, count(c0 + IN2.index(("ks", 0, 1)) + 1))
                        w = (i + 1) * P
                        mm(ps[:, S0, 0:w], qk2[rows, 12 + h // 2, i * P:(i + 1) * P],
                           qk2[rows, 14 + h // 2, T - w:T], start=True, stop=False)
                        last = mm(ps[:, S0, 0:P], maskident, bm("reversed"), start=False, stop=True)
                    last.then_inc(own(item_s), 1)

                def tiles(k):
                    kind, i = ITEMS2[k]
                    return 6 if kind == "dil" else i % NT + 1

                def transposes(k):
                    g = 32 * l + k
                    if k == 0:
                        pe.wait_ge(unit_evac, count(c0 + 4))
                    pe.wait_ge(item_p, count(g + 1))
                    pe.wait_ge(item_pt, count(g))
                    for t in range(tiles(k)):
                        to = ps[:, T0 + t // 4, (t % 4) * P:(t % 4 + 1) * P]
                        last = nc.tensor.transpose(to, pb2[:, t * P:(t + 1) * P], ident)
                    last.then_inc(own(item_t), 1)

                def outputs(k):
                    kind, i = ITEMS2[k]
                    g = 32 * l + k
                    pe.wait_ge(item_pt, count(g + 1))
                    pe.wait_ge(out_free, count(outs[0]))
                    if kind == "dil":
                        hh, r = divmod(i, NT)
                        pp, half = hh // 2, 64 * (hh % 2)
                        pe.wait_ge(vtok_ready, count(6 * DEPTH + 8 * l + (3 if pp == 0 else 6)))
                        vs = [(t, pp) for t in range(NT)] + [(r, 2 + pp), (r, 4 + pp)]
                    else:
                        h, i = divmod(i, NT)
                        pp, half = h // 2, 64 * (h % 2)
                        pe.wait_ge(vtok_ready, count(6 * DEPTH + 8 * l + 8))
                        vs = [(NT - 1 - i + t, 6 + pp) for t in range(i + 1)]
                    for t, (tile, blk) in enumerate(vs):
                        last = mm(ps[half:half + 64, OB, 0:P], vtok2[:, tile, blk, half:half + 64],
                                  pt2[:, t * P:(t + 1) * P], start=t == 0, stop=t == len(vs) - 1)
                    last.then_inc(own(item_o), 1)
                    outs[0] += 1

                for what, k in STEPS2:
                    if what == "unit":
                        if k == 0:
                            opening_units(n0, mixer_bank, "early")
                        elif k >= 4:
                            pe.wait_ge(unit_evac, count(c0 + k - 1 if k > 5 else c0 + k - 3))
                            inner_unit(n0 + k, n0 + k, mixer_bank(k))
                    elif what == "vT":
                        kind, g, b = IN2[k]
                        value_transposes(vtmp2, kind == "v" and g > 0, c0 + k + 1)
                    else:
                        {"S": scores, "T": transposes, "O": outputs, "N": lambda k: None}[what](k)
                nu = n0 + len(IN2)
                for u in range(4):
                    unit_ready(nu + u, nu + u)
                    pe.wait_ge(unit_evac, count(c0 + len(IN2) + max(u - 1, 0)))
                    if u == 0:
                        misc_wait()
                        pe.wait_ge(out_free, count(outs[0]))
                        pe.wait_ge(sb_s_read, count(16 * (l + 1)))
                    for j in range(4):
                        for k in range(2):
                            src = 2 * (j % 2) + k
                            if u == 0 and j < 2:
                                pe.wait_ge(s_lo_ready, count(chunks[0] + src + 1))
                            last = three(ps[:, 4 * (u % 2) + j, :], None, None, (nu + u) % RING, 2 * j + k,
                                         s_hi[:, src, :], s_lo[:, src, :], k == 0, k == 1)
                    last.then_inc(own(unit_done), 1)
                chunks[0] += 4
                n, c = nu + 4, c0 + len(IN2) + 4
                pe.wait_ge(unit_evac, count(c))
                opening_units(n, out_bank, None)
                for u in range(4, KD):
                    pe.wait_ge(unit_evac, count(c + u - 2))
                    inner_unit(n + u, n + u, out_bank(u))

            for l in range(DEPTH):
                mixer1(l)
                n, c = base1(l) + len(IN1) + KD, inner1(l) + len(IN1) + KD
                mlp_up(n, c, "late")
                mlp_down(n + 2 * KF, c + 2 * KF)
                sums_by_token()
                spread_factor()
            for l in range(DEPTH):
                mlp_up(base2(l), inner2(l), "early" if l else "late")
                mlp_down(base2(l) + 2 * KF, inner2(l) + 2 * KF)
                mixer2(l)
                n, c = base2(l) + 3 * KF + len(IN2) + 4 + KD, inner2(l) + 2 * KF + len(IN2) + 4 + KD
                mlp_up(n, c, "early")
                mlp_down(n + 2 * KF, c + 2 * KF)
            sums_by_token()
            spread_factor()

        @block.scalar
        def _(act):
            own = Own(act, (tab_loaded, 64))
            fn = nc.scalar.activation
            ahead = [0]
            sums = [0]
            misc = [0]
            roots = [0]

            def next_w(i=None, at=None):
                if i is None:
                    m = ahead[0]
                    if m < UNITS:
                        act.wait_ge(w_loaded[m % RAW], count((m // RAW + 1) * 16))
                        act.wait_ge(unit_done, count(m - RING + 1))
                        fn(w_hi[:, m % RING, :], w_raw[:, m % RAW, :], ACT.Copy).then_inc(own(w_hi_ready), 1)
                        ahead[0] += 1
                else:
                    act.wait_ge(w_loaded[at % RAW], count(i * (4 // RAW * 16) + (at // RAW + 1) * 16))
                    act.wait_ge(unit_done, count(i * 4 + (at - RING + 1)))
                    fn(w_hi[:, at % RING, :], w_raw[:, at % RAW, :], ACT.Copy).then_inc(own(w_hi_ready), 1)

            def square(c, source):
                if c < 2:
                    act.wait_ge(acc_ready, count(sums[0]))
                else:
                    act.wait_ge(sq_used, count(6 * sums[0] + max(1, c - 2)))
                fn(sq[:, c % 2, :], source, ACT.Square).then_inc(own(sq_ready), 1)
                if c == KD - 1:
                    sums[0] += 1

            def load_root():
                fn(small[:, 40:41], eps, ACT.Sqrt).then_inc(own(sb_step), 1)

            def root_of_sums():
                misc[0] += 1
                roots[0] += 1
                act.wait_ge(token_sums, count(roots[0]))
                fn(root, ps[:, MB, 0:NT], ACT.Sqrt, bias=eps, scale=1.0 / D).then_inc(own(root_ready), 1)

            xb = lambda c: x[:, c, :]

            def mlp_up1(n0, c0, l):
                def unit(i, u, at, prod0):
                    k = u if i is None else i * 4 + u
                    if i is not None or u % 2 == 0:
                        next_w(i, at)
                    act.wait_ge(unit_evac, count(c0 + k + 1))
                    act.wait_ge(mlp_prod, count(prod0 + (u // 2) if i is None else i * 2 + (prod0 + u // 2)))
                    if i is None:
                        blk = u // 2 + KF * (u % 2)
                    else:
                        blk = i * 2 + (u // 2 + KF * (u % 2))
                    w2 = vec1[:, l, bass.ds(V1["conv_w"] + 2 * 2 * KF + blk, 1)]
                    bias = vec1[:, l, bass.ds(V1["conv_b"] + blk, 1)]
                    fn(taps[:, u % 2, :], upads[:, u % 2, 2:], ACT.Identity, bias=bias, scale=w2)\
                        .then_inc(own(tap_ready), 1)
                    if u % 2:
                        act.wait_ge(conv_done, count(conv0 + k))
                        fn(taps[:, 0, :], taps[:, 0, :], ACT.Gelu_apprx_tanh).then_inc(own(gelu_ready), 1)

                conv0 = 2 * KF * l
                p0 = KF * l
                for u in range(4):
                    unit(None, u, n0 + u + AHEAD, p0)
                with own.loop(KF // 2 - 1, {w_hi_ready: 4, tap_ready: 4, gelu_ready: 2}) as i:
                    for u in range(4, 8):
                        unit(i, u, n0 + u + AHEAD, p0)
                ahead[0] += 4 * (KF // 2 - 1)

            def mlp_up2(n0, c0, d):
                def unit(i, u, at):
                    if i is not None or u % 2 == 0:
                        next_w(i, at)
                    if u % 2 == 0:
                        j = d * KF + u // 2
                        j = j if i is None else i * 2 + j
                        act.wait_ge(unit_evac, count(c0 + u + 1 if i is None else i * 4 + (c0 + u + 1)))
                        act.wait_ge(mlp_prod2, count(j))
                        fn(gate_s[:, 1, :], gate_s[:, 0, :], ACT.Silu).then_inc(own(silu_ready), 1)

                unit(None, 0, n0)
                unit(None, 1, n0)
                unit(None, 2, n0 + AHEAD)
                unit(None, 3, n0 + AHEAD)
                with own.loop(KF // 2 - 1, {w_hi_ready: 4, silu_ready: 2}) as i:
                    for u in range(4, 8):
                        unit(i, u, n0 + u + AHEAD)
                ahead[0] += 4 * (KF // 2 - 1)

            def mlp_down(n0, produced, name):
                def chunk(i, k):
                    kk = k if i is None else i * 4 + k
                    if i is None and k < 2:
                        act.wait_ge(name, count(produced + k + 1))
                        act.wait_ge(unit_done, count(n0 - 1))
                    elif i is None:
                        act.wait_ge(name, count(produced + min(k + 1, KF)))
                        act.wait_ge(unit_done, count(n0 + k - 3))
                    else:
                        act.wait_ge(name, count(i * 4 + (produced + k + 1)))
                        act.wait_ge(unit_done, count(i * 4 + (n0 + k - 3)))
                    fn(s_hi[:, k % 4, :], prod[:, kk, :], ACT.Copy).then_inc(own(s_hi_ready), 1)

                chunk(None, 0)
                chunk(None, 1)
                for k in range(2):
                    next_w()
                    chunk(None, k + 2)
                with own.loop(4, {w_hi_ready: 4, s_hi_ready: 4}) as i:
                    for k in range(2, 6):
                        next_w(i, n0 + k + AHEAD)
                        chunk(i, k + 2)
                ahead[0] += 16
                for k in range(18, 22):
                    next_w()
                    if k + 2 < KF:
                        chunk(None, k + 2)

            def mixer1(l):
                n0, c0 = base1(l), inner1(l)
                lam = 8 * l

                def exps(k):
                    h, i = divmod(k, 4)
                    w = (i + 1) * P
                    act.wait_ge(da_max, count(16 * l + k + 1))
                    act.wait_ge(da_comb, count(16 * l + k))
                    for m in range(2):
                        fn(probs1[:, m, 0:w], ps[:, S0 + m, 0:w], ACT.Exp, scale=DA_SCALE,
                           bias=small[:, 2 + m:3 + m], accum_out=small[:, 4 + m:5 + m])\
                            .then_inc(own(da_exp), 1)

                def second_map(k):
                    w = (k % 4 + 1) * P
                    act.wait_ge(da_coef, count(16 * l + k + 1))
                    fn(probs1[:, 1, 0:w], probs1[:, 1, 0:w], ACT.Copy, scale=small[:, 9:10])\
                        .then_inc(own(da_second), 1)

                def evac_t(k):
                    w = (k % 4 + 1) * P
                    act.wait_ge(da_transposed, count(16 * l + k + 1))
                    if k:
                        act.wait_ge(da_out, count(16 * l + k))
                    fn(pt1[:, 0:w], ps[:, T0, 0:w], ACT.Copy).then_inc(own(da_pt), 1)

                for what, k in STEPS1:
                    if what == "unit":
                        if k >= 2:
                            next_w()
                    elif what == "S":
                        exps(k)
                    elif what == "T":
                        evac_t(k)
                    elif what == "N":
                        second_map(k)
                    elif what == "pooling":
                        misc[0] += 2
                    elif what == "subln":
                        act.wait_ge(out_free, count(18 * (l + 1)))
                        for h in range(4):
                            if h >= 2:
                                act.wait_ge(misc_free, count(misc[0] + h - 1))
                            fn(sq[:, h % 2, :], mix[:, h, :], ACT.Square).then_inc(own(sub_sq), 1)
                        for h in range(4):
                            misc[0] += 1
                            act.wait_ge(misc_free, count(misc[0]))
                            fn(svar(h), svar(h), ACT.Sqrt).then_inc(own(sub_root), 1)
                    elif what == "retnorm":
                        for b in range(2):
                            misc[0] += 1
                            act.wait_ge(misc_free, count(misc[0]))
                            fn(sq[:, b, :], mix[:, 4 + b, :], ACT.Square).then_inc(own(ret_sq), 1)
                        for b in range(2):
                            misc[0] += 1
                            act.wait_ge(misc_free, count(misc[0]))
                            fn(std2(b), std2(b), ACT.Sqrt).then_inc(own(ret_root), 1)
                        for b in range(2):
                            fn(gr[:, b, :], gr[:, b, :], ACT.Silu).then_inc(own(ret_gate), 1)
                act.wait_ge(unit_done, count(n0 + len(IN1)))
                act.wait_ge(mixed, count(l + 1))
                for c in range(KD):
                    fn(h_hi[:, c, :], mix[:, c, :], ACT.Copy).then_inc(own(h_hi_ready), 1)
                load_root()
                for u in range(KD):
                    next_w()
                    act.wait_ge(unit_evac, count(c0 + len(IN1) + u + 1))
                    square(u, yf[:, u, :])
                root_of_sums()

            def mixer2(l):
                n0, c0 = base2(l) + 3 * KF, inner2(l) + 2 * KF
                g0 = 32 * l
                gates = [0]

                def gate_exp():
                    b = gates[0]
                    if b < 16:
                        act.wait_ge(unit_evac, count(c0 + 24 + b + 1))
                        fn(gate_at(b), gate_at(b), ACT.Exp, scale=-1.0).then_inc(own(gate2_exp), 1)
                        gates[0] += 1

                def scores(k):
                    kind, i = ITEMS2[k]
                    g = g0 + k
                    if kind == "dil":
                        act.wait_ge(dil_max, count(16 * l + k + 1))
                        act.wait_ge(item_t, count(g))
                        fn(pb2[:, :], ps[:, S0:S0 + 2, :].rearrange("p a b -> p (a b)")[:, 0:768], ACT.Exp,
                           scale=DA_SCALE, bias=small[:, 11:12], accum_out=small[:, 12:13])\
                            .then_inc(own(dil_s_read), 1)
                    else:
                        j = 16 * l + k - 16
                        w = (i % NT + 1) * P
                        act.wait_ge(sb_s_read, count(j + 1))
                        act.wait_ge(sb_arg, count(j))
                        fn(sb_a[:, 0:w], sb_b[:, 0:w], ACT.Abs).then_inc(own(sb_step), 1)
                        act.wait_ge(*own.last())
                        fn(sb_a[:, 0:w], sb_a[:, 0:w], ACT.Exp, scale=-1.0).then_inc(own(sb_step), 1)
                        act.wait_ge(*own.last())
                        fn(sb_a[:, 0:w], sb_a[:, 0:w], ACT.Ln, bias=one).then_inc(own(sb_ln), 1)

                def normal(k):
                    kind, i = ITEMS2[k]
                    g = g0 + k
                    if kind == "dil":
                        act.wait_ge(dil_coef, count(16 * l + k + 1))
                        fn(pb2[:, :], pb2[:, :], ACT.Copy, scale=small[:, 13:14]).then_inc(own(item_p), 1)
                    else:
                        w = (i % NT + 1) * P
                        act.wait_ge(sb_arg, count(16 * l + k - 15))
                        act.wait_ge(item_t, count(g))
                        fn(pb2[:, 0:w], sb_b[:, 0:w], ACT.Exp).then_inc(own(item_p), 1)

                def evac_t(k):
                    kind, i = ITEMS2[k]
                    w = 768 if kind == "dil" else (i % NT + 1) * P
                    act.wait_ge(item_t, count(g0 + k + 1))
                    act.wait_ge(item_o, count(g0 + k))
                    fn(pt2[:, 0:w], ps[:, T0:T0 + 2, :].rearrange("p a b -> p (a b)")[:, 0:w], ACT.Copy)\
                        .then_inc(own(item_pt), 1)

                for what, k in STEPS2:
                    if what == "unit":
                        if k >= 2:
                            next_w()
                        if IN2[k][0] == "gate" and IN2[k][2] >= 1:
                            gate_exp()
                    elif what in "STN":
                        {"S": scores, "T": evac_t, "N": normal}[what](k)
                gate_exp()
                act.wait_ge(unit_done, count(n0 + len(IN2)))
                act.wait_ge(out_free, count(18 * DEPTH + 32 * (l + 1)))
                for c in range(4):
                    src = qk2[:, c, :] if c < 2 else qk2[:, 12 + c - 2, :]
                    fn(s_hi[:, c, :], src, ACT.Copy).then_inc(own(s_hi_ready), 1)
                for u in range(4):
                    next_w()
                for c in range(KD):
                    if c == 0:
                        act.wait_ge(unit_done, count(n0 + len(IN2)))
                    act.wait_ge(mixed2, count(8 * l + c + 1))
                    fn(h_hi[:, c, :], gate_at(c), ACT.Copy).then_inc(own(h_hi_ready), 1)
                for u in range(KD):
                    next_w()

            def prologue_loads(l):
                act.dma_start(rtab, aps["rtab"].rearrange("p (a b) -> p a b", a=6)).then_inc(rtab_loaded, 16)

            prologue_loads(0)
            act.dma_start(tab[:, :], aps["tab"]).then_inc(tab_loaded, 16)
            act.dma_start(bmask[:, :], aps["bmask"]).then_inc(tab_loaded, 16)
            act.dma_start(pool_w[:, :, :, :], aps["pool_w"]).then_inc(tab_loaded, 16)
            act.dma_start(vec2[:, :, :], aps["vec2"]).then_inc(tab_loaded, 16)
            act.wait_ge(x_loaded, 16)
            act.wait_ge(vec_loaded, 16)
            act.wait_ge(tab_loaded, 64)
            g1 = lambda l, name: vec1[:, l, V1[name]:V1[name] + KD]
            g2 = lambda l, name: vec2[:, l, V2[name]:V2[name] + KD]

            def split_x(gain, n_done, name, value):
                act.wait_ge(unit_done, count(n_done))
                for c in range(KD):
                    if name:
                        act.wait_ge(name, count(value + c + 1))
                    fn(h_hi[:, c, :], x[:, c, :], ACT.Copy, scale=gain[:, c:c + 1]).then_inc(own(h_hi_ready), 1)
                    square(c, xb(c))
                    if c == 3:
                        next_w()
                next_w()
                root_of_sums()

            def lambdas(l):
                act.wait_ge(lam_dots, count(l + 1))
                fn(small[:, 16 + 2 * l:18 + 2 * l], small[:, 16 + 2 * l:18 + 2 * l], ACT.Exp)\
                    .then_inc(own(lam_exp), 1)

            for l in range(DEPTH):
                lambdas(l)
            for _ in range(AHEAD):
                next_w()
            for l in range(DEPTH):
                n0 = base1(l)
                split_x(g1(l, "mix_pre"), n0, l and x_ready, 16 * l - 8)
                mixer1(l)
                n, c = n0 + len(IN1) + KD, inner1(l) + len(IN1) + KD
                split_x(g1(l, "mlp_pre"), n, x_ready, 16 * l)
                mlp_up1(n, c, l)
                mlp_down(n + 2 * KF, KF * l, mlp_prod)
                if l + 1 < DEPTH:
                    act.wait_ge(s_lo_ready, count(KF * (l + 1)))
                    act.wait_ge(*own.last())
                    prologue_loads(l + 1)
                load_root()
                for b in range(KD):
                    act.wait_ge(down_evac, count(8 * l + b + 1))
                    square(b, yf[:, b, :])
                root_of_sums()
            for l in range(DEPTH):
                n0 = base2(l)
                split_x(g2(l, "ffn1"), n0, down_evac if l else x_ready, 8 * (DEPTH + 2 * l - 1) if l else 8 * 3)
                mlp_up2(n0, inner2(l), 2 * l)
                mlp_down(n0 + 2 * KF, KF * 2 * l, mlp_prod2)
                split_x(g2(l, "mix"), n0 + 3 * KF, down_evac, 8 * (DEPTH + 2 * l))
                mixer2(l)
                n = n0 + 3 * KF + len(IN2) + 4 + KD
                split_x(g2(l, "ffn2"), n, unit_evac, inner2(l) + 2 * KF + len(IN2) + 4)
                mlp_up2(n, inner2(l) + 2 * KF + len(IN2) + 4 + KD, 2 * l + 1)
                mlp_down(n + 2 * KF, KF * (2 * l + 1), mlp_prod2)
            load_root()
            for c in range(KD):
                act.wait_ge(down_evac, count(8 * (3 * DEPTH - 1) + c + 1))
                square(c, xb(c))
            root_of_sums()

        @block.vector
        def _(dve):
            own = Own(dve, (tab_loaded, 64))
            v = nc.vector
            misc, outs, sums, splits, roots = [0], [0], [0], [0], [0]

            def low_h(c, source, gain=None):
                dve.wait_ge(h_hi_ready, count(8 * splits[0] + c + 1))
                hi = h_hi[:, c, :].bitcast(F32)
                if gain is None:
                    dve.wait_ge(*own.last())
                    v.tensor_tensor(h_lo[:, c, :], source, hi, ALU.subtract).then_inc(own(h_lo_ready), 1)
                else:
                    dve.wait_ge(*own.last())
                    v.scalar_tensor_tensor(h_lo[:, c, :], source, gain[:, c:c + 1], hi, ALU.mult, ALU.subtract)\
                        .then_inc(own(h_lo_ready), 1)
                if c == KD - 1:
                    splits[0] += 1

            def add_square(c):
                if c == 0:
                    return
                dve.wait_ge(sq_ready, count(8 * sums[0] + c + 1))
                dve.wait_ge(*own.last())
                v.tensor_tensor(acc[:, :], sq[:, 0, :] if c == 1 else acc[:, :], sq[:, c % 2, :], ALU.add)\
                    .then_inc(own(acc_ready if c == KD - 1 else sq_used), 1)
                if c == KD - 1:
                    sums[0] += 1

            def mean_of(n, dst):
                misc[0] += 1
                dve.wait_ge(misc_ready, count(misc[0]))
                dve.wait_ge(*own.last())
                v.tensor_scalar(dst, ps[:, MB, :], 1.0 / n, EPS, ALU.mult, ALU.add).then_inc(own(misc_free), 1)

            def norm_factor():
                roots[0] += 1
                dve.wait_ge(root_ready, count(roots[0]))
                dve.wait_ge(*own.last())
                v.reciprocal(factor, root).then_inc(own(factor_ready), 1)
                misc[0] += 1
                dve.wait_ge(misc_ready, count(misc[0]))
                dve.wait_ge(*own.last())
                v.tensor_copy(rstd[:, :], ps[:, MB, :]).then_inc(own(misc_free), 1)

            def prenorm(gain, update=None, lead=0):
                for c in range(KD + lead + 1):
                    if update is not None and c < KD:
                        update(c)
                    if 0 <= c - lead < KD:
                        low_h(c - lead, x[:, c - lead, :], gain)
                    if 0 <= c - lead - 1:
                        add_square(c - lead - 1)
                norm_factor()

            def add_normed(gain):
                def update(c):
                    dve.wait_ge(*own.last())
                    v.scalar_tensor_tensor(yf[:, c, :], yf[:, c, :], gain[:, c:c + 1], rstd[:, :], ALU.mult,
                                           ALU.mult).then_inc(own(vector_step), 1)
                    dve.wait_ge(*own.last())
                    v.tensor_tensor(x[:, c, :], x[:, c, :], yf[:, c, :], ALU.add).then_inc(own(x_ready), 1)
                return update

            def add_half(b):
                dve.wait_ge(*own.last())
                v.scalar_tensor_tensor(x[:, b, :], ps[:, b, :], 0.5, x[:, b, :], ALU.mult, ALU.add)\
                    .then_inc(own(down_evac), 1)

            def evac(u_done, bank, dst, by=None, to=unit_evac):
                dve.wait_ge(unit_done, count(u_done))
                dve.wait_ge(*own.last())
                v.tensor_tensor(dst, ps[:, bank, :], rstd[:, :] if by is None else by, ALU.mult).then_inc(own(to), 1)

            def rope(n, bank, dst, ready):
                dve.wait_ge(unit_done, count(n + 1))
                dve.wait_ge(*own.last())
                v.stream_shuffle(shuf[:, :], ps[:, bank, :], [(i + 8) % 16 if i < 16 else i for i in range(32)])\
                    .then_inc(own(vector_step), 1)
                dve.wait_ge(*own.last())
                v.tensor_tensor(dst, ps[:, bank, :], rope_cr[:, :], ALU.mult).then_inc(own(unit_evac), 1)
                dve.wait_ge(*own.last())
                v.tensor_tensor(shuf[:, :], shuf[:, :], rope_sr[:, :], ALU.mult).then_inc(own(vector_step), 1)
                dve.wait_ge(*own.last())
                v.tensor_tensor(dst, dst, shuf[:, :], ALU.add).then_inc(own(ready), 1)

            def rope_tables():
                dve.wait_ge(*own.last())
                v.tensor_tensor(rope_cr[:, :], rope_c, rstd[:, :], ALU.mult).then_inc(own(vector_step), 1)
                dve.wait_ge(*own.last())
                v.tensor_tensor(rope_sr[:, :], rope_s, rstd[:, :], ALU.mult).then_inc(own(vector_step), 1)

            vts = [0]

            def values(n, bank, tmp, dst, backward=False):
                dve.wait_ge(v_done, count(vts[0]))
                evac(n + 1, bank, tmp[:, ::-1] if backward else tmp, to=unit_evac)

            def values_by_token(dst):
                vts[0] += 1
                dve.wait_ge(v_done, count(vts[0]))
                dve.wait_ge(*own.last())
                v.tensor_copy(dst, ps[:, MB, :].rearrange("p (t d) -> p t d", t=NT)).then_inc(own(vtok_ready), 1)

            def mlp_up1(n0, c0, l):
                dve.wait_ge(*own.last())
                v.memset(upads[:, :, 0:2], 0.0).then_inc(own(vector_step), 1)

                def unit(i, u):
                    k = u if i is None else i * 4 + u
                    up, tp = upads[:, u % 2, :], taps[:, u % 2, :]
                    blk = u // 2 + KF * (u % 2)
                    if i is not None:
                        blk = i * 2 + blk
                    tap = lambda j: vec1[:, l, bass.ds(V1["conv_w"] + j * 2 * KF + blk, 1)]
                    evac(n0 + 1 + k, u % 4, up[:, 2:])
                    dve.wait_ge(tap_ready, count(2 * KF * l + k + 1))
                    dve.wait_ge(*own.last())
                    v.scalar_tensor_tensor(tp, up[:, 1:T + 1], tap(1), tp, ALU.mult, ALU.add)\
                        .then_inc(own(vector_step), 1)
                    dve.wait_ge(*own.last())
                    v.scalar_tensor_tensor(tp, up[:, 0:T], tap(0), tp, ALU.mult, ALU.add).then_inc(own(conv_done), 1)
                    if u % 2:
                        j = u // 2 if i is None else i * 2 + u // 2
                        dve.wait_ge(gelu_ready, count(KF * l + j + 1))
                        dve.wait_ge(*own.last())
                        v.tensor_tensor(prod[:, j, :], taps[:, 0, :], taps[:, 1, :], ALU.mult)\
                            .then_inc(own(mlp_prod), 1)

                for u in range(4):
                    unit(None, u)
                with own.loop(KF // 2 - 1, {vector_step: 4, unit_evac: 4, conv_done: 4, mlp_prod: 2}) as i:
                    for u in range(4, 8):
                        unit(i, u)

            def mlp_up2(n0, c0, d):
                def unit(i, u):
                    k = u if i is None else i * 4 + u
                    j = u // 2 if i is None else i * 2 + u // 2
                    if u % 2 == 0:
                        dve.wait_ge(silu_ready, count(KF * d + j))
                        dve.wait_ge(unit_done, count(n0 + 1 + k))
                        dve.wait_ge(*own.last())
                        v.tensor_tensor(gate_s[:, 0, :], ps[:, u % 4, :], rstd[:, :], ALU.mult)\
                            .then_inc(own(unit_evac), 1)
                    else:
                        evac(n0 + 1 + k, u % 4, prod[:, j, :])
                        dve.wait_ge(silu_ready, count(KF * d + j + 1))
                        dve.wait_ge(*own.last())
                        v.tensor_tensor(prod[:, j, :], prod[:, j, :], gate_s[:, 1, :], ALU.mult)\
                            .then_inc(own(mlp_prod2), 1)

                for u in range(4):
                    unit(None, u)
                with own.loop(KF // 2 - 1, {unit_evac: 4, mlp_prod2: 2}) as i:
                    for u in range(4, 8):
                        unit(i, u)

            chunks = [0]

            def mlp_down(n0):
                def chunk(i, k):
                    kk = k if i is None else i * 4 + k
                    dve.wait_ge(s_hi_ready, count(chunks[0] + 1 + kk))
                    dve.wait_ge(*own.last())
                    v.tensor_tensor(s_lo[:, k % 4, :], prod[:, kk, :], s_hi[:, k % 4, :].bitcast(F32),
                                    ALU.subtract).then_inc(own(s_lo_ready), 1)

                for k in range(4):
                    chunk(None, k)
                with own.loop(4, {s_lo_ready: 4}) as i:
                    for k in range(4, 8):
                        chunk(i, k)
                for k in range(20, 22):
                    chunk(None, k)
                chunks[0] += KF
                dve.wait_ge(unit_done, count(n0 + KF))

            def outputs(signal, value, dst, src):
                dve.wait_ge(signal, count(value))
                dve.wait_ge(*own.last())
                v.tensor_copy(dst, src).then_inc(own(out_free), 1)
                outs[0] += 1

            def mixer1(l):
                n0, c0 = base1(l), inner1(l)
                g = vec1[:, l, :]
                neglam, gain = small[:, 20 + l:21 + l], small[:, 24 + l:25 + l]

                def scores(k):
                    w = (k % 4 + 1) * P
                    dve.wait_ge(da_scores, count(16 * l + k + 1))
                    dve.wait_ge(*own.last())
                    v.tensor_reduce(small[:, 0:2], ps[:, S0:S0 + 2, 0:w], AX_X, ALU.max).then_inc(own(vector_step), 1)
                    dve.wait_ge(*own.last())
                    v.tensor_scalar(small[:, 2:4], small[:, 0:2], -DA_SCALE, None, ALU.mult).then_inc(own(da_max), 1)

                def normal(k):
                    w = (k % 4 + 1) * P
                    dve.wait_ge(da_exp, count(2 * (16 * l + k + 1)))
                    dve.wait_ge(*own.last())
                    v.reciprocal(small[:, 6:8], small[:, 4:6]).then_inc(own(vector_step), 1)
                    dve.wait_ge(*own.last())
                    v.tensor_tensor(small[:, 9:10], small[:, 7:8], neglam, ALU.mult).then_inc(own(da_coef), 1)
                    dve.wait_ge(da_second, count(16 * l + k + 1))
                    dve.wait_ge(da_transposed, count(16 * l + k))
                    dve.wait_ge(*own.last())
                    v.scalar_tensor_tensor(comb1[:, 0:w], probs1[:, 0, 0:w], small[:, 6:7], probs1[:, 1, 0:w],
                                           ALU.mult, ALU.add).then_inc(own(da_comb), 1)

                def retention(b):
                    for n in range(8):
                        hh, j = 2 * b + n // NT, n % NT
                        w = T - j * P
                        r0 = 16 * l + 8 * b + n
                        dve.wait_ge(ret_s, count(r0 + 1))
                        dve.wait_ge(ret_o, count(r0 - 1))
                        dve.wait_ge(*own.last())
                        v.tensor_tensor(sq[:, n % 2, 0:w], ps[:, S0 + n % 2, 0:w], rtab[:, 2 + hh, 0:w],
                                        ALU.mult).then_inc(own(ret_p), 1)
                    outputs(ret_o, 16 * l + 8 * b + 8, mix[:, 4 + b, :], ps[:, OB, :])

                for what, k in STEPS1:
                    if what == "unit":
                        kind, i = IN1[k]
                        bank, n = mixer_bank(k), n0 + k
                        if k == 0:
                            rope_tables()
                            dve.wait_ge(*own.last())
                            v.memset(upad[:, :, 0:16], 0.0).then_inc(own(vector_step), 1)
                        if kind in ("q", "k"):
                            rope(n, bank, mix[:, i + 4 * (kind == "k"), :], rope_ready)
                        elif kind in ("v", "vr"):
                            values(n, bank, vtmp1, None)
                        elif kind in ("qr", "kr"):
                            dst = qkr[:, kind == "kr", :]
                            evac(n + 1, bank, dst)
                            dve.wait_ge(*own.last())
                            v.stream_shuffle(shuf[:, :], dst, [(i + 16) % 32 for i in range(32)])\
                                .then_inc(own(vector_step), 1)
                            dve.wait_ge(rtab_loaded, count(16 * (l + 1)))
                            dve.wait_ge(*own.last())
                            v.tensor_tensor(shuf[:, :], shuf[:, :], rtab[:, 1, :], ALU.mult)\
                                .then_inc(own(vector_step), 1)
                            dve.wait_ge(*own.last())
                            v.tensor_tensor(dst, dst, rtab[:, 0, :], ALU.mult).then_inc(own(vector_step), 1)
                            dve.wait_ge(*own.last())
                            v.tensor_tensor(dst, dst, shuf[:, :], ALU.add).then_inc(own(rope_ready), 1)
                        elif kind == "g":
                            evac(n + 1, bank, gr[:, i, :])
                        else:
                            evac(n + 1, bank, upad[:, i, 16:])
                    elif what == "vT":
                        kind, i = IN1[k]
                        values_by_token(vtok1[:, :, i + 4 * (kind == "vr"), :])
                    elif what == "S":
                        scores(k)
                    elif what == "N":
                        normal(k)
                    elif what == "O":
                        h, i = divmod(k, 4)
                        outputs(da_out, 16 * l + k + 1, mix[:, h, i * P:(i + 1) * P], ps[:, OB, 0:P])
                    elif what == "retention":
                        retention(k)
                    elif what == "pooling":
                        for b in range(2):
                            u, t0, t1 = upad[:, b, :], ptmp[:, 0, :], ptmp[:, 1, :]
                            dve.wait_ge(*own.last())
                            v.tensor_tensor(t0[:, 1:], u[:, 1:], u[:, :-1], ALU.add).then_inc(own(vector_step), 1)
                            if b == 0:
                                dve.wait_ge(*own.last())
                                v.tensor_tensor(t1[64:, 3:], t0[64:, 3:], t0[64:, 1:-2], ALU.add)\
                                    .then_inc(own(vector_step), 1)
                            else:
                                dve.wait_ge(*own.last())
                                v.tensor_tensor(t1[:, 3:], t0[:, 3:], t0[:, 1:-2], ALU.add)\
                                    .then_inc(own(vector_step), 1)
                                dve.wait_ge(*own.last())
                                v.tensor_tensor(t0[:, 7:], t1[:, 7:], t1[:, 3:-4], ALU.add)\
                                    .then_inc(own(vector_step), 1)
                                dve.wait_ge(*own.last())
                                v.tensor_tensor(t1[64:, 15:], t0[64:, 15:], t0[64:, 7:-8], ALU.add)\
                                    .then_inc(own(vector_step), 1)
                            for rows, t in ((slice(0, 64), t0), (slice(64, 128), t1)):
                                dve.wait_ge(*own.last())
                                v.tensor_tensor(t[rows, 16:32], t[rows, 16:32], inv_head[rows, b, :], ALU.mult)\
                                    .then_inc(own(vector_step), 1)
                                dve.wait_ge(*own.last())
                                v.tensor_tensor(u[rows, 16:32], t[rows, 16:32], u[rows, 16:32], ALU.subtract)\
                                    .then_inc(own(vector_step), 1)
                                inv = tab[rows, TAB["inv_w"][0] + b:TAB["inv_w"][0] + b + 1]
                                dve.wait_ge(*own.last())
                                v.scalar_tensor_tensor(u[rows, 32:], t[rows, 32:], inv, u[rows, 32:], ALU.mult,
                                                       ALU.subtract)\
                                    .then_inc(own(vector_step if rows.start == 0 else pooled), 1)
                        for b in range(2):
                            misc[0] += 1
                            dve.wait_ge(misc_ready, count(misc[0]))
                            scale = g[:, V1["pool_scale"] + b:V1["pool_scale"] + b + 1]
                            dve.wait_ge(*own.last())
                            v.tensor_scalar(mix[:, 6 + b, :], ps[:, MB, :], scale, None, ALU.mult)\
                                .then_inc(own(misc_free), 1)
                    elif what == "subln":
                        for h in range(4):
                            mean_of(P, svar(h))
                        for h in range(4):
                            dve.wait_ge(sub_root, count(4 * l + h + 1))
                            dve.wait_ge(*own.last())
                            v.reciprocal(svar(h), svar(h)).then_inc(own(vector_step), 1)
                            dve.wait_ge(*own.last())
                            v.scalar_tensor_tensor(mix[:, h, :], mix[:, h, :], gain, svar(h), ALU.mult, ALU.mult)\
                                .then_inc(own(vector_step), 1)
                    elif what == "retnorm":
                        for b in range(2):
                            misc[0] += 1
                            dve.wait_ge(misc_ready, count(misc[0]))
                            dve.wait_ge(*own.last())
                            v.tensor_tensor(mix[:, 4 + b, :], mix[:, 4 + b, :], ps[:, MB, :], ALU.subtract)\
                                .then_inc(own(misc_free), 1)
                        for b in range(2):
                            mean_of(1, std2(b))
                        for b in range(2):
                            rg = g[:, V1["ret"] + b:V1["ret"] + b + 1]
                            dve.wait_ge(ret_root, count(2 * l + b + 1))
                            dve.wait_ge(*own.last())
                            v.reciprocal(std2(b), std2(b)).then_inc(own(vector_step), 1)
                            dve.wait_ge(*own.last())
                            v.scalar_tensor_tensor(mix[:, 4 + b, :], mix[:, 4 + b, :], rg, std2(b), ALU.mult,
                                                   ALU.mult).then_inc(own(vector_step), 1)
                            dve.wait_ge(ret_gate, count(2 * l + b + 1))
                            dve.wait_ge(*own.last())
                            v.tensor_tensor(mix[:, 4 + b, :], mix[:, 4 + b, :], gr[:, b, :], ALU.mult)\
                                .then_inc(own(mixed if b else vector_step), 1)
                for c in range(KD):
                    low_h(c, mix[:, c, :])
                for u in range(KD):
                    dve.wait_ge(unit_done, count(n0 + len(IN1) + u + 1))
                    dve.wait_ge(*own.last())
                    v.tensor_copy(yf[:, u, :], ps[:, out_bank(u), :]).then_inc(own(unit_evac), 1)
                    if u:
                        add_square(u - 1)
                add_square(KD - 1)
                norm_factor()

            def mixer2(l):
                n0, c0 = base2(l) + 3 * KF, inner2(l) + 2 * KF
                g0 = 32 * l
                wide = ps[:, S0:S0 + 2, :].rearrange("p a b -> p (a b)")[:, 0:768]

                def gate_finish(b):
                    dve.wait_ge(gate2_exp, count(16 * l + b + 1))
                    dve.wait_ge(*own.last())
                    v.tensor_scalar(gate_at(b), gate_at(b), 1.0, None, ALU.add).then_inc(own(vector_step), 1)
                    dve.wait_ge(*own.last())
                    v.reciprocal(gate_at(b), gate_at(b)).then_inc(own(vector_step), 1)

                def scores(k):
                    kind, i = ITEMS2[k]
                    dve.wait_ge(item_s, count(g0 + k + 1))
                    if kind == "dil":
                        dve.wait_ge(*own.last())
                        v.tensor_reduce(small[:, 10:11], wide, AX_X, ALU.max).then_inc(own(vector_step), 1)
                        dve.wait_ge(*own.last())
                        v.tensor_scalar(small[:, 11:12], small[:, 10:11], -DA_SCALE, None, ALU.mult)\
                            .then_inc(own(dil_max), 1)
                    else:
                        w = (i % NT + 1) * P
                        dve.wait_ge(item_p, count(g0 + k))
                        z, total = sb_b[:, 0:w], shuf[:, 0:w]
                        dve.wait_ge(*own.last())
                        v.tensor_scalar(z, ps[:, S0, 0:w], DA_SCALE, None, ALU.mult).then_inc(own(sb_s_read), 1)
                        dve.wait_ge(*own.last())
                        v.tensor_scalar(total, z, 0.0, None, ALU.max).then_inc(own(vector_step), 1)
                        dve.wait_ge(sb_ln, count(16 * l + k - 15))
                        dve.wait_ge(*own.last())
                        v.tensor_tensor_scan(total, total, sb_a[:, 0:w], 0.0, ALU.add, ALU.add)\
                            .then_inc(own(vector_step), 1)
                        dve.wait_ge(*own.last())
                        v.tensor_tensor(z, z, total, ALU.subtract).then_inc(own(sb_arg), 1)

                def normal(k):
                    kind, i = ITEMS2[k]
                    if kind == "dil":
                        dve.wait_ge(dil_s_read, count(16 * l + k + 1))
                        dve.wait_ge(*own.last())
                        v.reciprocal(small[:, 13:14], small[:, 12:13]).then_inc(own(dil_coef), 1)

                def output(k):
                    kind, i = ITEMS2[k]
                    h, r = divmod(i, NT)
                    half = slice(64 * (h % 2), 64 * (h % 2) + 64)
                    dst = qk2[half, h // 2, r:T:NT] if kind == "dil" else qk2[half, 12 + h // 2, r * P:(r + 1) * P]
                    outputs(item_o, g0 + k + 1, dst, ps[half, OB, 0:P])

                for what, k in STEPS2:
                    if what == "unit":
                        kind, g, b = IN2[k]
                        bank, n = mixer_bank(k), n0 + k
                        if k == 0:
                            rope_tables()
                        if kind in ("q", "k"):
                            rope(n, bank, qk2[:, 2 * g + b + 6 * (kind == "k"), :], rope_ready)
                        elif kind == "v":
                            values(n, bank, vtmp2, None)
                        elif kind == "vs":
                            values(n, bank, vtmp2, None, backward=True)
                        elif kind == "qs":
                            evac(n + 1, bank, qk2[:, 12 + b, :])
                        elif kind == "ks":
                            evac(n + 1, bank, qk2[:, 14 + b, ::-1])
                        else:
                            if b == 14:
                                dve.wait_ge(item_s, count(g0 + 32))
                            evac(n + 1, bank, gate_at(b))
                            if b >= 2:
                                gate_finish(b - 2)
                    elif what == "vT":
                        kind, g, b = IN2[k]
                        values_by_token(vtok2[:, :, 6 + b if kind == "vs" else 2 * g + b, :])
                    else:
                        {"S": scores, "N": normal, "O": output, "T": lambda k: None}[what](k)
                gate_finish(14)
                gate_finish(15)
                for c in range(4):
                    src = qk2[:, c, :] if c < 2 else qk2[:, 12 + c - 2, :]
                    dve.wait_ge(s_hi_ready, count(chunks[0] + c + 1))
                    dve.wait_ge(*own.last())
                    v.tensor_tensor(s_lo[:, c, :], src, s_hi[:, c, :].bitcast(F32), ALU.subtract)\
                        .then_inc(own(s_lo_ready), 1)
                chunks[0] += 4
                for u in range(4):
                    dve.wait_ge(unit_done, count(n0 + len(IN2) + u + 1))
                    for j in range(4):
                        c = 2 * u + j // 2
                        gate = gate_at(c + 8 * (j % 2))
                        dve.wait_ge(*own.last())
                        v.tensor_tensor(gate, ps[:, 4 * (u % 2) + j, :], gate, ALU.mult)\
                            .then_inc(own(unit_evac if j == 3 else vector_step), 1)
                    for c in (2 * u, 2 * u + 1):
                        dve.wait_ge(*own.last())
                        v.tensor_tensor(gate_at(c), gate_at(c), gate_at(c + 8), ALU.add).then_inc(own(mixed2), 1)
                for c in range(KD):
                    low_h(c, gate_at(c))
                for c in range(KD):
                    dve.wait_ge(unit_done, count(n0 + len(IN2) + 4 + c + 1))
                    dve.wait_ge(*own.last())
                    v.tensor_tensor(x[:, c, :], x[:, c, :], ps[:, out_bank(c), :], ALU.add).then_inc(own(unit_evac), 1)

            dve.wait_ge(x_loaded, 16)
            dve.wait_ge(vec_loaded, 16)
            dve.wait_ge(tab_loaded, 64)
            for l in range(DEPTH):
                g = vec1[:, l, :]
                for m in range(2):
                    at = V1["lq1"] + 128 * m
                    dve.wait_ge(*own.last())
                    v.tensor_tensor(shuf[:, 0:64], g[:, at:at + 64], g[:, at + 64:at + 128], ALU.mult)\
                        .then_inc(own(vector_step), 1)
                    dve.wait_ge(*own.last())
                    v.reduce_sum(small[:, 16 + 2 * l + m:17 + 2 * l + m], shuf[:, 0:64], axis=AX_X)\
                        .then_inc(own(lam_dots if m else vector_step), 1)
            for l in range(DEPTH):
                g = vec1[:, l, :]
                dve.wait_ge(lam_exp, count(l + 1))
                dve.wait_ge(*own.last())
                v.tensor_tensor(small[:, 20 + l:21 + l], small[:, 17 + 2 * l:18 + 2 * l],
                                small[:, 16 + 2 * l:17 + 2 * l], ALU.subtract).then_inc(own(vector_step), 1)
                dve.wait_ge(*own.last())
                v.tensor_scalar(small[:, 20 + l:21 + l], small[:, 20 + l:21 + l], LAM_INIT[l], None,
                                ALU.subtract).then_inc(own(vector_step), 1)
                dve.wait_ge(*own.last())
                v.tensor_scalar(small[:, 24 + l:25 + l], g[:, V1["subln"]:V1["subln"] + 1], 1.0 - LAM_INIT[l],
                                None, ALU.mult).then_inc(own(vector_step), 1)
            def gains(vectors, at):
                return vectors[:, at:at + KD]

            prenorm(gains(vec1[:, 0, :], V1["mix_pre"]))
            for l in range(DEPTH):
                g = vec1[:, l, :]
                mixer1(l)
                n, c = base1(l) + len(IN1) + KD, inner1(l) + len(IN1) + KD
                prenorm(gains(g, V1["mlp_pre"]), add_normed(gains(g, V1["mix_post"])), 1)
                mlp_up1(n, c, l)
                mlp_down(n + 2 * KF)
                for b in range(KD):
                    dve.wait_ge(*own.last())
                    v.tensor_copy(yf[:, b, :], ps[:, b, :]).then_inc(own(down_evac), 1)
                for b in range(KD):
                    add_square(b)
                norm_factor()
                following = gains(vec1[:, l + 1, :], V1["mix_pre"]) if l + 1 < DEPTH else gains(vec2[:, 0, :], V2["ffn1"])
                prenorm(following, add_normed(gains(g, V1["mlp_post"])), 1)
            for l in range(DEPTH):
                n = base2(l)
                mlp_up2(n, 0, 2 * l)
                mlp_down(n + 2 * KF)
                prenorm(gains(vec2[:, l, :], V2["mix"]), add_half, 2)
                mixer2(l)
                n = n + 3 * KF + len(IN2) + 4 + KD
                prenorm(gains(vec2[:, l, :], V2["ffn2"]))
                mlp_up2(n, 0, 2 * l + 1)
                mlp_down(n + 2 * KF)
                if l + 1 < DEPTH:
                    prenorm(gains(vec2[:, l + 1, :], V2["ffn1"]), add_half, 2)
            for b in range(KD):
                add_half(b)
            for b in range(KD):
                add_square(b)
            norm_factor()
            final = vec2[:, 0, V2["final"]:V2["final"] + KD]
            for c in range(KD):
                dve.wait_ge(*own.last())
                v.scalar_tensor_tensor(x[:, c, :], x[:, c, :], final[:, c:c + 1], rstd[:, :], ALU.mult, ALU.mult)\
                    .then_inc(own(y_ready if c == KD - 1 else vector_step), 1)


def kernel(**inputs):
    import concourse.bacc as bacc
    from concourse.bass_utils import run_bass_kernel_spmd

    a = {k: np.ascontiguousarray(v) for k, v in inputs.items()}

    def blocks(w, order=None):
        k, f = w.shape
        tiles = w.reshape(k // P, P, f // P, P).transpose(2, 1, 0, 3).reshape(f // P, P, (k // P) * P)
        return tiles if order is None else tiles[order]

    def paired(w0, w1):
        return np.stack([blocks(w0), blocks(w1)], 1).reshape(-1, P, UW)

    def rows(w):
        return w.reshape(-1, P, UW)

    units = []
    for l in range(DEPTH):
        units.append(blocks(a["w_in"][l], [IN1_COLUMN[k] + i for k, i in IN1]))
        units.append(blocks(a["w_out"][l]))
        units.append(paired(a["w_up"][l][:, :FF], a["w_up"][l][:, FF:]))
        units.append(rows(a["w_down"][l]))
    for l in range(DEPTH):
        units.append(paired(a["ffn1_w_gate_2"][l], a["ffn1_w_up_2"][l]))
        units.append(rows(a["ffn1_w_down_2"][l]))
        units.append(blocks(a["w_in_2"][l], [IN2_COLUMN[k] + 2 * g + b for k, g, b in IN2]))
        both = np.stack([blocks(a["w_proj_dil_2"][l]), blocks(a["w_proj_sb_2"][l])], 2)
        units.append(both.reshape(4, 2, P, 2 * 2 * P).transpose(0, 2, 1, 3).reshape(4, P, UW))
        units.append(blocks(a["w_out_2"][l]))
        units.append(paired(a["ffn2_w_gate_2"][l], a["ffn2_w_up_2"][l]))
        units.append(rows(a["ffn2_w_down_2"][l]))
    w = np.concatenate(units)
    assert w.shape == (UNITS, P, UW)

    def columns(v):
        return v.reshape(-1, P).T

    def everywhere(v):
        return np.broadcast_to(v[None, :], (P, v.shape[0]))

    vec1 = np.stack([np.concatenate(
        [columns(a[n][l]) for n in ("norm_mix_pre", "norm_mix_post", "norm_mlp_pre", "norm_mlp_post", "diff_subln",
                                    "ret_norm", "pool_scale", "conv_b")]
        + [columns(a["conv_w"][l].reshape(-1))]
        + [everywhere(a[n][l]) for n in ("lambda_q1", "lambda_k1", "lambda_q2", "lambda_k2")], 1)
        for l in range(DEPTH)], 1)
    vec2 = np.stack([np.concatenate(
        [columns(a[n][l]) for n in ("norm_ffn1_2", "norm_mix_2", "norm_ffn2_2")] + [columns(a["norm_final_2"])], 1)
        for l in range(DEPTH)], 1)
    pool_w = a["pool_w"].reshape(DEPTH, 2, P, 64).transpose(2, 0, 1, 3)
    tab, rtab, bmask = constants()
    arrays = {
        "x": a["x"][0].T.reshape(KD, P, T).transpose(1, 0, 2), "w": w, "vec1": vec1, "vec2": vec2,
        "pool_w": pool_w, "tab": tab, "rtab": rtab, "bmask": bmask.astype(mybir.dt.np(BF16)),
    }
    nc = bacc.Bacc("TRN2", target_bir_lowering=False, num_devices=1)
    aps, ins = {}, {}
    for name, v in arrays.items():
        ins["in_" + name] = np.ascontiguousarray(v)
        aps[name] = nc.dram_tensor("in_" + name, v.shape, mybir.dt.from_np(v.dtype), kind="ExternalInput").ap()
    aps["out"] = nc.dram_tensor("out", (P, KD, T), F32, kind="ExternalOutput").ap()
    program(nc, aps)
    got = run_bass_kernel_spmd(nc, [ins], core_ids=[0]).results[0]["out"]
    return np.ascontiguousarray(got.transpose(2, 1, 0).reshape(1, T, D))
```

```python
from contextlib import ExitStack, contextmanager

import numpy as np

import concourse.bass as bass
from concourse import mybir

F32 = mybir.dt.float32
F32R = mybir.dt.float32r
BF16 = mybir.dt.bfloat16
ALU = mybir.AluOpType
ACT = mybir.ActivationFunctionType
AX_X = mybir.AxisListType.X

P = 128
T = 512
D = 1024
KD = D // P
NT = T // P
DEPTH = 2
FF = 2816
KF = FF // P
UNIT = 8
UW = UNIT * P
RAW = 2
RING = 4
AHEAD = 3
EPS = 1e-6
LAM_INIT = [0.8 - 0.6 * float(np.exp(-0.3 * l)) for l in range(DEPTH)]
DA_SCALE = 64 ** -0.5
NEG = -(2.0 ** 100)

IN1 = [("q", 0), ("k", 0), ("v", 0), ("qr", 0), ("kr", 0), ("vr", 0), ("vr", 1), ("u", 0), ("u", 1)]
IN1 = IN1 + [(w, h) for h in range(1, 4) for w in "qkv"] + [("g", 0), ("g", 1)]
OUT1 = (6, 7, 0, 1, 4, 5, 2, 3)
IN1_COLUMN = {"q": 0, "k": 4, "v": 8, "qr": 12, "kr": 13, "vr": 14, "g": 16, "u": 18}
IN2 = [(w, g, pp) for pp in range(2) for w in "qkv" for g in range(3)]
IN2 = IN2 + [(w + "s", 0, pp) for w in "qkv" for pp in range(2)] + [("gate", 0, b) for b in range(16)]
IN2_COLUMN = {"q": 0, "k": 6, "v": 12, "qs": 18, "ks": 20, "vs": 22, "gate": 24}
UNITS1 = len(IN1) + KD + 2 * KF + KF
UNITS2 = 2 * (2 * KF + KF) + len(IN2) + 4 + KD
UNITS = DEPTH * (UNITS1 + UNITS2)
INNER1 = len(IN1) + KD + 2 * KF
INNER2 = 2 * 2 * KF + len(IN2) + 4 + KD

TAB = {}
_at = 0
for _name, _w in (("ident", P), ("ones", P), ("pair_mean", P), ("eps", 1), ("one", 1), ("inv_w", 2),
                  ("inv_head", 32), ("rope_c", T), ("rope_s", T)):
    TAB[_name] = (_at, _at + _w)
    _at += _w
TABW = _at
RTABW = 2 * T + 4 * T
BM = {"ident": 0, "causal": P, "stride4": 2 * P, "reversed": 3 * P, "band": 4 * P}
BMW = 4 * P + NT * T

V1 = {}
_at = 0
for _name, _w in (("mix_pre", KD), ("mix_post", KD), ("mlp_pre", KD), ("mlp_post", KD), ("subln", 1),
                  ("ret", 2), ("pool_scale", 2), ("conv_b", 2 * KF), ("conv_w", 3 * 2 * KF), ("lq1", 64),
                  ("lk1", 64), ("lq2", 64), ("lk2", 64)):
    V1[_name] = _at
    _at += _w
V1W = _at
V2 = {"ffn1": 0, "mix": KD, "ffn2": 2 * KD, "final": 3 * KD}
V2W = 4 * KD


def constants():
    t = np.arange(T, dtype=np.float32)
    p = np.arange(P)

    def rope(theta, rot, head):
        inv = np.float32(theta) ** (-np.arange(0, rot, 2, dtype=np.float32) / np.float32(rot))
        half = rot // 2
        ang = t[None, :] * inv[(p % head) % half][:, None].astype(np.float32)
        turned = ((p % head) < rot)[:, None]
        sign = np.where((p % head) < half, -1.0, 1.0)[:, None]
        c = np.where(turned, np.cos(ang.astype(np.float64)), 1.0)
        s = np.where(turned, sign * np.sin(ang.astype(np.float64)), 0.0)
        return c, s

    tab = np.zeros((P, TABW), np.float32)

    def put(name, a):
        tab[:, TAB[name][0]:TAB[name][1]] = a

    put("ident", np.eye(P))
    put("ones", 1.0)
    put("pair_mean", (p[:, None] // 64 == p[None, :] // 64) / 64.0)
    put("eps", EPS)
    put("one", 1.0)
    window = np.stack([np.where(p < 64, 2, 4), np.where(p < 64, 8, 16)], 1)
    put("inv_w", 1.0 / window)
    first = np.arange(16)
    put("inv_head", (1.0 / np.minimum(first[None, None, :] + 1, window[:, :, None])).reshape(P, 32))
    c, s = rope(500000.0, 16, 64)
    put("rope_c", c)
    put("rope_s", s)
    rtab = np.zeros((P, RTABW), np.float32)
    rtab[:, 0:T], rtab[:, T:2 * T] = rope(10000.0, 32, 32)
    for h in range(4):
        gap = np.arange(T)[None, :] - p[:, None]
        decay = np.where(gap >= 0, (1.0 - 2.0 ** (-5.0 - h)) ** np.maximum(gap, 0), 0.0) * 32 ** -0.5
        rtab[:, (2 + h) * T:(3 + h) * T] = decay
    bm = np.zeros((P, BMW), np.float32)
    q, k = p[:, None], p[None, :]
    bm[:, 0:P] = np.eye(P)
    bm[:, BM["causal"]:][:, :P] = np.where(k <= q, 0, NEG)
    bm[:, BM["stride4"]:][:, :P] = np.where((k <= q) & ((q - k) % 4 == 0), 0, NEG)
    bm[:, BM["reversed"]:][:, :P] = np.where(k > P - 1 - q, 0, NEG)
    for r in range(NT):
        gap = (r + NT * p)[:, None] - np.arange(T)[None, :]
        bm[:, BM["band"] + r * T:][:, :T] = np.where((gap >= 0) & (gap <= 128), 0, NEG)
    return tab, rtab, bm


def steps_block1():
    def pieces(k):
        return [("S", k)] * (k < 16) + [("T", k - 1)] * (1 <= k <= 16) + [("O", k - 2)] * (k >= 2) \
            + [("N", k)] * (k < 16)

    after_half = {7: [("R", 0)], 8: [("R", 2)], 9: [("R", 4)], 10: [("R", 6)], 11: [("R", 8), ("poolmm", 0)],
                  12: [("poolmm", 1), ("mean", 0)], 13: [("mean", 1)], 15: pieces(9),
                  17: pieces(12) + [("roots", 0)], 18: [("spread", 1)] + pieces(14), 19: pieces(16)}
    after_unit = {4: pieces(0), 5: pieces(1), 6: pieces(2), 7: pieces(3) + [("R", 1)], 8: [("R", 3)],
                  9: [("R", 5), ("pool", 0)], 10: [("R", 7), ("pool", 1)] + pieces(4), 11: pieces(5),
                  12: pieces(6), 13: pieces(7), 14: pieces(8), 15: pieces(10), 16: pieces(11) + [("squares", 0)],
                  17: pieces(13), 18: pieces(15), 19: pieces(17) + [("silu", 0), ("gated", 0), ("squares", 1)]}
    out = []
    for u, (kind, i) in enumerate(IN1):
        out += [("unit", u)] + after_half.get(u, []) + [("rest", u)]
        if u == 17:
            out.append(("spread", 0))
        if kind in ("v", "vr"):
            out.append(("vT", u))
        out += after_unit.get(u, [])
    after_chunk = {0: [("roots", 1)], 1: [("spread", 2)]}
    for i in range(KD):
        out += [("split", i), ("out", i)] + after_chunk.get(i, [])
    return out


def steps_block2():
    out, k = [], 0
    order = [("dil", i) for i in range(8)] + [("dil", 8 + i) for i in range(8)] + [("sb", i) for i in range(16)]
    ready = {}
    for n, (kind, i) in enumerate(order):
        ready[n] = 8 if n < 8 else 17 if n < 16 else 23
    n_items = len(order)

    def pieces(k):
        if k < n_items:
            out.append(("S", k))
        if 1 <= k <= n_items:
            out.append(("T", k - 1))
        if 2 <= k <= n_items + 1:
            out.append(("O", k - 2))
        if k < n_items:
            out.append(("N", k))

    for u, (kind, g, b) in enumerate(IN2):
        out += [("unit", u), ("rest", u)]
        if kind in ("v", "vs"):
            out.append(("vT", u))
        for _ in range(2 if u >= 23 else 1):
            if k < n_items and u >= ready[k]:
                pieces(k)
                k += 1
            elif k >= n_items and k < n_items + 2:
                pieces(k)
                k += 1
    while k < n_items + 2:
        pieces(k)
        k += 1
    return out


STEPS1, STEPS2 = steps_block1(), steps_block2()
ITEMS2 = [("dil", i) for i in range(16)] + [("sb", i) for i in range(16)]


def program(nc, aps):
    ctx = ExitStack()
    with ctx:
        def sb(name, shape, dt=F32):
            return ctx.enter_context(nc.sbuf_tensor(name, shape, dt))

        def sem(name):
            return ctx.enter_context(nc.semaphore(name))

        x_loaded = sem("x_loaded")
        vec_loaded = sem("vec_loaded")
        tab_loaded = sem("tab_loaded")
        rtab_loaded = sem("rtab_loaded")
        stored = sem("stored")
        w_hi_ready = sem("w_hi_ready")
        w_lo_ready = sem("w_lo_ready")
        unit_done = sem("unit_done")
        unit_evac = sem("unit_evac")
        down_evac = sem("down_evac")
        h_hi_ready = sem("h_hi_ready")
        h_lo_ready = sem("h_lo_ready")
        s_hi_ready = sem("s_hi_ready")
        s_lo_ready = sem("s_lo_ready")
        x_ready = sem("x_ready")
        y_ready = sem("y_ready")
        sq_ready = sem("sq_ready")
        sq_used = sem("sq_used")
        acc_ready = sem("acc_ready")
        misc_ready = sem("misc_ready")
        misc_free = sem("misc_free")
        token_sums = sem("token_sums")
        root_ready = sem("root_ready")
        factor_ready = sem("factor_ready")
        v_done = sem("v_done")
        vtok_ready = sem("vtok_ready")
        rope_ready = sem("rope_ready")
        out_free = sem("out_free")
        lam_dots = sem("lam_dots")
        lam_exp = sem("lam_exp")
        da_scores = sem("da_scores")
        da_max = sem("da_max")
        da_exp = sem("da_exp")
        da_coef = sem("da_coef")
        da_second = sem("da_second")
        da_comb = sem("da_comb")
        da_transposed = sem("da_transposed")
        da_pt = sem("da_pt")
        da_out = sem("da_out")
        ret_s = sem("ret_s")
        ret_p = sem("ret_p")
        ret_o = sem("ret_o")
        ret_gate = sem("ret_gate")
        pooled = sem("pooled")
        mix_sq = sem("mix_sq")
        mix_sums = sem("mix_sums")
        mix_root = sem("mix_root")
        mix_factor = sem("mix_factor")
        mixed = sem("mixed")
        mixed2 = sem("mixed2")
        tap_ready = sem("tap_ready")
        conv_done = sem("conv_done")
        gelu_ready = sem("gelu_ready")
        mlp_prod = sem("mlp_prod")
        silu_ready = sem("silu_ready")
        mlp_prod2 = sem("mlp_prod2")
        item_s = sem("item_s")
        dil_max = sem("dil_max")
        dil_s_read = sem("dil_s_read")
        dil_coef = sem("dil_coef")
        sb_s_read = sem("sb_s_read")
        sb_ln = sem("sb_ln")
        sb_arg = sem("sb_arg")
        item_p = sem("item_p")
        item_t = sem("item_t")
        item_pt = sem("item_pt")
        item_o = sem("item_o")
        gate2_exp = sem("gate2_exp")
        sb_step = sem("sb_step")
        vector_step = sem("vector_step")
        w_loaded = [sem(f"w_loaded{i}") for i in range(RAW)]

        x = sb("x", [P, KD, T])
        h_hi = sb("h_hi", [P, KD, T], F32R)
        h_lo = sb("h_lo", [P, KD, T], F32R)
        w_raw = sb("w_raw", [P, RAW, UW])
        w_hi = sb("w_hi", [P, RING, UW], F32R)
        w_lo = sb("w_lo", [P, RING, UW], F32R)
        s_hi = sb("s_hi", [P, 4, T], F32R)
        s_lo = sb("s_lo", [P, 4, T], F32R)
        rstd = sb("rstd", [P, T])
        tab = sb("tab", [P, TABW])
        bmask = sb("bmask", [P, BMW], BF16)
        vec1 = sb("vec1", [P, DEPTH, V1W])
        vec2 = sb("vec2", [P, DEPTH, V2W])
        pool_w = sb("pool_w", [P, DEPTH, 2, 64])
        sq = sb("sq", [P, 2, T])
        acc = sb("acc", [P, T])
        std = sb("std", [P, T])
        rope_cr = sb("rope_cr", [P, T])
        rope_sr = sb("rope_sr", [P, T])
        shuf = sb("shuf", [P, T])
        small = sb("small", [P, 112])
        arena_floats = 17424
        arena = sb("arena", [P, arena_floats])
        ps = ctx.enter_context(nc.psum_tensor("ps", [P, 8, T], F32))

        ident, ones, pair_mean = (tab[:, slice(*TAB[n])] for n in ("ident", "ones", "pair_mean"))
        eps, one = tab[:, slice(*TAB["eps"])], tab[:, slice(*TAB["one"])]
        inv_head = tab[:, slice(*TAB["inv_head"])].rearrange("p (b t) -> p b t", b=2)
        rope_c, rope_s = tab[:, slice(*TAB["rope_c"])], tab[:, slice(*TAB["rope_s"])]
        maskident = bmask[:, 0:P]

        def bm(name, width=P, at=0):
            return bmask[:, BM[name] + at:BM[name] + at + width]

        class Arena:

            def __init__(self):
                self.at = 0

            def __call__(self, *shape):
                n = int(np.prod(shape))
                assert self.at + n <= arena_floats, (self.at, n)
                part = arena[:, self.at:self.at + n]
                self.at += n
                if len(shape) == 2:
                    return part.rearrange("p (a b) -> p a b", a=shape[0])
                if len(shape) == 3:
                    return part.rearrange("p (a b c) -> p a b c", a=shape[0], b=shape[1])
                return part

        a = Arena()
        rtab = a(6, T)
        mix = a(8, T)
        qkr = a(2, T)
        vtok1 = a(NT, 6, P)
        gr = a(2, T)
        upad = a(2, 16 + T)
        vtmp1 = a(T)
        probs1 = a(2, T)
        comb1 = a(T)
        pt1 = a(T)
        ptmp = a(2, 16 + T)
        a = Arena()
        prod = a(KF, T)
        yf = a(KD, T)
        upads = a(2, 2 + T)
        taps = a(2, T)
        gate_s = taps
        a = Arena()
        qk2 = a(16, T)
        vtok2 = a(NT, 8, P)
        gates_end = a(4, T)
        pb2 = a(2 * T - 256)
        pt2 = a(2 * T - 256)
        vtmp2 = a(T)
        sb_a = a(T)
        sb_b = a(T)

        def k_at(h):
            return (mix[:, 4, :], rtab[:, 0, :], rtab[:, 1, :], qkr[:, 0, :])[h]

        HEAD_NORMS = ((0, 1, 4, 5), (2, 3))
        square_at = {0: sq[:, 0, :], 1: sq[:, 1, :], 4: std[:, :], 5: acc[:, :], 2: sq[:, 0, :], 3: sq[:, 1, :]}
        mix_roots, mix_factors = small[:, 48:80], small[:, 80:112]
        norm_columns = lambda c: slice(NT * c, NT * (c + 1)) if c < 4 else slice(8 * c - 16, 8 * c - 8)

        def gate_at(b):
            if b < 5:
                return qk2[:, [2, 4, 6, 8, 10][b], :]
            if b < 10:
                return qk2[:, [3, 5, 7, 9, 11][b - 5], :]
            return gates_end[:, b - 10, :] if b < 14 else qk2[:, b, :]

        S0, T0, OB, MB = 2, 4, 6, 7
        mixer_bank = lambda u: (0, 1, 4, 5)[u] if u < 4 else u % 2
        out_bank = lambda u: (0, 1, 5, 2, 3, 4, 6, 0)[u]
        RB = 5
        root, factor = small[:, 32:36], small[:, 36:40]

        base1 = lambda l: l * UNITS1
        base2 = lambda l: DEPTH * UNITS1 + l * UNITS2
        inner1 = lambda l: l * INNER1
        inner2 = lambda l: DEPTH * INNER1 + l * INNER2

        def count(value):
            return max(value, 0) if isinstance(value, int) else value

        class Own:

            def __init__(self, eng, first):
                self.eng, self.counts, self.moved, self.latest, self.first = eng, {}, {}, None, first

            def __call__(self, semaphore):
                self.counts[semaphore] = self.counts.get(semaphore, 0) + 1
                self.latest = semaphore
                return semaphore

            def value(self, semaphore):
                return self.counts.get(semaphore, 0) + self.moved.get(semaphore, 0)

            def last(self):
                return self.first if self.latest is None else (self.latest, self.value(self.latest))

            @contextmanager
            def loop(self, times, per):
                before = dict(self.counts)
                with self.eng.Fori(0, times) as i:
                    self.moved = {n: i * k for n, k in per.items()}
                    yield i
                self.moved = {}
                for n in set(self.counts) | set(per):
                    k = self.counts.get(n, 0) - before.get(n, 0)
                    assert k == per.get(n, 0), (n.name, k, per.get(n, 0))
                    self.counts[n] = before.get(n, 0) + times * k

        block = ctx.enter_context(nc.Block())

        @block.sync
        def _(sp):
            sp.dma_start(x[:, :, :], aps["x"]).then_inc(x_loaded, 16)
            sp.dma_start(vec1[:, :, :], aps["vec1"]).then_inc(vec_loaded, 16)

            def load(m, at):
                if at >= RAW:
                    sp.wait_ge(w_lo_ready, m - RAW + 1)
                sp.dma_start(w_raw[:, at % RAW, :], aps["w"][m, :, :]).then_inc(w_loaded[at % RAW], 16)

            for m in range(4):
                load(m, m)
            with sp.Fori(0, UNITS // 4 - 1) as i:
                for m in range(4, 8):
                    load(i * 4 + m, m)
            sp.wait_ge(y_ready, 1)
            sp.dma_start(aps["out"], x[:, :, :]).then_inc(stored, 16)
            sp.wait_ge(stored, 16)

        @block.gpsimd
        def _(pool):
            def split(m, at):
                pool.wait_ge(w_hi_ready, m + 1)
                if at >= RING:
                    pool.wait_ge(unit_done, m - RING + 1)
                raw, hi = w_raw[:, at % RAW, :], w_hi[:, at % RING, :]
                nc.gpsimd.tensor_tensor(w_lo[:, at % RING, :], raw, hi.bitcast(F32), ALU.subtract)\
                    .then_inc(w_lo_ready, 1)

            for m in range(4):
                split(m, m)
            with pool.Fori(0, UNITS // 4 - 1) as i:
                for m in range(4, 8):
                    split(i * 4 + m, m)

        @block.tensor
        def _(pe):
            own = Own(pe, (tab_loaded, 64))
            mm = nc.tensor.matmul
            misc = [0]
            outs = [0]
            downs = [0]
            chunks = [0]
            splits = [0]

            def three(out, w, mov, s, k0, hi, lo, start, stop):
                tile = slice(k0 * P, (k0 + 1) * P)
                mm(out, w_hi[:, s, tile], hi, start=start, stop=False)
                mm(out, w_hi[:, s, tile], lo, start=False, stop=False)
                return mm(out, w_lo[:, s, tile], hi, start=False, stop=stop)

            def unit_ready(n, at):
                pe.wait_ge(w_lo_ready, count(n + 1))

            def half_unit(n, bank, half):
                if half == 0:
                    unit_ready(n, n)
                for k in range(half * KD // 2, (half + 1) * KD // 2):
                    last = three(ps[:, bank, :], None, None, n % RING, k, h_hi[:, k, :], h_lo[:, k, :], k == 0,
                                 k == KD - 1)
                if half:
                    last.then_inc(own(unit_done), 1)

            def inner_unit(n, at, bank):
                unit_ready(n, at)
                for k in range(KD):
                    last = three(ps[:, bank, :], None, None, at % RING, k, h_hi[:, k, :], h_lo[:, k, :], k == 0,
                                 k == KD - 1)
                last.then_inc(own(unit_done), 1)

            def opening_block(n0, bank, i, k):
                pe.wait_ge(h_lo_ready, count(8 * splits[0] + i + 1))
                for u in range(3):
                    if i == 0:
                        unit_ready(n0 + u, n0 + u)
                        pe.wait_ge(down_evac, count(8 * (downs[0] - 1) + bank(u) + 1))
                    last = three(ps[:, bank(u), :], None, None, (n0 + u) % RING, k, h_hi[:, k, :],
                                 h_lo[:, k, :], i == 0, i == KD - 1)
                    if i == KD - 1:
                        last.then_inc(own(unit_done), 1)
                if i == KD - 1:
                    splits[0] += 1

            def opening_units(n0, bank, norm):
                for k in range(KD):
                    opening_block(n0, bank, k, k)
                if norm == "early":
                    sums_by_token()
                pe.wait_ge(down_evac, count(8 * (downs[0] - 1) + bank(3) + 1))
                half_unit(n0 + 3, bank(3), 0)
                if norm == "early":
                    spread_factor()
                elif norm == "late":
                    sums_by_token()
                half_unit(n0 + 3, bank(3), 1)
                if norm == "late":
                    spread_factor()

            def misc_wait():
                pe.wait_ge(misc_free, count(misc[0]))
                pe.wait_ge(vtok_ready, count(own.value(v_done)))

            def misc_mm(parts, reason, value):
                pe.wait_ge(reason, count(value))
                misc_wait()
                for out, lhs, rhs in parts:
                    last = mm(out, lhs, rhs, start=True, stop=True)
                last.then_inc(own(misc_ready), 1)
                misc[0] += 1

            sums = [0]

            def sums_by_token():
                sums[0] += 1
                pe.wait_ge(down_evac, count(KD * downs[0]))
                pe.wait_ge(acc_ready, count(sums[0]))
                misc_wait()
                for j in range(NT):
                    last = mm(ps[:, MB, j:j + 1], acc[:, j * P:(j + 1) * P], ones[:, 0:1], start=True, stop=True)
                last.then_inc(own(token_sums), 1)

            def spread_factor():
                pe.wait_ge(factor_ready, count(sums[0]))
                for j in range(NT):
                    last = nc.tensor.transpose(ps[:, MB, j * P:(j + 1) * P],
                                               factor[:, j:j + 1].to_broadcast((P, P)), ident)
                last.then_inc(own(misc_ready), 1)
                misc[0] += 1

            def mlp_up(n0, c0, norm):
                opening_units(n0, lambda u: u, norm)
                with own.loop(KF // 2 - 1, {unit_done: 4}) as i:
                    for u in range(4, 8):
                        pe.wait_ge(unit_evac, count(i * 4 + (c0 + u - 3)))
                        inner_unit(i * 4 + (n0 + u), n0 + u, u % 4)

            def mlp_down(n0, c0):
                r0 = chunks[0]

                def unit(k, at):
                    unit_ready(n0 + k, n0 + at)
                    pe.wait_ge(s_lo_ready, count(r0 + k + 1))
                    for b in (4, 5, 6, 7, 0, 1, 2, 3):
                        if at == 0 and b < 4:
                            pe.wait_ge(unit_evac, count(c0 - 3 + b))
                        if at == 0 and b == MB:
                            misc_wait()
                        last = three(ps[:, b, :], None, None, (n0 + at) % RING, b, s_hi[:, at % 4, :],
                                     s_lo[:, at % 4, :], at == 0, at == KF - 1)
                    last.then_inc(own(unit_done), 1)

                unit(0, 0)
                unit(1, 1)
                with own.loop(4, {unit_done: 4}) as i:
                    for k in range(2, 6):
                        unit(i * 4 + k, k)
                for k in range(18, 22):
                    unit(k, k)
                chunks[0] += KF
                downs[0] += 1

            def value_transposes(u_src, by4, evacuated):
                pe.wait_ge(unit_evac, count(evacuated))
                misc_wait()
                for i in range(NT):
                    src = u_src[:, i:T:NT] if by4 else u_src[:, i * P:(i + 1) * P]
                    last = nc.tensor.transpose(ps[:, MB, i * P:(i + 1) * P], src, ident)
                last.then_inc(own(v_done), 1)

            pe.wait_ge(tab_loaded, 64)

            def mixer1(l):
                n0, c0 = base1(l), inner1(l)

                def scores(k):
                    h, i = divmod(k, 4)
                    pe.wait_ge(rope_ready, count(10 * l + (2 * h + 4 if h else 2)))
                    pe.wait_ge(da_exp, count(2 * (16 * l + k)))
                    pe.wait_ge(ret_p, count(own.value(ret_s)))
                    w = (i + 1) * P
                    for m in range(2):
                        rows = slice(64 * m, 64 * m + 64)
                        mm(ps[:, S0 + m, 0:w], mix[rows, h, i * P:w], k_at(h)[rows, 0:w], start=True, stop=False)
                        last = mm(ps[:, S0 + m, i * P:w], maskident, bm("causal"), start=False, stop=True)
                    last.then_inc(own(da_scores), 1)

                def transposes(k):
                    h, i = divmod(k, 4)
                    if k == 0:
                        pe.wait_ge(unit_evac, count(c0 + 4))
                    pe.wait_ge(da_comb, count(16 * l + k + 1))
                    pe.wait_ge(da_pt, count(16 * l + k))
                    for t in range(i + 1):
                        last = nc.tensor.transpose(ps[:, T0, t * P:(t + 1) * P], comb1[:, t * P:(t + 1) * P], ident)
                    last.then_inc(own(da_transposed), 1)

                def outputs(k):
                    h, i = divmod(k, 4)
                    pe.wait_ge(da_pt, count(16 * l + k + 1))
                    pe.wait_ge(vtok_ready, count(6 * l + (h + 3 if h else 1)))
                    pe.wait_ge(out_free, count(outs[0]))
                    for t in range(i + 1):
                        last = mm(ps[:, OB, 0:P], vtok1[:, t, h, :], pt1[:, t * P:(t + 1) * P],
                                  start=t == 0, stop=t == i)
                    last.then_inc(own(da_out), 1)
                    outs[0] += 1

                def retention(n):
                    r0 = 8 * l
                    if n < 8:
                        hh = n // 2
                        rows = slice(32 * hh, 32 * hh + 32)
                        pe.wait_ge(rope_ready, count(10 * l + 4))
                        pe.wait_ge(da_exp, count(2 * own.value(da_scores)))
                        pe.wait_ge(ret_p, count(r0 + n))
                        for j in (2 * (n % 2), 2 * (n % 2) + 1):
                            last = mm(ps[:, S0 + j % 2, 0:T - j * P], qkr[rows, 1, j * P:(j + 1) * P],
                                      qkr[rows, 0, j * P:T], start=True, stop=True)
                        last.then_inc(own(ret_s), 1)
                    if n:
                        hh = (n - 1) // 2
                        half = slice(64 * (hh % 2), 64 * (hh % 2) + 64)
                        pe.wait_ge(ret_p, count(r0 + n))
                        pe.wait_ge(vtok_ready, count(6 * l + 3))
                        pe.wait_ge(unit_evac, count(c0 + 4))
                        if n in (1, 5):
                            pe.wait_ge(out_free, count(outs[0]))
                        for j in (2 * ((n - 1) % 2), 2 * ((n - 1) % 2) + 1):
                            last = mm(ps[half, RB, j * P:T], vtok1[:, j, 4 + hh // 2, half],
                                      sq[:, j % 2, 0:T - j * P], start=j == 0, stop=j == NT - 1)
                        last.then_inc(own(ret_o), 1)
                        if n in (4, 8):
                            outs[0] += 1

                def sums_of_heads(i):
                    pe.wait_ge(mix_sq, count(2 * l + i + 1))
                    misc_wait()
                    for c in HEAD_NORMS[i]:
                        to = ps[:, MB, norm_columns(c)]
                        for j in range(NT):
                            if c < 4:
                                last = mm(to[:, j:j + 1], square_at[c][:, j * P:(j + 1) * P], ones[:, 0:1],
                                          start=True, stop=True)
                            else:
                                last = mm(to[:, 2 * j:2 * j + 2], square_at[c][:, j * P:(j + 1) * P],
                                          pair_mean[:, 0:P:64], start=True, stop=True)
                    last.then_inc(own(mix_sums), 1)

                def spread_heads(i):
                    blocks = ((0, 1), (4, 5), (2, 3))[i]
                    pe.wait_ge(mix_factor, count(2 * l + (1 if i < 2 else 2)))
                    misc_wait()
                    for c, bank in zip(blocks, (MB, RB if i < 2 else S0 + 1)):
                        for j in range(NT):
                            f = mix_factors[:, norm_columns(c)]
                            tile = slice(j * P, (j + 1) * P)
                            if c < 4:
                                last = mm(ps[:, bank, tile], f[:, j:j + 1].to_broadcast((P, P)), ident,
                                          start=True, stop=True)
                            else:
                                for half in range(2):
                                    at = 2 * j + half
                                    last = mm(ps[64 * half:64 * half + 64, bank, tile],
                                              f[:, at:at + 1].to_broadcast((P, 64)), ident, start=True, stop=True)
                    last.then_inc(own(misc_ready), 1)
                    misc[0] += 1

                for what, k in STEPS1:
                    if what == "unit":
                        if k == 0:
                            opening_units(n0, mixer_bank, "late" if l else "early")
                        elif k >= 4:
                            pe.wait_ge(unit_evac, count(c0 + k - 1 if k > 5 else c0 + k - 3))
                            half_unit(n0 + k, mixer_bank(k), 0)
                    elif what == "rest" and k >= 4:
                        half_unit(n0 + k, mixer_bank(k), 1)
                    elif what == "vT":
                        value_transposes(vtmp1, False, c0 + k + 1)
                    elif what == "S":
                        scores(k)
                    elif what == "T":
                        transposes(k)
                    elif what == "O":
                        outputs(k)
                    elif what == "R":
                        retention(k)
                    elif what == "poolmm":
                        misc_mm([(ps[r:r + 64, MB, :], pool_w[r:r + 64, l, k, :], upad[r:r + 64, k, 16:])
                                 for r in (0, 64)], pooled, 2 * l + k + 1)
                    elif what == "mean":
                        misc_mm([(ps[:, MB, :], pair_mean, mix[:, 4 + k, :])], out_free, outs[0])
                    elif what == "roots":
                        sums_of_heads(k)
                    elif what == "spread":
                        spread_heads(k)
                    elif what == "out":
                        if k == 0:
                            pe.wait_ge(unit_evac, count(c0 + len(IN1)))
                            misc_wait()
                        opening_block(n0 + len(IN1), out_bank, k, OUT1[k])
                n = n0 + len(IN1)
                for u in range(3, KD):
                    pe.wait_ge(unit_evac, count(c0 + len(IN1) + u - 2 if u > 3 else 0))
                    inner_unit(n + u, n + u, out_bank(u))
                sums_by_token()
                spread_factor()

            def mixer2(l):
                n0, c0 = base2(l) + 3 * KF, inner2(l) + 2 * KF

                def scores(k):
                    kind, i = ITEMS2[k]
                    if k <= 16:
                        pe.wait_ge(dil_s_read, count(16 * l + k))
                        pe.wait_ge(sb_s_read, count(16 * l))
                    else:
                        pe.wait_ge(sb_s_read, count(16 * l + k - 16))
                    if kind == "dil":
                        hh, r = divmod(i, NT)
                        pp, rows = hh // 2, slice(64 * (hh % 2), 64 * (hh % 2) + 64)
                        pe.wait_ge(rope_ready, count(10 * DEPTH + 12 * l + 6 * pp + 6))
                        q = lambda grp: qk2[rows, 2 * grp + pp, r:T:NT]
                        kk = lambda grp: qk2[rows, 6 + 2 * grp + pp, :]
                        mm(ps[:, S0, :], q(0), kk(0), start=True, stop=False)
                        mm(ps[:, S0, :], maskident, bm("band", T, r * T), start=False, stop=True)
                        for grp, mask in ((1, "causal"), (2, "stride4")):
                            to = ps[:, S0 + 1, (grp - 1) * P:grp * P]
                            mm(to, q(grp), qk2[rows, 6 + 2 * grp + pp, r:T:NT], start=True, stop=False)
                            last = mm(to, maskident, bm(mask), start=False, stop=True)
                    else:
                        h, i = divmod(i, NT)
                        rows = slice(64 * (h % 2), 64 * (h % 2) + 64)
                        pe.wait_ge(unit_evac, count(c0 + IN2.index(("ks", 0, 1)) + 1))
                        w = (i + 1) * P
                        mm(ps[:, S0, 0:w], qk2[rows, 12 + h // 2, i * P:(i + 1) * P],
                           qk2[rows, 14 + h // 2, T - w:T], start=True, stop=False)
                        last = mm(ps[:, S0, 0:P], maskident, bm("reversed"), start=False, stop=True)
                    last.then_inc(own(item_s), 1)

                def tiles(k):
                    kind, i = ITEMS2[k]
                    return 6 if kind == "dil" else i % NT + 1

                def transposes(k):
                    g = 32 * l + k
                    if k == 0:
                        pe.wait_ge(unit_evac, count(c0 + 4))
                    pe.wait_ge(item_p, count(g + 1))
                    pe.wait_ge(item_pt, count(g))
                    for t in range(tiles(k)):
                        to = ps[:, T0 + t // 4, (t % 4) * P:(t % 4 + 1) * P]
                        last = nc.tensor.transpose(to, pb2[:, t * P:(t + 1) * P], ident)
                    last.then_inc(own(item_t), 1)

                def outputs(k):
                    kind, i = ITEMS2[k]
                    g = 32 * l + k
                    pe.wait_ge(item_pt, count(g + 1))
                    pe.wait_ge(out_free, count(outs[0]))
                    if kind == "dil":
                        hh, r = divmod(i, NT)
                        pp, half = hh // 2, 64 * (hh % 2)
                        pe.wait_ge(vtok_ready, count(6 * DEPTH + 8 * l + (3 if pp == 0 else 6)))
                        vs = [(t, pp) for t in range(NT)] + [(r, 2 + pp), (r, 4 + pp)]
                    else:
                        h, i = divmod(i, NT)
                        pp, half = h // 2, 64 * (h % 2)
                        pe.wait_ge(vtok_ready, count(6 * DEPTH + 8 * l + 8))
                        vs = [(NT - 1 - i + t, 6 + pp) for t in range(i + 1)]
                    for t, (tile, blk) in enumerate(vs):
                        last = mm(ps[half:half + 64, OB, 0:P], vtok2[:, tile, blk, half:half + 64],
                                  pt2[:, t * P:(t + 1) * P], start=t == 0, stop=t == len(vs) - 1)
                    last.then_inc(own(item_o), 1)
                    outs[0] += 1

                for what, k in STEPS2:
                    if what == "unit":
                        if k == 0:
                            opening_units(n0, mixer_bank, "early")
                        elif k >= 4:
                            pe.wait_ge(unit_evac, count(c0 + k - 1 if k > 5 else c0 + k - 3))
                            half_unit(n0 + k, mixer_bank(k), 0)
                    elif what == "rest":
                        if k >= 4:
                            half_unit(n0 + k, mixer_bank(k), 1)
                    elif what == "vT":
                        kind, g, b = IN2[k]
                        value_transposes(vtmp2, kind == "v" and g > 0, c0 + k + 1)
                    else:
                        {"S": scores, "T": transposes, "O": outputs, "N": lambda k: None}[what](k)
                nu = n0 + len(IN2)
                for u in range(4):
                    unit_ready(nu + u, nu + u)
                    pe.wait_ge(unit_evac, count(c0 + len(IN2) + max(u - 1, 0)))
                    if u == 0:
                        misc_wait()
                        pe.wait_ge(out_free, count(outs[0]))
                        pe.wait_ge(sb_s_read, count(16 * (l + 1)))
                    for j in range(4):
                        for k in range(2):
                            src = 2 * (j % 2) + k
                            if u == 0 and j < 2:
                                pe.wait_ge(s_lo_ready, count(chunks[0] + src + 1))
                            last = three(ps[:, 4 * (u % 2) + j, :], None, None, (nu + u) % RING, 2 * j + k,
                                         s_hi[:, src, :], s_lo[:, src, :], k == 0, k == 1)
                    last.then_inc(own(unit_done), 1)
                chunks[0] += 4
                n, c = nu + 4, c0 + len(IN2) + 4
                pe.wait_ge(unit_evac, count(c))
                opening_units(n, out_bank, None)
                for u in range(4, KD):
                    pe.wait_ge(unit_evac, count(c + u - 2))
                    inner_unit(n + u, n + u, out_bank(u))

            for l in range(DEPTH):
                mixer1(l)
                n, c = base1(l) + len(IN1) + KD, inner1(l) + len(IN1) + KD
                mlp_up(n, c, "late")
                mlp_down(n + 2 * KF, c + 2 * KF)
                sums_by_token()
                spread_factor()
            for l in range(DEPTH):
                mlp_up(base2(l), inner2(l), "early" if l else "late")
                mlp_down(base2(l) + 2 * KF, inner2(l) + 2 * KF)
                mixer2(l)
                n, c = base2(l) + 3 * KF + len(IN2) + 4 + KD, inner2(l) + 2 * KF + len(IN2) + 4 + KD
                mlp_up(n, c, "early")
                mlp_down(n + 2 * KF, c + 2 * KF)
            sums_by_token()
            spread_factor()

        @block.scalar
        def _(act):
            own = Own(act, (tab_loaded, 64))
            fn = nc.scalar.activation
            ahead = [0]
            sums = [0]
            misc = [0]
            roots = [0]

            def next_w(i=None, at=None):
                if i is None:
                    m = ahead[0]
                    if m < UNITS:
                        act.wait_ge(w_loaded[m % RAW], count((m // RAW + 1) * 16))
                        act.wait_ge(unit_done, count(m - RING + 1))
                        fn(w_hi[:, m % RING, :], w_raw[:, m % RAW, :], ACT.Copy).then_inc(own(w_hi_ready), 1)
                        ahead[0] += 1
                else:
                    act.wait_ge(w_loaded[at % RAW], count(i * (4 // RAW * 16) + (at // RAW + 1) * 16))
                    act.wait_ge(unit_done, count(i * 4 + (at - RING + 1)))
                    fn(w_hi[:, at % RING, :], w_raw[:, at % RAW, :], ACT.Copy).then_inc(own(w_hi_ready), 1)

            def square(c, source):
                if c < 2:
                    act.wait_ge(acc_ready, count(sums[0]))
                else:
                    act.wait_ge(sq_used, count(6 * sums[0] + max(1, c - 2)))
                fn(sq[:, c % 2, :], source, ACT.Square).then_inc(own(sq_ready), 1)
                if c == KD - 1:
                    sums[0] += 1

            def load_root():
                fn(small[:, 40:41], eps, ACT.Sqrt).then_inc(own(sb_step), 1)

            def root_of_sums():
                misc[0] += 1
                roots[0] += 1
                act.wait_ge(token_sums, count(roots[0]))
                fn(root, ps[:, MB, 0:NT], ACT.Sqrt, bias=eps, scale=1.0 / D).then_inc(own(root_ready), 1)

            xb = lambda c: x[:, c, :]

            def mlp_up1(n0, c0, l):
                def unit(i, u, at, prod0):
                    k = u if i is None else i * 4 + u
                    if i is not None or u % 2 == 0:
                        next_w(i, at)
                    act.wait_ge(unit_evac, count(c0 + k + 1))
                    act.wait_ge(mlp_prod, count(prod0 + (u // 2) if i is None else i * 2 + (prod0 + u // 2)))
                    if i is None:
                        blk = u // 2 + KF * (u % 2)
                    else:
                        blk = i * 2 + (u // 2 + KF * (u % 2))
                    w2 = vec1[:, l, bass.ds(V1["conv_w"] + 2 * 2 * KF + blk, 1)]
                    bias = vec1[:, l, bass.ds(V1["conv_b"] + blk, 1)]
                    fn(taps[:, u % 2, :], upads[:, u % 2, 2:], ACT.Identity, bias=bias, scale=w2)\
                        .then_inc(own(tap_ready), 1)
                    if u % 2:
                        act.wait_ge(conv_done, count(conv0 + k))
                        fn(taps[:, 0, :], taps[:, 0, :], ACT.Gelu_apprx_tanh).then_inc(own(gelu_ready), 1)

                conv0 = 2 * KF * l
                p0 = KF * l
                for u in range(4):
                    unit(None, u, n0 + u + AHEAD, p0)
                with own.loop(KF // 2 - 1, {w_hi_ready: 4, tap_ready: 4, gelu_ready: 2}) as i:
                    for u in range(4, 8):
                        unit(i, u, n0 + u + AHEAD, p0)
                ahead[0] += 4 * (KF // 2 - 1)

            def mlp_up2(n0, c0, d):
                def unit(i, u, at):
                    if i is not None or u % 2 == 0:
                        next_w(i, at)
                    if u % 2 == 0:
                        j = d * KF + u // 2
                        j = j if i is None else i * 2 + j
                        act.wait_ge(unit_evac, count(c0 + u + 1 if i is None else i * 4 + (c0 + u + 1)))
                        act.wait_ge(mlp_prod2, count(j))
                        fn(gate_s[:, 1, :], gate_s[:, 0, :], ACT.Silu).then_inc(own(silu_ready), 1)

                unit(None, 0, n0)
                unit(None, 1, n0)
                unit(None, 2, n0 + AHEAD)
                unit(None, 3, n0 + AHEAD)
                with own.loop(KF // 2 - 1, {w_hi_ready: 4, silu_ready: 2}) as i:
                    for u in range(4, 8):
                        unit(i, u, n0 + u + AHEAD)
                ahead[0] += 4 * (KF // 2 - 1)

            def mlp_down(n0, produced, name):
                def chunk(i, k):
                    kk = k if i is None else i * 4 + k
                    if i is None and k < 2:
                        act.wait_ge(name, count(produced + k + 1))
                        act.wait_ge(unit_done, count(n0 - 1))
                    elif i is None:
                        act.wait_ge(name, count(produced + min(k + 1, KF)))
                        act.wait_ge(unit_done, count(n0 + k - 3))
                    else:
                        act.wait_ge(name, count(i * 4 + (produced + k + 1)))
                        act.wait_ge(unit_done, count(i * 4 + (n0 + k - 3)))
                    fn(s_hi[:, k % 4, :], prod[:, kk, :], ACT.Copy).then_inc(own(s_hi_ready), 1)

                chunk(None, 0)
                chunk(None, 1)
                for k in range(2):
                    next_w()
                    chunk(None, k + 2)
                with own.loop(4, {w_hi_ready: 4, s_hi_ready: 4}) as i:
                    for k in range(2, 6):
                        next_w(i, n0 + k + AHEAD)
                        chunk(i, k + 2)
                ahead[0] += 16
                for k in range(18, 22):
                    next_w()
                    if k + 2 < KF:
                        chunk(None, k + 2)

            def mixer1(l):
                n0, c0 = base1(l), inner1(l)
                lam = 8 * l

                def exps(k):
                    h, i = divmod(k, 4)
                    w = (i + 1) * P
                    act.wait_ge(da_max, count(16 * l + k + 1))
                    act.wait_ge(da_comb, count(16 * l + k))
                    for m in range(2):
                        fn(probs1[:, m, 0:w], ps[:, S0 + m, 0:w], ACT.Exp, scale=DA_SCALE,
                           bias=small[:, 2 + m:3 + m], accum_out=small[:, 4 + m:5 + m])\
                            .then_inc(own(da_exp), 1)

                def second_map(k):
                    w = (k % 4 + 1) * P
                    act.wait_ge(da_coef, count(16 * l + k + 1))
                    fn(probs1[:, 1, 0:w], probs1[:, 1, 0:w], ACT.Copy, scale=small[:, 9:10])\
                        .then_inc(own(da_second), 1)

                def evac_t(k):
                    w = (k % 4 + 1) * P
                    act.wait_ge(da_transposed, count(16 * l + k + 1))
                    if k:
                        act.wait_ge(da_out, count(16 * l + k))
                    fn(pt1[:, 0:w], ps[:, T0, 0:w], ACT.Copy).then_inc(own(da_pt), 1)

                made = {}
                for what, k in STEPS1:
                    if what == "unit":
                        if k >= 2:
                            next_w()
                    elif what == "S":
                        exps(k)
                    elif what == "T":
                        evac_t(k)
                    elif what == "N":
                        second_map(k)
                    elif what == "poolmm":
                        misc[0] += 1
                        made[6 + k] = (misc_free, misc[0])
                    elif what == "mean":
                        misc[0] += 1
                        centred = misc[0]
                    elif what == "squares":
                        if k == 0:
                            act.wait_ge(misc_free, count(centred))
                            act.wait_ge(ret_o, count(8 * (l + 1)))
                        act.wait_ge(out_free, count(18 * l + (10 if k == 0 else 18)))
                        for c in HEAD_NORMS[k]:
                            fn(square_at[c], mix[:, c, :], ACT.Square)\
                                .then_inc(own(mix_sq if c == HEAD_NORMS[k][-1] else sb_step), 1)
                    elif what == "roots":
                        act.wait_ge(mix_sums, count(2 * l + k + 1))
                        at = slice(0, 8) if k == 0 else slice(8, 16)
                        fn(mix_roots[:, at], ps[:, MB, at], ACT.Sqrt, bias=eps, scale=1.0 / P)\
                            .then_inc(own(sb_step if k == 0 else mix_root), 1)
                        if k == 0:
                            fn(mix_roots[:, 16:32], ps[:, MB, 16:32], ACT.Sqrt, bias=eps).then_inc(own(mix_root), 1)
                    elif what == "spread":
                        misc[0] += 1
                        if k != 1:
                            c = 0 if k == 0 else 2
                            made[c] = (mixed, 4 * l + (1 if k == 0 else 4))
                            made[c + 1] = (misc_free, misc[0])
                    elif what == "silu":
                        act.wait_ge(unit_evac, count(c0 + len(IN1)))
                        for b in range(2):
                            fn(gr[:, b, :], gr[:, b, :], ACT.Silu).then_inc(own(ret_gate), 1)
                            made[4 + b] = (mixed, 4 * l + 2 + b)
                    elif what == "split":
                        if k == 0:
                            act.wait_ge(unit_done, count(n0 + len(IN1)))
                        c = OUT1[k]
                        act.wait_ge(*made[c])
                        fn(h_hi[:, c, :], mix[:, c, :], ACT.Copy).then_inc(own(h_hi_ready), 1)
                load_root()
                for u in range(KD):
                    next_w()
                    act.wait_ge(unit_evac, count(c0 + len(IN1) + u + 1))
                    square(u, yf[:, u, :])
                root_of_sums()

            def mixer2(l):
                n0, c0 = base2(l) + 3 * KF, inner2(l) + 2 * KF
                g0 = 32 * l
                gates = [0]

                def gate_exp():
                    b = gates[0]
                    if b < 16:
                        act.wait_ge(unit_evac, count(c0 + 24 + b + 1))
                        fn(gate_at(b), gate_at(b), ACT.Exp, scale=-1.0).then_inc(own(gate2_exp), 1)
                        gates[0] += 1

                def scores(k):
                    kind, i = ITEMS2[k]
                    g = g0 + k
                    if kind == "dil":
                        act.wait_ge(dil_max, count(16 * l + k + 1))
                        act.wait_ge(item_t, count(g))
                        fn(pb2[:, :], ps[:, S0:S0 + 2, :].rearrange("p a b -> p (a b)")[:, 0:768], ACT.Exp,
                           scale=DA_SCALE, bias=small[:, 11:12], accum_out=small[:, 12:13])\
                            .then_inc(own(dil_s_read), 1)
                    else:
                        j = 16 * l + k - 16
                        w = (i % NT + 1) * P
                        act.wait_ge(sb_s_read, count(j + 1))
                        act.wait_ge(sb_arg, count(j))
                        fn(sb_a[:, 0:w], sb_b[:, 0:w], ACT.Abs).then_inc(own(sb_step), 1)
                        act.wait_ge(*own.last())
                        fn(sb_a[:, 0:w], sb_a[:, 0:w], ACT.Exp, scale=-1.0).then_inc(own(sb_step), 1)
                        act.wait_ge(*own.last())
                        fn(sb_a[:, 0:w], sb_a[:, 0:w], ACT.Ln, bias=one).then_inc(own(sb_ln), 1)

                def normal(k):
                    kind, i = ITEMS2[k]
                    g = g0 + k
                    if kind == "dil":
                        act.wait_ge(dil_coef, count(16 * l + k + 1))
                        fn(pb2[:, :], pb2[:, :], ACT.Copy, scale=small[:, 13:14]).then_inc(own(item_p), 1)
                    else:
                        w = (i % NT + 1) * P
                        act.wait_ge(sb_arg, count(16 * l + k - 15))
                        act.wait_ge(item_t, count(g))
                        fn(pb2[:, 0:w], sb_b[:, 0:w], ACT.Exp).then_inc(own(item_p), 1)

                def evac_t(k):
                    kind, i = ITEMS2[k]
                    w = 768 if kind == "dil" else (i % NT + 1) * P
                    act.wait_ge(item_t, count(g0 + k + 1))
                    act.wait_ge(item_o, count(g0 + k))
                    fn(pt2[:, 0:w], ps[:, T0:T0 + 2, :].rearrange("p a b -> p (a b)")[:, 0:w], ACT.Copy)\
                        .then_inc(own(item_pt), 1)

                for what, k in STEPS2:
                    if what == "unit":
                        if k >= 2:
                            next_w()
                        if IN2[k][0] == "gate" and IN2[k][2] >= 1:
                            gate_exp()
                    elif what in "STN":
                        {"S": scores, "T": evac_t, "N": normal}[what](k)
                gate_exp()
                act.wait_ge(unit_done, count(n0 + len(IN2)))
                act.wait_ge(out_free, count(18 * DEPTH + 32 * (l + 1)))
                for c in range(4):
                    src = qk2[:, c, :] if c < 2 else qk2[:, 12 + c - 2, :]
                    fn(s_hi[:, c, :], src, ACT.Copy).then_inc(own(s_hi_ready), 1)
                for u in range(4):
                    next_w()
                for c in range(KD):
                    if c == 0:
                        act.wait_ge(unit_done, count(n0 + len(IN2)))
                    act.wait_ge(mixed2, count(8 * l + c + 1))
                    fn(h_hi[:, c, :], gate_at(c), ACT.Copy).then_inc(own(h_hi_ready), 1)
                for u in range(KD):
                    next_w()

            def prologue_loads(l):
                act.dma_start(rtab, aps["rtab"].rearrange("p (a b) -> p a b", a=6)).then_inc(rtab_loaded, 16)

            prologue_loads(0)
            act.dma_start(tab[:, :], aps["tab"]).then_inc(tab_loaded, 16)
            act.dma_start(bmask[:, :], aps["bmask"]).then_inc(tab_loaded, 16)
            act.dma_start(pool_w[:, :, :, :], aps["pool_w"]).then_inc(tab_loaded, 16)
            act.dma_start(vec2[:, :, :], aps["vec2"]).then_inc(tab_loaded, 16)
            act.wait_ge(x_loaded, 16)
            act.wait_ge(vec_loaded, 16)
            act.wait_ge(tab_loaded, 64)
            g1 = lambda l, name: vec1[:, l, V1[name]:V1[name] + KD]
            g2 = lambda l, name: vec2[:, l, V2[name]:V2[name] + KD]

            def split_x(gain, n_done, name, value):
                act.wait_ge(unit_done, count(n_done))
                for c in range(KD):
                    if name:
                        act.wait_ge(name, count(value + c + 1))
                    fn(h_hi[:, c, :], x[:, c, :], ACT.Copy, scale=gain[:, c:c + 1]).then_inc(own(h_hi_ready), 1)
                    square(c, xb(c))
                    if c == 3:
                        next_w()
                next_w()
                root_of_sums()

            def lambdas(l):
                act.wait_ge(lam_dots, count(l + 1))
                fn(small[:, 16 + 2 * l:18 + 2 * l], small[:, 16 + 2 * l:18 + 2 * l], ACT.Exp)\
                    .then_inc(own(lam_exp), 1)

            for l in range(DEPTH):
                lambdas(l)
            for _ in range(AHEAD):
                next_w()
            for l in range(DEPTH):
                n0 = base1(l)
                split_x(g1(l, "mix_pre"), n0, l and x_ready, 16 * l - 8)
                mixer1(l)
                n, c = n0 + len(IN1) + KD, inner1(l) + len(IN1) + KD
                split_x(g1(l, "mlp_pre"), n, x_ready, 16 * l)
                mlp_up1(n, c, l)
                mlp_down(n + 2 * KF, KF * l, mlp_prod)
                if l + 1 < DEPTH:
                    act.wait_ge(s_lo_ready, count(KF * (l + 1)))
                    act.wait_ge(*own.last())
                    prologue_loads(l + 1)
                load_root()
                for b in range(KD):
                    act.wait_ge(down_evac, count(8 * l + b + 1))
                    square(b, yf[:, b, :])
                root_of_sums()
            for l in range(DEPTH):
                n0 = base2(l)
                split_x(g2(l, "ffn1"), n0, down_evac if l else x_ready, 8 * (DEPTH + 2 * l - 1) if l else 8 * 3)
                mlp_up2(n0, inner2(l), 2 * l)
                mlp_down(n0 + 2 * KF, KF * 2 * l, mlp_prod2)
                split_x(g2(l, "mix"), n0 + 3 * KF, down_evac, 8 * (DEPTH + 2 * l))
                mixer2(l)
                n = n0 + 3 * KF + len(IN2) + 4 + KD
                split_x(g2(l, "ffn2"), n, unit_evac, inner2(l) + 2 * KF + len(IN2) + 4)
                mlp_up2(n, inner2(l) + 2 * KF + len(IN2) + 4 + KD, 2 * l + 1)
                mlp_down(n + 2 * KF, KF * (2 * l + 1), mlp_prod2)
            load_root()
            for c in range(KD):
                act.wait_ge(down_evac, count(8 * (3 * DEPTH - 1) + c + 1))
                square(c, xb(c))
            root_of_sums()

        @block.vector
        def _(dve):
            own = Own(dve, (tab_loaded, 64))
            v = nc.vector
            misc, outs, sums, splits, roots = [0], [0], [0], [0], [0]

            def low_h(c, source, gain=None, i=None):
                i = c if i is None else i
                dve.wait_ge(h_hi_ready, count(8 * splits[0] + i + 1))
                hi = h_hi[:, c, :].bitcast(F32)
                if gain is None:
                    dve.wait_ge(*own.last())
                    v.tensor_tensor(h_lo[:, c, :], source, hi, ALU.subtract).then_inc(own(h_lo_ready), 1)
                else:
                    dve.wait_ge(*own.last())
                    v.scalar_tensor_tensor(h_lo[:, c, :], source, gain[:, c:c + 1], hi, ALU.mult, ALU.subtract)\
                        .then_inc(own(h_lo_ready), 1)
                if i == KD - 1:
                    splits[0] += 1

            def add_square(c):
                if c == 0:
                    return
                dve.wait_ge(sq_ready, count(8 * sums[0] + c + 1))
                dve.wait_ge(*own.last())
                v.tensor_tensor(acc[:, :], sq[:, 0, :] if c == 1 else acc[:, :], sq[:, c % 2, :], ALU.add)\
                    .then_inc(own(acc_ready if c == KD - 1 else sq_used), 1)
                if c == KD - 1:
                    sums[0] += 1

            def norm_factor():
                roots[0] += 1
                dve.wait_ge(root_ready, count(roots[0]))
                dve.wait_ge(*own.last())
                v.reciprocal(factor, root).then_inc(own(factor_ready), 1)
                misc[0] += 1
                dve.wait_ge(misc_ready, count(misc[0]))
                dve.wait_ge(*own.last())
                v.tensor_copy(rstd[:, :], ps[:, MB, :]).then_inc(own(misc_free), 1)

            def prenorm(gain, update=None, lead=0):
                for c in range(KD + lead + 1):
                    if update is not None and c < KD:
                        update(c)
                    if 0 <= c - lead < KD:
                        low_h(c - lead, x[:, c - lead, :], gain)
                    if 0 <= c - lead - 1:
                        add_square(c - lead - 1)
                norm_factor()

            def add_normed(gain):
                def update(c):
                    dve.wait_ge(*own.last())
                    v.scalar_tensor_tensor(yf[:, c, :], yf[:, c, :], gain[:, c:c + 1], rstd[:, :], ALU.mult,
                                           ALU.mult).then_inc(own(vector_step), 1)
                    dve.wait_ge(*own.last())
                    v.tensor_tensor(x[:, c, :], x[:, c, :], yf[:, c, :], ALU.add).then_inc(own(x_ready), 1)
                return update

            def add_half(b):
                dve.wait_ge(*own.last())
                v.scalar_tensor_tensor(x[:, b, :], ps[:, b, :], 0.5, x[:, b, :], ALU.mult, ALU.add)\
                    .then_inc(own(down_evac), 1)

            def evac(u_done, bank, dst, by=None, to=unit_evac):
                dve.wait_ge(unit_done, count(u_done))
                dve.wait_ge(*own.last())
                v.tensor_tensor(dst, ps[:, bank, :], rstd[:, :] if by is None else by, ALU.mult).then_inc(own(to), 1)

            def rope(n, bank, dst, ready):
                dve.wait_ge(unit_done, count(n + 1))
                dve.wait_ge(*own.last())
                v.stream_shuffle(shuf[:, :], ps[:, bank, :], [(i + 8) % 16 if i < 16 else i for i in range(32)])\
                    .then_inc(own(vector_step), 1)
                dve.wait_ge(*own.last())
                v.tensor_tensor(dst, ps[:, bank, :], rope_cr[:, :], ALU.mult).then_inc(own(unit_evac), 1)
                dve.wait_ge(*own.last())
                v.tensor_tensor(shuf[:, :], shuf[:, :], rope_sr[:, :], ALU.mult).then_inc(own(vector_step), 1)
                dve.wait_ge(*own.last())
                v.tensor_tensor(dst, dst, shuf[:, :], ALU.add).then_inc(own(ready), 1)

            def rope_tables():
                dve.wait_ge(*own.last())
                v.tensor_tensor(rope_cr[:, :], rope_c, rstd[:, :], ALU.mult).then_inc(own(vector_step), 1)
                dve.wait_ge(*own.last())
                v.tensor_tensor(rope_sr[:, :], rope_s, rstd[:, :], ALU.mult).then_inc(own(vector_step), 1)

            vts = [0]

            def values(n, bank, tmp, dst, backward=False):
                dve.wait_ge(v_done, count(vts[0]))
                evac(n + 1, bank, tmp[:, ::-1] if backward else tmp, to=unit_evac)

            def values_by_token(dst):
                vts[0] += 1
                dve.wait_ge(v_done, count(vts[0]))
                dve.wait_ge(*own.last())
                v.tensor_copy(dst, ps[:, MB, :].rearrange("p (t d) -> p t d", t=NT)).then_inc(own(vtok_ready), 1)

            def mlp_up1(n0, c0, l):
                dve.wait_ge(*own.last())
                v.memset(upads[:, :, 0:2], 0.0).then_inc(own(vector_step), 1)

                def unit(i, u):
                    k = u if i is None else i * 4 + u
                    up, tp = upads[:, u % 2, :], taps[:, u % 2, :]
                    blk = u // 2 + KF * (u % 2)
                    if i is not None:
                        blk = i * 2 + blk
                    tap = lambda j: vec1[:, l, bass.ds(V1["conv_w"] + j * 2 * KF + blk, 1)]
                    evac(n0 + 1 + k, u % 4, up[:, 2:])
                    dve.wait_ge(tap_ready, count(2 * KF * l + k + 1))
                    dve.wait_ge(*own.last())
                    v.scalar_tensor_tensor(tp, up[:, 1:T + 1], tap(1), tp, ALU.mult, ALU.add)\
                        .then_inc(own(vector_step), 1)
                    dve.wait_ge(*own.last())
                    v.scalar_tensor_tensor(tp, up[:, 0:T], tap(0), tp, ALU.mult, ALU.add).then_inc(own(conv_done), 1)
                    if u % 2:
                        j = u // 2 if i is None else i * 2 + u // 2
                        dve.wait_ge(gelu_ready, count(KF * l + j + 1))
                        dve.wait_ge(*own.last())
                        v.tensor_tensor(prod[:, j, :], taps[:, 0, :], taps[:, 1, :], ALU.mult)\
                            .then_inc(own(mlp_prod), 1)

                for u in range(4):
                    unit(None, u)
                with own.loop(KF // 2 - 1, {vector_step: 4, unit_evac: 4, conv_done: 4, mlp_prod: 2}) as i:
                    for u in range(4, 8):
                        unit(i, u)

            def mlp_up2(n0, c0, d):
                def unit(i, u):
                    k = u if i is None else i * 4 + u
                    j = u // 2 if i is None else i * 2 + u // 2
                    if u % 2 == 0:
                        dve.wait_ge(silu_ready, count(KF * d + j))
                        dve.wait_ge(unit_done, count(n0 + 1 + k))
                        dve.wait_ge(*own.last())
                        v.tensor_tensor(gate_s[:, 0, :], ps[:, u % 4, :], rstd[:, :], ALU.mult)\
                            .then_inc(own(unit_evac), 1)
                    else:
                        evac(n0 + 1 + k, u % 4, prod[:, j, :])
                        dve.wait_ge(silu_ready, count(KF * d + j + 1))
                        dve.wait_ge(*own.last())
                        v.tensor_tensor(prod[:, j, :], prod[:, j, :], gate_s[:, 1, :], ALU.mult)\
                            .then_inc(own(mlp_prod2), 1)

                for u in range(4):
                    unit(None, u)
                with own.loop(KF // 2 - 1, {unit_evac: 4, mlp_prod2: 2}) as i:
                    for u in range(4, 8):
                        unit(i, u)

            chunks = [0]

            def mlp_down(n0):
                def chunk(i, k):
                    kk = k if i is None else i * 4 + k
                    dve.wait_ge(s_hi_ready, count(chunks[0] + 1 + kk))
                    dve.wait_ge(*own.last())
                    v.tensor_tensor(s_lo[:, k % 4, :], prod[:, kk, :], s_hi[:, k % 4, :].bitcast(F32),
                                    ALU.subtract).then_inc(own(s_lo_ready), 1)

                for k in range(4):
                    chunk(None, k)
                with own.loop(4, {s_lo_ready: 4}) as i:
                    for k in range(4, 8):
                        chunk(i, k)
                for k in range(20, 22):
                    chunk(None, k)
                chunks[0] += KF
                dve.wait_ge(unit_done, count(n0 + KF))

            def outputs(signal, value, dst, src):
                dve.wait_ge(signal, count(value))
                dve.wait_ge(*own.last())
                v.tensor_copy(dst, src).then_inc(own(out_free), 1)
                outs[0] += 1

            def mixer1(l):
                n0, c0 = base1(l), inner1(l)
                g = vec1[:, l, :]
                neglam, gain = small[:, 20 + l:21 + l], small[:, 24 + l:25 + l]

                def scores(k):
                    w = (k % 4 + 1) * P
                    dve.wait_ge(da_scores, count(16 * l + k + 1))
                    dve.wait_ge(*own.last())
                    v.tensor_reduce(small[:, 0:2], ps[:, S0:S0 + 2, 0:w], AX_X, ALU.max).then_inc(own(vector_step), 1)
                    dve.wait_ge(*own.last())
                    v.tensor_scalar(small[:, 2:4], small[:, 0:2], -DA_SCALE, None, ALU.mult).then_inc(own(da_max), 1)

                def normal(k):
                    w = (k % 4 + 1) * P
                    dve.wait_ge(da_exp, count(2 * (16 * l + k + 1)))
                    dve.wait_ge(*own.last())
                    v.reciprocal(small[:, 6:8], small[:, 4:6]).then_inc(own(vector_step), 1)
                    dve.wait_ge(*own.last())
                    v.tensor_tensor(small[:, 9:10], small[:, 7:8], neglam, ALU.mult).then_inc(own(da_coef), 1)
                    dve.wait_ge(da_second, count(16 * l + k + 1))
                    dve.wait_ge(da_transposed, count(16 * l + k))
                    dve.wait_ge(*own.last())
                    v.scalar_tensor_tensor(comb1[:, 0:w], probs1[:, 0, 0:w], small[:, 6:7], probs1[:, 1, 0:w],
                                           ALU.mult, ALU.add).then_inc(own(da_comb), 1)

                def retention(n):
                    if n in (4, 8):
                        outputs(ret_o, 8 * l + n, mix[:, 4 + n // 4 - 1, :], ps[:, RB, :])
                    if n < 8:
                        hh = n // 2
                        dve.wait_ge(ret_s, count(8 * l + n + 1))
                        dve.wait_ge(ret_o, count(8 * l + n))
                        for j in (2 * (n % 2), 2 * (n % 2) + 1):
                            w = T - j * P
                            dve.wait_ge(*own.last())
                            v.tensor_tensor(sq[:, j % 2, 0:w], ps[:, S0 + j % 2, 0:w], rtab[:, 2 + hh, 0:w],
                                            ALU.mult).then_inc(own(ret_p if j % 2 else vector_step), 1)

                for what, k in STEPS1:
                    if what == "rest":
                        kind, i = IN1[k]
                        bank, n = mixer_bank(k), n0 + k
                        if k == 0:
                            rope_tables()
                            dve.wait_ge(*own.last())
                            v.memset(upad[:, :, 0:16], 0.0).then_inc(own(vector_step), 1)
                        if kind in ("q", "k"):
                            rope(n, bank, mix[:, i, :] if kind == "q" else k_at(i), rope_ready)
                        elif kind in ("v", "vr"):
                            values(n, bank, vtmp1, None)
                        elif kind in ("qr", "kr"):
                            dst = qkr[:, kind == "kr", :]
                            evac(n + 1, bank, dst)
                            dve.wait_ge(*own.last())
                            v.stream_shuffle(shuf[:, :], dst, [(i + 16) % 32 for i in range(32)])\
                                .then_inc(own(vector_step), 1)
                            dve.wait_ge(rtab_loaded, count(16 * (l + 1)))
                            dve.wait_ge(*own.last())
                            v.tensor_tensor(shuf[:, :], shuf[:, :], rtab[:, 1, :], ALU.mult)\
                                .then_inc(own(vector_step), 1)
                            dve.wait_ge(*own.last())
                            v.tensor_tensor(dst, dst, rtab[:, 0, :], ALU.mult).then_inc(own(vector_step), 1)
                            dve.wait_ge(*own.last())
                            v.tensor_tensor(dst, dst, shuf[:, :], ALU.add).then_inc(own(rope_ready), 1)
                        elif kind == "g":
                            evac(n + 1, bank, gr[:, i, :])
                        else:
                            evac(n + 1, bank, upad[:, i, 16:])
                    elif what == "vT":
                        kind, i = IN1[k]
                        values_by_token(vtok1[:, :, i + 4 * (kind == "vr"), :])
                    elif what == "S":
                        scores(k)
                    elif what == "N":
                        normal(k)
                    elif what == "O":
                        h, i = divmod(k, 4)
                        outputs(da_out, 16 * l + k + 1, mix[:, h, i * P:(i + 1) * P], ps[:, OB, 0:P])
                    elif what == "R":
                        retention(k)
                    elif what == "pool":
                        b = k
                        u, t0, t1 = upad[:, b, :], ptmp[:, 0, :], ptmp[:, 1, :]
                        dve.wait_ge(*own.last())
                        v.tensor_tensor(t0[:, 1:], u[:, 1:], u[:, :-1], ALU.add).then_inc(own(vector_step), 1)
                        if b == 0:
                            dve.wait_ge(*own.last())
                            v.tensor_tensor(t1[64:, 3:], t0[64:, 3:], t0[64:, 1:-2], ALU.add)\
                                .then_inc(own(vector_step), 1)
                        else:
                            dve.wait_ge(*own.last())
                            v.tensor_tensor(t1[:, 3:], t0[:, 3:], t0[:, 1:-2], ALU.add)\
                                .then_inc(own(vector_step), 1)
                            dve.wait_ge(*own.last())
                            v.tensor_tensor(t0[:, 7:], t1[:, 7:], t1[:, 3:-4], ALU.add)\
                                .then_inc(own(vector_step), 1)
                            dve.wait_ge(*own.last())
                            v.tensor_tensor(t1[64:, 15:], t0[64:, 15:], t0[64:, 7:-8], ALU.add)\
                                .then_inc(own(vector_step), 1)
                        for rows, t in ((slice(0, 64), t0), (slice(64, 128), t1)):
                            dve.wait_ge(*own.last())
                            v.tensor_tensor(t[rows, 16:32], t[rows, 16:32], inv_head[rows, b, :], ALU.mult)\
                                .then_inc(own(vector_step), 1)
                            dve.wait_ge(*own.last())
                            v.tensor_tensor(u[rows, 16:32], t[rows, 16:32], u[rows, 16:32], ALU.subtract)\
                                .then_inc(own(vector_step), 1)
                            inv = tab[rows, TAB["inv_w"][0] + b:TAB["inv_w"][0] + b + 1]
                            dve.wait_ge(*own.last())
                            v.scalar_tensor_tensor(u[rows, 32:], t[rows, 32:], inv, u[rows, 32:], ALU.mult,
                                                   ALU.subtract)\
                                .then_inc(own(vector_step if rows.start == 0 else pooled), 1)
                    elif what == "poolmm":
                        misc[0] += 1
                        dve.wait_ge(misc_ready, count(misc[0]))
                        scale = g[:, V1["pool_scale"] + k:V1["pool_scale"] + k + 1]
                        dve.wait_ge(*own.last())
                        v.tensor_scalar(mix[:, 6 + k, :], ps[:, MB, :], scale, None, ALU.mult)\
                            .then_inc(own(misc_free), 1)
                    elif what == "mean":
                        misc[0] += 1
                        dve.wait_ge(misc_ready, count(misc[0]))
                        dve.wait_ge(*own.last())
                        v.tensor_tensor(mix[:, 4 + k, :], mix[:, 4 + k, :], ps[:, MB, :], ALU.subtract)\
                            .then_inc(own(misc_free), 1)
                    elif what == "roots":
                        dve.wait_ge(mix_root, count(2 * l + k + 1))
                        at = slice(0, 8) if k == 0 else slice(8, 16)
                        dve.wait_ge(*own.last())
                        v.reciprocal(mix_factors[:, at], mix_roots[:, at])\
                            .then_inc(own(vector_step if k == 0 else mix_factor), 1)
                        if k == 0:
                            dve.wait_ge(*own.last())
                            v.reciprocal(mix_factors[:, 16:32], mix_roots[:, 16:32]).then_inc(own(mix_factor), 1)
                    elif what == "spread":
                        misc[0] += 1
                        dve.wait_ge(misc_ready, count(misc[0]))
                        first = (0, 4, 2)[k]
                        for c, bank in ((first, MB), (first + 1, RB if k < 2 else S0 + 1)):
                            by = gain if c < 4 else g[:, V1["ret"] + c - 4:V1["ret"] + c - 3]
                            dve.wait_ge(*own.last())
                            v.scalar_tensor_tensor(mix[:, c, :], mix[:, c, :], by, ps[:, bank, :], ALU.mult,
                                                   ALU.mult)\
                                .then_inc(own(misc_free if bank != MB else vector_step if k == 1 else mixed), 1)
                    elif what == "gated":
                        for b in range(2):
                            dve.wait_ge(ret_gate, count(2 * l + b + 1))
                            dve.wait_ge(*own.last())
                            v.tensor_tensor(mix[:, 4 + b, :], mix[:, 4 + b, :], gr[:, b, :], ALU.mult)\
                                .then_inc(own(mixed), 1)
                    elif what == "split":
                        low_h(OUT1[k], mix[:, OUT1[k], :], None, k)
                for u in range(KD):
                    dve.wait_ge(unit_done, count(n0 + len(IN1) + u + 1))
                    dve.wait_ge(*own.last())
                    v.tensor_copy(yf[:, u, :], ps[:, out_bank(u), :]).then_inc(own(unit_evac), 1)
                    if u:
                        add_square(u - 1)
                add_square(KD - 1)
                norm_factor()

            def mixer2(l):
                n0, c0 = base2(l) + 3 * KF, inner2(l) + 2 * KF
                g0 = 32 * l
                wide = ps[:, S0:S0 + 2, :].rearrange("p a b -> p (a b)")[:, 0:768]

                def gate_finish(b):
                    dve.wait_ge(gate2_exp, count(16 * l + b + 1))
                    dve.wait_ge(*own.last())
                    v.tensor_scalar(gate_at(b), gate_at(b), 1.0, None, ALU.add).then_inc(own(vector_step), 1)
                    dve.wait_ge(*own.last())
                    v.reciprocal(gate_at(b), gate_at(b)).then_inc(own(vector_step), 1)

                def scores(k):
                    kind, i = ITEMS2[k]
                    dve.wait_ge(item_s, count(g0 + k + 1))
                    if kind == "dil":
                        dve.wait_ge(*own.last())
                        v.tensor_reduce(small[:, 10:11], wide, AX_X, ALU.max).then_inc(own(vector_step), 1)
                        dve.wait_ge(*own.last())
                        v.tensor_scalar(small[:, 11:12], small[:, 10:11], -DA_SCALE, None, ALU.mult)\
                            .then_inc(own(dil_max), 1)
                    else:
                        w = (i % NT + 1) * P
                        dve.wait_ge(item_p, count(g0 + k))
                        z, total = sb_b[:, 0:w], shuf[:, 0:w]
                        dve.wait_ge(*own.last())
                        v.tensor_scalar(z, ps[:, S0, 0:w], DA_SCALE, None, ALU.mult).then_inc(own(sb_s_read), 1)
                        dve.wait_ge(*own.last())
                        v.tensor_scalar(total, z, 0.0, None, ALU.max).then_inc(own(vector_step), 1)
                        dve.wait_ge(sb_ln, count(16 * l + k - 15))
                        dve.wait_ge(*own.last())
                        v.tensor_tensor_scan(total, total, sb_a[:, 0:w], 0.0, ALU.add, ALU.add)\
                            .then_inc(own(vector_step), 1)
                        dve.wait_ge(*own.last())
                        v.tensor_tensor(z, z, total, ALU.subtract).then_inc(own(sb_arg), 1)

                def normal(k):
                    kind, i = ITEMS2[k]
                    if kind == "dil":
                        dve.wait_ge(dil_s_read, count(16 * l + k + 1))
                        dve.wait_ge(*own.last())
                        v.reciprocal(small[:, 13:14], small[:, 12:13]).then_inc(own(dil_coef), 1)

                def output(k):
                    kind, i = ITEMS2[k]
                    h, r = divmod(i, NT)
                    half = slice(64 * (h % 2), 64 * (h % 2) + 64)
                    dst = qk2[half, h // 2, r:T:NT] if kind == "dil" else qk2[half, 12 + h // 2, r * P:(r + 1) * P]
                    outputs(item_o, g0 + k + 1, dst, ps[half, OB, 0:P])

                for what, k in STEPS2:
                    if what == "rest":
                        kind, g, b = IN2[k]
                        bank, n = mixer_bank(k), n0 + k
                        if k == 0:
                            rope_tables()
                        if kind in ("q", "k"):
                            rope(n, bank, qk2[:, 2 * g + b + 6 * (kind == "k"), :], rope_ready)
                        elif kind == "v":
                            values(n, bank, vtmp2, None)
                        elif kind == "vs":
                            values(n, bank, vtmp2, None, backward=True)
                        elif kind == "qs":
                            evac(n + 1, bank, qk2[:, 12 + b, :])
                        elif kind == "ks":
                            evac(n + 1, bank, qk2[:, 14 + b, ::-1])
                        else:
                            if b == 14:
                                dve.wait_ge(item_s, count(g0 + 32))
                            evac(n + 1, bank, gate_at(b))
                            if b >= 2:
                                gate_finish(b - 2)
                    elif what == "vT":
                        kind, g, b = IN2[k]
                        values_by_token(vtok2[:, :, 6 + b if kind == "vs" else 2 * g + b, :])
                    elif what in "SNO":
                        {"S": scores, "N": normal, "O": output}[what](k)
                gate_finish(14)
                gate_finish(15)
                for c in range(4):
                    src = qk2[:, c, :] if c < 2 else qk2[:, 12 + c - 2, :]
                    dve.wait_ge(s_hi_ready, count(chunks[0] + c + 1))
                    dve.wait_ge(*own.last())
                    v.tensor_tensor(s_lo[:, c, :], src, s_hi[:, c, :].bitcast(F32), ALU.subtract)\
                        .then_inc(own(s_lo_ready), 1)
                chunks[0] += 4
                for u in range(4):
                    dve.wait_ge(unit_done, count(n0 + len(IN2) + u + 1))
                    for j in range(4):
                        c = 2 * u + j // 2
                        gate = gate_at(c + 8 * (j % 2))
                        dve.wait_ge(*own.last())
                        v.tensor_tensor(gate, ps[:, 4 * (u % 2) + j, :], gate, ALU.mult)\
                            .then_inc(own(unit_evac if j == 3 else vector_step), 1)
                    for c in (2 * u, 2 * u + 1):
                        dve.wait_ge(*own.last())
                        v.tensor_tensor(gate_at(c), gate_at(c), gate_at(c + 8), ALU.add).then_inc(own(mixed2), 1)
                for c in range(KD):
                    low_h(c, gate_at(c))
                for c in range(KD):
                    dve.wait_ge(unit_done, count(n0 + len(IN2) + 4 + c + 1))
                    dve.wait_ge(*own.last())
                    v.tensor_tensor(x[:, c, :], x[:, c, :], ps[:, out_bank(c), :], ALU.add).then_inc(own(unit_evac), 1)

            dve.wait_ge(x_loaded, 16)
            dve.wait_ge(vec_loaded, 16)
            dve.wait_ge(tab_loaded, 64)
            for l in range(DEPTH):
                g = vec1[:, l, :]
                for m in range(2):
                    at = V1["lq1"] + 128 * m
                    dve.wait_ge(*own.last())
                    v.tensor_tensor(shuf[:, 0:64], g[:, at:at + 64], g[:, at + 64:at + 128], ALU.mult)\
                        .then_inc(own(vector_step), 1)
                    dve.wait_ge(*own.last())
                    v.reduce_sum(small[:, 16 + 2 * l + m:17 + 2 * l + m], shuf[:, 0:64], axis=AX_X)\
                        .then_inc(own(lam_dots if m else vector_step), 1)
            for l in range(DEPTH):
                g = vec1[:, l, :]
                dve.wait_ge(lam_exp, count(l + 1))
                dve.wait_ge(*own.last())
                v.tensor_tensor(small[:, 20 + l:21 + l], small[:, 17 + 2 * l:18 + 2 * l],
                                small[:, 16 + 2 * l:17 + 2 * l], ALU.subtract).then_inc(own(vector_step), 1)
                dve.wait_ge(*own.last())
                v.tensor_scalar(small[:, 20 + l:21 + l], small[:, 20 + l:21 + l], LAM_INIT[l], None,
                                ALU.subtract).then_inc(own(vector_step), 1)
                dve.wait_ge(*own.last())
                v.tensor_scalar(small[:, 24 + l:25 + l], g[:, V1["subln"]:V1["subln"] + 1], 1.0 - LAM_INIT[l],
                                None, ALU.mult).then_inc(own(vector_step), 1)
            def gains(vectors, at):
                return vectors[:, at:at + KD]

            prenorm(gains(vec1[:, 0, :], V1["mix_pre"]))
            for l in range(DEPTH):
                g = vec1[:, l, :]
                mixer1(l)
                n, c = base1(l) + len(IN1) + KD, inner1(l) + len(IN1) + KD
                prenorm(gains(g, V1["mlp_pre"]), add_normed(gains(g, V1["mix_post"])), 1)
                mlp_up1(n, c, l)
                mlp_down(n + 2 * KF)
                for b in range(KD):
                    dve.wait_ge(*own.last())
                    v.tensor_copy(yf[:, b, :], ps[:, b, :]).then_inc(own(down_evac), 1)
                for b in range(KD):
                    add_square(b)
                norm_factor()
                following = gains(vec1[:, l + 1, :], V1["mix_pre"]) if l + 1 < DEPTH else gains(vec2[:, 0, :], V2["ffn1"])
                prenorm(following, add_normed(gains(g, V1["mlp_post"])), 1)
            for l in range(DEPTH):
                n = base2(l)
                mlp_up2(n, 0, 2 * l)
                mlp_down(n + 2 * KF)
                prenorm(gains(vec2[:, l, :], V2["mix"]), add_half, 2)
                mixer2(l)
                n = n + 3 * KF + len(IN2) + 4 + KD
                prenorm(gains(vec2[:, l, :], V2["ffn2"]))
                mlp_up2(n, 0, 2 * l + 1)
                mlp_down(n + 2 * KF)
                if l + 1 < DEPTH:
                    prenorm(gains(vec2[:, l + 1, :], V2["ffn1"]), add_half, 2)
            for b in range(KD):
                add_half(b)
            for b in range(KD):
                add_square(b)
            norm_factor()
            final = vec2[:, 0, V2["final"]:V2["final"] + KD]
            for c in range(KD):
                dve.wait_ge(*own.last())
                v.scalar_tensor_tensor(x[:, c, :], x[:, c, :], final[:, c:c + 1], rstd[:, :], ALU.mult, ALU.mult)\
                    .then_inc(own(y_ready if c == KD - 1 else vector_step), 1)


def kernel(**inputs):
    import concourse.bacc as bacc
    from concourse.bass_utils import run_bass_kernel_spmd

    a = {k: np.ascontiguousarray(v) for k, v in inputs.items()}

    def blocks(w, order=None):
        k, f = w.shape
        tiles = w.reshape(k // P, P, f // P, P).transpose(2, 1, 0, 3).reshape(f // P, P, (k // P) * P)
        return tiles if order is None else tiles[order]

    def paired(w0, w1):
        return np.stack([blocks(w0), blocks(w1)], 1).reshape(-1, P, UW)

    def rows(w):
        return w.reshape(-1, P, UW)

    units = []
    for l in range(DEPTH):
        units.append(blocks(a["w_in"][l], [IN1_COLUMN[k] + i for k, i in IN1]))
        units.append(blocks(a["w_out"][l]))
        units.append(paired(a["w_up"][l][:, :FF], a["w_up"][l][:, FF:]))
        units.append(rows(a["w_down"][l]))
    for l in range(DEPTH):
        units.append(paired(a["ffn1_w_gate_2"][l], a["ffn1_w_up_2"][l]))
        units.append(rows(a["ffn1_w_down_2"][l]))
        units.append(blocks(a["w_in_2"][l], [IN2_COLUMN[k] + 2 * g + b for k, g, b in IN2]))
        both = np.stack([blocks(a["w_proj_dil_2"][l]), blocks(a["w_proj_sb_2"][l])], 2)
        units.append(both.reshape(4, 2, P, 2 * 2 * P).transpose(0, 2, 1, 3).reshape(4, P, UW))
        units.append(blocks(a["w_out_2"][l]))
        units.append(paired(a["ffn2_w_gate_2"][l], a["ffn2_w_up_2"][l]))
        units.append(rows(a["ffn2_w_down_2"][l]))
    w = np.concatenate(units)
    assert w.shape == (UNITS, P, UW)

    def columns(v):
        return v.reshape(-1, P).T

    def everywhere(v):
        return np.broadcast_to(v[None, :], (P, v.shape[0]))

    vec1 = np.stack([np.concatenate(
        [columns(a[n][l]) for n in ("norm_mix_pre", "norm_mix_post", "norm_mlp_pre", "norm_mlp_post", "diff_subln",
                                    "ret_norm", "pool_scale", "conv_b")]
        + [columns(a["conv_w"][l].reshape(-1))]
        + [everywhere(a[n][l]) for n in ("lambda_q1", "lambda_k1", "lambda_q2", "lambda_k2")], 1)
        for l in range(DEPTH)], 1)
    vec2 = np.stack([np.concatenate(
        [columns(a[n][l]) for n in ("norm_ffn1_2", "norm_mix_2", "norm_ffn2_2")] + [columns(a["norm_final_2"])], 1)
        for l in range(DEPTH)], 1)
    pool_w = a["pool_w"].reshape(DEPTH, 2, P, 64).transpose(2, 0, 1, 3)
    tab, rtab, bmask = constants()
    arrays = {
        "x": a["x"][0].T.reshape(KD, P, T).transpose(1, 0, 2), "w": w, "vec1": vec1, "vec2": vec2,
        "pool_w": pool_w, "tab": tab, "rtab": rtab, "bmask": bmask.astype(mybir.dt.np(BF16)),
    }
    nc = bacc.Bacc("TRN2", target_bir_lowering=False, num_devices=1)
    aps, ins = {}, {}
    for name, v in arrays.items():
        ins["in_" + name] = np.ascontiguousarray(v)
        aps[name] = nc.dram_tensor("in_" + name, v.shape, mybir.dt.from_np(v.dtype), kind="ExternalInput").ap()
    aps["out"] = nc.dram_tensor("out", (P, KD, T), F32, kind="ExternalOutput").ap()
    program(nc, aps)
    got = run_bass_kernel_spmd(nc, [ins], core_ids=[0]).results[0]["out"]
    return np.ascontiguousarray(got.transpose(2, 1, 0).reshape(1, T, D))
```

```python
from contextlib import ExitStack, contextmanager

import numpy as np

import concourse.bass as bass
from concourse import mybir

F32 = mybir.dt.float32
F32R = mybir.dt.float32r
BF16 = mybir.dt.bfloat16
ALU = mybir.AluOpType
ACT = mybir.ActivationFunctionType
AX_X = mybir.AxisListType.X

P = 128
T = 512
D = 1024
KD = D // P
NT = T // P
DEPTH = 2
FF = 2816
KF = FF // P
UNIT = 8
UW = UNIT * P
RAW = 2
RING = 4
AHEAD = 3
EPS = 1e-6
LAM_INIT = [0.8 - 0.6 * float(np.exp(-0.3 * l)) for l in range(DEPTH)]
DA_SCALE = 64 ** -0.5
NEG = -(2.0 ** 100)

IN1 = [("q", 0), ("k", 0), ("v", 0), ("qr", 0), ("kr", 0), ("vr", 0), ("vr", 1), ("u", 0), ("u", 1)]
IN1 = IN1 + [(w, h) for h in range(1, 4) for w in "qkv"] + [("g", 0), ("g", 1)]
OUT1 = (6, 7, 0, 1, 4, 5, 2, 3)
IN1_COLUMN = {"q": 0, "k": 4, "v": 8, "qr": 12, "kr": 13, "vr": 14, "g": 16, "u": 18}
IN2 = [(w, g, pp) for pp in range(2) for w in "qkv" for g in range(3)]
IN2 = IN2 + [(w + "s", 0, pp) for w in "qkv" for pp in range(2)] + [("gate", 0, b) for b in range(16)]
IN2_COLUMN = {"q": 0, "k": 6, "v": 12, "qs": 18, "ks": 20, "vs": 22, "gate": 24}
UNITS1 = len(IN1) + KD + 2 * KF + KF
UNITS2 = 2 * (2 * KF + KF) + len(IN2) + 4 + KD
UNITS = DEPTH * (UNITS1 + UNITS2)
INNER1 = len(IN1) + KD + 2 * KF
INNER2 = 2 * 2 * KF + len(IN2) + 4 + KD

TAB = {}
_at = 0
for _name, _w in (("ident", P), ("ones", P), ("pair_mean", P), ("eps", 1), ("one", 1), ("inv_w", 2),
                  ("inv_head", 32), ("rope_c", T), ("rope_s", T)):
    TAB[_name] = (_at, _at + _w)
    _at += _w
TABW = _at
RTABW = 2 * T + 4 * T
BM = {"ident": 0, "causal": P, "stride4": 2 * P, "reversed": 3 * P, "band": 4 * P}
BMW = 4 * P + NT * T

V1 = {}
_at = 0
for _name, _w in (("mix_pre", KD), ("mix_post", KD), ("mlp_pre", KD), ("mlp_post", KD), ("subln", 1),
                  ("ret", 2), ("pool_scale", 2), ("conv_b", 2 * KF), ("conv_w", 3 * 2 * KF), ("lq1", 64),
                  ("lk1", 64), ("lq2", 64), ("lk2", 64)):
    V1[_name] = _at
    _at += _w
V1W = _at
V2 = {"ffn1": 0, "mix": KD, "ffn2": 2 * KD, "final": 3 * KD}
V2W = 4 * KD


def constants():
    t = np.arange(T, dtype=np.float32)
    p = np.arange(P)

    def rope(theta, rot, head):
        inv = np.float32(theta) ** (-np.arange(0, rot, 2, dtype=np.float32) / np.float32(rot))
        half = rot // 2
        ang = t[None, :] * inv[(p % head) % half][:, None].astype(np.float32)
        turned = ((p % head) < rot)[:, None]
        sign = np.where((p % head) < half, -1.0, 1.0)[:, None]
        c = np.where(turned, np.cos(ang.astype(np.float64)), 1.0)
        s = np.where(turned, sign * np.sin(ang.astype(np.float64)), 0.0)
        return c, s

    tab = np.zeros((P, TABW), np.float32)

    def put(name, a):
        tab[:, TAB[name][0]:TAB[name][1]] = a

    put("ident", np.eye(P))
    put("ones", 1.0)
    put("pair_mean", (p[:, None] // 64 == p[None, :] // 64) / 64.0)
    put("eps", EPS)
    put("one", 1.0)
    window = np.stack([np.where(p < 64, 2, 4), np.where(p < 64, 8, 16)], 1)
    put("inv_w", 1.0 / window)
    first = np.arange(16)
    put("inv_head", (1.0 / np.minimum(first[None, None, :] + 1, window[:, :, None])).reshape(P, 32))
    c, s = rope(500000.0, 16, 64)
    put("rope_c", c)
    put("rope_s", s)
    rtab = np.zeros((P, RTABW), np.float32)
    rtab[:, 0:T], rtab[:, T:2 * T] = rope(10000.0, 32, 32)
    for h in range(4):
        gap = np.arange(T)[None, :] - p[:, None]
        decay = np.where(gap >= 0, (1.0 - 2.0 ** (-5.0 - h)) ** np.maximum(gap, 0), 0.0) * 32 ** -0.5
        rtab[:, (2 + h) * T:(3 + h) * T] = decay
    bm = np.zeros((P, BMW), np.float32)
    q, k = p[:, None], p[None, :]
    bm[:, 0:P] = np.eye(P)
    bm[:, BM["causal"]:][:, :P] = np.where(k <= q, 0, NEG)
    bm[:, BM["stride4"]:][:, :P] = np.where((k <= q) & ((q - k) % 4 == 0), 0, NEG)
    bm[:, BM["reversed"]:][:, :P] = np.where(k > P - 1 - q, 0, NEG)
    for r in range(NT):
        gap = (r + NT * p)[:, None] - np.arange(T)[None, :]
        bm[:, BM["band"] + r * T:][:, :T] = np.where((gap >= 0) & (gap <= 128), 0, NEG)
    return tab, rtab, bm


def steps_block1():
    def pieces(k):
        return [("S", k)] * (k < 16) + [("T", k - 1)] * (1 <= k <= 16) + [("O", k - 2)] * (k >= 2) \
            + [("N", k)] * (k < 16)

    after_half = {7: [("R", 0)], 8: [("R", 2)], 9: [("R", 4)], 10: [("R", 6)],
                  11: [("R", 8), ("poolmm", 0)], 12: [("poolmm", 1), ("mean", 0)] + pieces(5),
                  13: [("mean", 1)], 15: pieces(9), 17: pieces(12) + [("roots", 0)], 18: [("spread", 1)] + pieces(14), 19: pieces(16)}
    after_unit = {4: pieces(0), 5: pieces(1), 6: pieces(2), 7: pieces(3) + [("R", 1)], 8: [("R", 3)],
                  9: [("R", 5), ("pool", 0)], 10: [("R", 7), ("pool", 1)], 11: pieces(4),
                  12: pieces(6), 13: pieces(7), 14: pieces(8), 15: pieces(10), 16: pieces(11) + [("squares", 0)],
                  17: pieces(13), 18: pieces(15),
                  19: [("split", 0), ("split", 1)] + pieces(17) + [("out", 0), ("silu", 0), ("squares", 1), ("out", 1),
                      ("gated", 0), ("split", 2), ("split", 3), ("out", 2), ("roots", 1), ("out", 3), ("split", 4),
                      ("split", 5), ("out", 4), ("spread", 2), ("out", 5), ("split", 6), ("split", 7), ("out", 6),
                      ("out", 7)]}
    out = []
    for u in range(len(IN1)):
        transposes = [("vT", 2)] if u == 5 else [("vT", u - 1)] if u > 5 and IN1[u - 1][0] in ("v", "vr") else []
        out += [("unit", u)] + transposes + after_half.get(u, []) + [("rest", u)]
        if u == 17:
            out.append(("spread", 0))
        out += after_unit.get(u, [])
    return out


def steps_block2():
    def pieces(k):
        return [("S", k)] * (k < 16) + [("T", k - 1)] * (1 <= k <= 16) + [("O", k - 2)] * (k >= 2) \
            + [("N", k)] * (k < 16)

    after_half = {9: pieces(2), 18: pieces(10), 19: pieces(12), 20: pieces(14), 21: pieces(16)}
    after_unit = {7: pieces(0), 8: pieces(1), 16: pieces(8), 17: pieces(9), 18: pieces(11), 19: pieces(13),
                  20: pieces(15), 21: pieces(17)}
    for k in range(3, 8):
        after_unit[k + 6] = pieces(k)
    for j in range(8):
        after_unit[22 + 2 * j] = [("S", 16 + j)]
        if j:
            after_unit[23 + 2 * j] = [("T", 15 + j)]
            after_half[24 + 2 * j] = [("O", 15 + j)]
    after_half[38] += [("E", 23)]
    after_unit[38] = [("T", 23)]
    after_half[39] = [("O", 23)]
    out = []
    for u in range(len(IN2)):
        transposes = [("vT", u - 1)] if u and IN2[u - 1][0] in ("v", "vs") else []
        out += [("unit", u)] + transposes + after_half.get(u, []) + [("rest", u)] + after_unit.get(u, [])
    return out


STEPS1, STEPS2 = steps_block1(), steps_block2()
ITEMS2 = [("dil", i) for i in range(16)] + [("sb", i) for i in range(8)]
NI = len(ITEMS2)


def program(nc, aps):
    ctx = ExitStack()
    with ctx:
        def sb(name, shape, dt=F32):
            return ctx.enter_context(nc.sbuf_tensor(name, shape, dt))

        def sem(name):
            return ctx.enter_context(nc.semaphore(name))

        x_loaded = [sem(f"x_loaded{i}") for i in range(4)]
        gains_loaded = sem("gains_loaded")
        tab_loaded = sem("tab_loaded")
        vec_loaded = sem("vec_loaded")
        rest_loaded = sem("rest_loaded")
        turns_loaded = sem("turns_loaded")
        rtab_loaded = sem("rtab_loaded")
        stored = sem("stored")
        w_hi_ready = sem("w_hi_ready")
        w_lo_ready = sem("w_lo_ready")
        unit_done = sem("unit_done")
        unit_evac = sem("unit_evac")
        down_done = sem("down_done")
        down_evac = sem("down_evac")
        h_hi_ready = sem("h_hi_ready")
        h_lo_ready = sem("h_lo_ready")
        s_hi_ready = sem("s_hi_ready")
        s_lo_ready = sem("s_lo_ready")
        x_ready = sem("x_ready")
        y_ready = sem("y_ready")
        sq_ready = sem("sq_ready")
        sq_used = sem("sq_used")
        acc_ready = sem("acc_ready")
        misc_ready = sem("misc_ready")
        misc_free = sem("misc_free")
        token_sums = sem("token_sums")
        root_ready = sem("root_ready")
        factor_ready = sem("factor_ready")
        v_done = sem("v_done")
        vtok_ready = sem("vtok_ready")
        rope_ready = sem("rope_ready")
        out_free = sem("out_free")
        lam_dots = sem("lam_dots")
        lam_exp = sem("lam_exp")
        da_scores = sem("da_scores")
        da_max = sem("da_max")
        da_exp = sem("da_exp")
        da_coef = sem("da_coef")
        da_second = sem("da_second")
        da_comb = sem("da_comb")
        da_transposed = sem("da_transposed")
        da_pt = sem("da_pt")
        da_out = sem("da_out")
        ret_s = sem("ret_s")
        ret_p = sem("ret_p")
        ret_o = sem("ret_o")
        ret_gate = sem("ret_gate")
        pooled = sem("pooled")
        mix_sq = sem("mix_sq")
        mix_sums = sem("mix_sums")
        mix_root = sem("mix_root")
        mix_factor = sem("mix_factor")
        mixed = sem("mixed")
        mixed2 = sem("mixed2")
        tap_ready = sem("tap_ready")
        conv_done = sem("conv_done")
        gelu_ready = sem("gelu_ready")
        mlp_prod = sem("mlp_prod")
        silu_ready = sem("silu_ready")
        mlp_prod2 = sem("mlp_prod2")
        item_s = sem("item_s")
        dil_max = sem("dil_max")
        dil_s_read = sem("dil_s_read")
        dil_coef = sem("dil_coef")
        sb_s_read = sem("sb_s_read")
        sb_ln = sem("sb_ln")
        sb_arg = sem("sb_arg")
        item_p = sem("item_p")
        item_t = sem("item_t")
        item_pt = sem("item_pt")
        item_o = sem("item_o")
        gate2_ready = sem("gate2_ready")
        sb_step = sem("sb_step")
        vector_step = sem("vector_step")
        w_loaded = [sem(f"w_loaded{i}") for i in range(RAW)]

        x = sb("x", [P, KD, T])
        h_hi = sb("h_hi", [P, KD, T], F32R)
        h_lo = sb("h_lo", [P, KD, T], F32R)
        w_raw = sb("w_raw", [P, RAW, UW])
        w_hi = sb("w_hi", [P, RING, UW], F32R)
        w_lo = sb("w_lo", [P, RING, UW], F32R)
        s_hi = sb("s_hi", [P, 4, T], F32R)
        s_lo = sb("s_lo", [P, 4, T], F32R)
        rstd = sb("rstd", [P, T])
        tab = sb("tab", [P, TABW])
        bmask = sb("bmask", [P, BMW], BF16)
        vec1 = sb("vec1", [P, DEPTH, V1W])
        vec2 = sb("vec2", [P, DEPTH, V2W])
        pool_w = sb("pool_w", [P, DEPTH, 2, 64])
        sq = sb("sq", [P, 2, T])
        acc = sb("acc", [P, T])
        std = sb("std", [P, T])
        rope_csr = sb("rope_csr", [P, 2, T])
        rope_cr, rope_sr = rope_csr[:, 0, :], rope_csr[:, 1, :]
        shuf = sb("shuf", [P, T])
        small = sb("small", [P, 112])
        arena_floats = 17424
        arena = sb("arena", [P, arena_floats])
        ps = ctx.enter_context(nc.psum_tensor("ps", [P, 8, T], F32))

        ident, ones, pair_mean = (tab[:, slice(*TAB[n])] for n in ("ident", "ones", "pair_mean"))
        eps, one = tab[:, slice(*TAB["eps"])], tab[:, slice(*TAB["one"])]
        inv_head = tab[:, slice(*TAB["inv_head"])].rearrange("p (b t) -> p b t", b=2)
        rope_c, rope_s = tab[:, slice(*TAB["rope_c"])], tab[:, slice(*TAB["rope_s"])]
        maskident = bmask[:, 0:P]

        def bm(name, width=P, at=0):
            return bmask[:, BM[name] + at:BM[name] + at + width]

        class Arena:

            def __init__(self):
                self.at = 0

            def __call__(self, *shape):
                n = int(np.prod(shape))
                assert self.at + n <= arena_floats, (self.at, n)
                part = arena[:, self.at:self.at + n]
                self.at += n
                if len(shape) == 2:
                    return part.rearrange("p (a b) -> p a b", a=shape[0])
                if len(shape) == 3:
                    return part.rearrange("p (a b c) -> p a b c", a=shape[0], b=shape[1])
                return part

        a = Arena()
        rtab = a(6, T)
        mix = a(8, T)
        qkr = a(2, T)
        vtok1 = a(NT, 6, P)
        gr = a(2, T)
        upad = a(2, 16 + T)
        vtmp1 = a(T)
        probs1 = a(2, T)
        comb1 = a(T)
        pt1 = a(T)
        ptmp = a(2, 16 + T)
        a = Arena()
        prod = a(KF, T)
        yf = a(KD, T)
        upads = a(2, 2 + T)
        taps = a(2, T)
        gate_s = taps
        a = Arena()
        qk2 = a(16, T)
        vtok2 = a(NT, 8, P)
        gates_end = a(4, T)
        pb2 = a(2 * T)
        pt2 = a(2 * T)
        sb_z = a(2, T)
        vtmp2 = std[:, :]
        sb_log = sq
        sb_sum = rope_csr

        def k_at(h):
            return (mix[:, 4, :], rtab[:, 0, :], rtab[:, 1, :], qkr[:, 0, :])[h]

        HEAD_NORMS = ((0, 1, 4, 5), (2, 3))
        square_at = {0: sq[:, 0, :], 1: sq[:, 1, :], 4: std[:, :], 5: acc[:, :], 2: sq[:, 0, :], 3: sq[:, 1, :]}
        mix_roots, mix_factors = small[:, 48:80], small[:, 80:112]
        norm_columns = lambda c: slice(NT * c, NT * (c + 1)) if c < 4 else slice(8 * c - 16, 8 * c - 8)

        def gate_at(b):
            if b < 5:
                return qk2[:, [2, 4, 6, 8, 10][b], :]
            if b < 10:
                return qk2[:, [3, 5, 7, 9, 11][b - 5], :]
            return gates_end[:, b - 10, :] if b < 14 else qk2[:, b, :]

        S0, T0, OB, MB = 2, 4, 6, 7
        mixer_bank = lambda u: (0, 1, 4, 5)[u] if u < 4 else u % 2
        out_bank = lambda u: (0, 1, 5, 2, 3, 4, 6, 0)[u]
        out_bank2 = lambda u: (0, 1, 2, 3, 4, 5, 6, 4)[u]
        RB = 5
        root, factor = small[:, 32:36], small[:, 36:40]

        base1 = lambda l: l * UNITS1
        base2 = lambda l: DEPTH * UNITS1 + l * UNITS2
        inner1 = lambda l: l * INNER1
        inner2 = lambda l: DEPTH * INNER1 + l * INNER2

        def count(value):
            return max(value, 0) if isinstance(value, int) else value

        class Own:

            def __init__(self, eng, first):
                self.eng, self.counts, self.moved, self.latest, self.first = eng, {}, {}, None, first

            def __call__(self, semaphore):
                self.counts[semaphore] = self.counts.get(semaphore, 0) + 1
                self.latest = semaphore
                return semaphore

            def value(self, semaphore):
                return self.counts.get(semaphore, 0) + self.moved.get(semaphore, 0)

            def last(self):
                return self.first if self.latest is None else (self.latest, self.value(self.latest))

            @contextmanager
            def loop(self, times, per):
                before = dict(self.counts)
                with self.eng.Fori(0, times) as i:
                    self.moved = {n: i * k for n, k in per.items()}
                    yield i
                self.moved = {}
                for n in set(self.counts) | set(per):
                    k = self.counts.get(n, 0) - before.get(n, 0)
                    assert k == per.get(n, 0), (n.name, k, per.get(n, 0))
                    self.counts[n] = before.get(n, 0) + times * k

        block = ctx.enter_context(nc.Block())

        @block.sync
        def _(sp):
            sp.dma_start(vec1[:, :, 0:4 * KD], aps["vec1"][:, :, 0:4 * KD]).then_inc(gains_loaded, 16)

            def load(m, at):
                if at >= RAW:
                    sp.wait_ge(w_lo_ready, m - RAW + 1)
                sp.dma_start(w_raw[:, at % RAW, :], aps["w"][m, :, :]).then_inc(w_loaded[at % RAW], 16)

            for m in range(4):
                load(m, m)
            with sp.Fori(0, UNITS // 4 - 1) as i:
                for m in range(4, 8):
                    load(i * 4 + m, m)
            for c in range(0, KD, 2):
                sp.wait_ge(y_ready, c + 2)
                sp.dma_start(aps["out"][:, c:c + 2, :], x[:, c:c + 2, :]).then_inc(stored, 16)
            sp.wait_ge(stored, 4 * 16)

        @block.gpsimd
        def _(pool):
            def split(m, at):
                pool.wait_ge(w_hi_ready, m + 1)
                if at >= RING:
                    pool.wait_ge(unit_done, m - RING + 1)
                raw, hi = w_raw[:, at % RAW, :], w_hi[:, at % RING, :]
                nc.gpsimd.tensor_tensor(w_lo[:, at % RING, :], raw, hi.bitcast(F32), ALU.subtract)\
                    .then_inc(w_lo_ready, 1)

            for m in range(4):
                split(m, m)
            with pool.Fori(0, UNITS // 4 - 1) as i:
                for m in range(4, 8):
                    split(i * 4 + m, m)

        @block.tensor
        def _(pe):
            own = Own(pe, (tab_loaded, 16))
            mm = nc.tensor.matmul
            misc = [0]
            outs = [0]
            downs = [0]
            chunks = [0]
            splits = [0]

            def three(out, s, k0, hi, lo, start, stop):
                tile = slice(k0 * P, (k0 + 1) * P)
                mm(out, w_hi[:, s, tile], hi, start=start, stop=False)
                mm(out, w_hi[:, s, tile], lo, start=False, stop=False)
                return mm(out, w_lo[:, s, tile], hi, start=False, stop=stop)

            def unit_ready(n, at):
                pe.wait_ge(w_lo_ready, count(n + 1))

            def half_unit(n, bank, half):
                if half == 0:
                    unit_ready(n, n)
                for k in range(half * KD // 2, (half + 1) * KD // 2):
                    last = three(ps[:, bank, :], n % RING, k, h_hi[:, k, :], h_lo[:, k, :], k == 0,
                                 k == KD - 1)
                if half:
                    last.then_inc(own(unit_done), 1)

            def inner_unit(n, at, bank):
                unit_ready(n, at)
                for k in range(KD):
                    last = three(ps[:, bank, :], at % RING, k, h_hi[:, k, :], h_lo[:, k, :], k == 0,
                                 k == KD - 1)
                last.then_inc(own(unit_done), 1)

            def opening_block(n0, bank, i, k):
                pe.wait_ge(h_lo_ready, count(8 * splits[0] + i + 1))
                for u in range(3):
                    if i == 0:
                        unit_ready(n0 + u, n0 + u)
                        pe.wait_ge(down_evac, count(8 * (downs[0] - 1) + bank(u) + 1))
                    last = three(ps[:, bank(u), :], (n0 + u) % RING, k, h_hi[:, k, :],
                                 h_lo[:, k, :], i == 0, i == KD - 1)
                    if i == KD - 1:
                        last.then_inc(own(unit_done), 1)
                if i == KD - 1:
                    splits[0] += 1

            def opening_units(n0, bank, norm):
                for k in range(KD):
                    opening_block(n0, bank, k, k)
                if norm == "early":
                    sums_by_token()
                pe.wait_ge(down_evac, count(8 * (downs[0] - 1) + bank(3) + 1))
                half_unit(n0 + 3, bank(3), 0)
                if norm == "early":
                    spread_factor()
                elif norm == "late":
                    sums_by_token()
                half_unit(n0 + 3, bank(3), 1)
                if norm == "late":
                    spread_factor()

            def misc_wait():
                pe.wait_ge(misc_free, count(misc[0]))
                pe.wait_ge(vtok_ready, count(own.value(v_done)))

            def misc_mm(parts, reason, value):
                pe.wait_ge(reason, count(value))
                misc_wait()
                for out, lhs, rhs in parts:
                    last = mm(out, lhs, rhs, start=True, stop=True)
                last.then_inc(own(misc_ready), 1)
                misc[0] += 1

            sums = [0]

            def sums_by_token():
                sums[0] += 1
                if sums[0] == 1:
                    pe.wait_ge(tab_loaded, 16)
                pe.wait_ge(down_evac, count(KD * downs[0]))
                pe.wait_ge(acc_ready, count(sums[0]))
                misc_wait()
                for j in range(NT):
                    last = mm(ps[:, MB, j:j + 1], acc[:, j * P:(j + 1) * P], ones[:, 0:1], start=True, stop=True)
                last.then_inc(own(token_sums), 1)

            def spread_factor():
                pe.wait_ge(factor_ready, count(sums[0]))
                for j in range(NT):
                    last = nc.tensor.transpose(ps[:, MB, j * P:(j + 1) * P],
                                               factor[:, j:j + 1].to_broadcast((P, P)), ident)
                last.then_inc(own(misc_ready), 1)
                misc[0] += 1

            def mlp_up(n0, c0, norm):
                opening_units(n0, lambda u: u, norm)
                with own.loop(KF // 2 - 1, {unit_done: 4}) as i:
                    for u in range(4, 8):
                        pe.wait_ge(unit_evac, count(i * 4 + (c0 + u - 3)))
                        inner_unit(i * 4 + (n0 + u), n0 + u, u % 4)

            def mlp_down(n0, c0):
                r0 = chunks[0]

                def unit(k, at):
                    unit_ready(n0 + k, n0 + at)
                    pe.wait_ge(s_lo_ready, count(r0 + k + 1))
                    for b in range(KD) if at >= 2 else (4, 5, 6, 7, 0, 1, 2, 3):
                        if at == 0 and b < 4:
                            pe.wait_ge(unit_evac, count(c0 - 3 + b))
                        if at == 0 and b == MB:
                            misc_wait()
                        last = three(ps[:, b, :], (n0 + at) % RING, b, s_hi[:, at % 4, :],
                                     s_lo[:, at % 4, :], at == 0, at == KF - 1)
                        if at == KF - 1 and b < KD - 1:
                            last.then_inc(own(down_done), 1)
                    last.then_inc(own(unit_done), 1)

                unit(0, 0)
                unit(1, 1)
                with own.loop(4, {unit_done: 4}) as i:
                    for k in range(2, 6):
                        unit(i * 4 + k, k)
                for k in range(18, 22):
                    unit(k, k)
                chunks[0] += KF
                downs[0] += 1

            def value_transposes(u_src, by4, evacuated):
                pe.wait_ge(unit_evac, count(evacuated))
                misc_wait()
                for i in range(NT):
                    src = u_src[:, i:T:NT] if by4 else u_src[:, i * P:(i + 1) * P]
                    last = nc.tensor.transpose(ps[:, MB, i * P:(i + 1) * P], src, ident)
                last.then_inc(own(v_done), 1)

            def mixer1(l):
                n0, c0 = base1(l), inner1(l)

                def scores(k):
                    h, i = divmod(k, 4)
                    pe.wait_ge(rope_ready, count(10 * l + (2 * h + 4 if h else 2)))
                    pe.wait_ge(da_exp, count(2 * (16 * l + k)))
                    pe.wait_ge(ret_p, count(own.value(ret_s)))
                    w = (i + 1) * P
                    for m in range(2):
                        rows = slice(64 * m, 64 * m + 64)
                        mm(ps[:, S0 + m, 0:w], mix[rows, h, i * P:w], k_at(h)[rows, 0:w], start=True, stop=False)
                        last = mm(ps[:, S0 + m, i * P:w], maskident, bm("causal"), start=False, stop=True)
                    last.then_inc(own(da_scores), 1)

                def transposes(k):
                    h, i = divmod(k, 4)
                    if k == 0:
                        pe.wait_ge(unit_evac, count(c0 + 4))
                    pe.wait_ge(da_comb, count(16 * l + k + 1))
                    pe.wait_ge(da_pt, count(16 * l + k))
                    for t in range(i + 1):
                        last = nc.tensor.transpose(ps[:, T0, t * P:(t + 1) * P], comb1[:, t * P:(t + 1) * P], ident)
                    last.then_inc(own(da_transposed), 1)

                def outputs(k):
                    h, i = divmod(k, 4)
                    pe.wait_ge(da_pt, count(16 * l + k + 1))
                    pe.wait_ge(vtok_ready, count(6 * l + (h + 3 if h else 1)))
                    pe.wait_ge(out_free, count(outs[0]))
                    for t in range(i + 1):
                        last = mm(ps[:, OB, 0:P], vtok1[:, t, h, :], pt1[:, t * P:(t + 1) * P],
                                  start=t == 0, stop=t == i)
                    last.then_inc(own(da_out), 1)
                    outs[0] += 1

                def retention(n):
                    r0 = 8 * l
                    if n < 8:
                        hh = n // 2
                        rows = slice(32 * hh, 32 * hh + 32)
                        pe.wait_ge(rope_ready, count(10 * l + 4))
                        pe.wait_ge(da_exp, count(2 * own.value(da_scores)))
                        pe.wait_ge(ret_p, count(r0 + n))
                        for j in (2 * (n % 2), 2 * (n % 2) + 1):
                            last = mm(ps[:, S0 + j % 2, 0:T - j * P], qkr[rows, 1, j * P:(j + 1) * P],
                                      qkr[rows, 0, j * P:T], start=True, stop=True)
                        last.then_inc(own(ret_s), 1)
                    if n:
                        hh = (n - 1) // 2
                        half = slice(64 * (hh % 2), 64 * (hh % 2) + 64)
                        pe.wait_ge(ret_p, count(r0 + n))
                        pe.wait_ge(vtok_ready, count(6 * l + 3))
                        pe.wait_ge(unit_evac, count(c0 + 4))
                        if n in (1, 5):
                            pe.wait_ge(out_free, count(outs[0]))
                        for j in (2 * ((n - 1) % 2), 2 * ((n - 1) % 2) + 1):
                            last = mm(ps[half, RB, j * P:T], vtok1[:, j, 4 + hh // 2, half],
                                      sq[:, j % 2, 0:T - j * P], start=j == 0, stop=j == NT - 1)
                        last.then_inc(own(ret_o), 1)
                        if n in (4, 8):
                            outs[0] += 1

                def sums_of_heads(i):
                    pe.wait_ge(mix_sq, count(2 * l + i + 1))
                    misc_wait()
                    for c in HEAD_NORMS[i]:
                        to = ps[:, MB, norm_columns(c)]
                        for j in range(NT):
                            if c < 4:
                                last = mm(to[:, j:j + 1], square_at[c][:, j * P:(j + 1) * P], ones[:, 0:1],
                                          start=True, stop=True)
                            else:
                                last = mm(to[:, 2 * j:2 * j + 2], square_at[c][:, j * P:(j + 1) * P],
                                          pair_mean[:, 0:P:64], start=True, stop=True)
                    last.then_inc(own(mix_sums), 1)

                def spread_heads(i):
                    blocks = ((0, 1), (4, 5), (2, 3))[i]
                    pe.wait_ge(mix_factor, count(2 * l + (1 if i < 2 else 2)))
                    misc_wait()
                    for c, bank in zip(blocks, (MB, RB if i < 2 else S0 + 1)):
                        for j in range(NT):
                            f = mix_factors[:, norm_columns(c)]
                            tile = slice(j * P, (j + 1) * P)
                            if c < 4:
                                last = mm(ps[:, bank, tile], f[:, j:j + 1].to_broadcast((P, P)), ident,
                                          start=True, stop=True)
                            else:
                                for half in range(2):
                                    at = 2 * j + half
                                    last = mm(ps[64 * half:64 * half + 64, bank, tile],
                                              f[:, at:at + 1].to_broadcast((P, 64)), ident, start=True, stop=True)
                    last.then_inc(own(misc_ready), 1)
                    misc[0] += 1

                for what, k in STEPS1:
                    if what == "unit":
                        if k == 0:
                            opening_units(n0, mixer_bank, "early")
                            if l == 0:
                                pe.wait_ge(rest_loaded, 48)
                        elif k >= 4:
                            pe.wait_ge(unit_evac, count(c0 + k - 1 if k > 5 else c0 + k - 3))
                            half_unit(n0 + k, mixer_bank(k), 0)
                    elif what == "rest" and k >= 4:
                        half_unit(n0 + k, mixer_bank(k), 1)
                    elif what == "vT":
                        value_transposes(vtmp1, False, c0 + k + 1)
                    elif what == "S":
                        scores(k)
                    elif what == "T":
                        transposes(k)
                    elif what == "O":
                        outputs(k)
                    elif what == "R":
                        retention(k)
                    elif what == "poolmm":
                        misc_mm([(ps[r:r + 64, MB, :], pool_w[r:r + 64, l, k, :], upad[r:r + 64, k, 16:])
                                 for r in (0, 64)], pooled, 2 * l + k + 1)
                    elif what == "mean":
                        misc_mm([(ps[:, MB, :], pair_mean, mix[:, 4 + k, :])], out_free, outs[0])
                    elif what == "roots":
                        sums_of_heads(k)
                    elif what == "spread":
                        spread_heads(k)
                    elif what == "out":
                        if k == 0:
                            pe.wait_ge(unit_evac, count(c0 + len(IN1)))
                            misc_wait()
                        opening_block(n0 + len(IN1), out_bank, k, OUT1[k])
                n = n0 + len(IN1)
                for u in range(3, KD):
                    pe.wait_ge(unit_evac, count(c0 + len(IN1) + u - 2 if u > 3 else 0))
                    inner_unit(n + u, n + u, out_bank(u))
                sums_by_token()
                spread_factor()

            def mixer2(l):
                n0, c0 = base2(l) + 3 * KF, inner2(l) + 2 * KF

                def scores(k):
                    kind, i = ITEMS2[k]
                    pe.wait_ge(dil_s_read, count(16 * l + min(k, 16)))
                    pe.wait_ge(sb_s_read, count(8 * l + max(k - 16, 0)))
                    if kind == "dil":
                        hh, r = divmod(i, NT)
                        pp, rows = hh // 2, slice(64 * (hh % 2), 64 * (hh % 2) + 64)
                        pe.wait_ge(rope_ready, count(10 * DEPTH + 12 * l + 6 * pp + 6))
                        q = lambda grp: qk2[rows, 2 * grp + pp, r:T:NT]
                        kk = lambda grp: qk2[rows, 6 + 2 * grp + pp, :]
                        mm(ps[:, S0, :], q(0), kk(0), start=True, stop=False)
                        mm(ps[:, S0, :], maskident, bm("band", T, r * T), start=False, stop=True)
                        for grp, mask in ((1, "causal"), (2, "stride4")):
                            to = ps[:, S0 + 1, (grp - 1) * P:grp * P]
                            mm(to, q(grp), qk2[rows, 6 + 2 * grp + pp, r:T:NT], start=True, stop=False)
                            last = mm(to, maskident, bm(mask), start=False, stop=True)
                    else:
                        pp, i = divmod(i, NT)
                        pe.wait_ge(unit_evac, count(c0 + IN2.index(("ks", 0, 1)) + 1))
                        w = (i + 1) * P
                        for hh in range(2):
                            rows = slice(64 * hh, 64 * hh + 64)
                            mm(ps[:, S0 + hh, 0:w], qk2[rows, 12 + pp, i * P:(i + 1) * P],
                               qk2[rows, 14 + pp, T - w:T], start=True, stop=False)
                            last = mm(ps[:, S0 + hh, 0:P], maskident, bm("reversed"), start=False, stop=True)
                    last.then_inc(own(item_s), 1)

                def tiles(k):
                    kind, i = ITEMS2[k]
                    return 6 if kind == "dil" else 2 * (i % NT + 1)

                def transposes(k):
                    g = NI * l + k
                    if k == 0:
                        pe.wait_ge(unit_evac, count(c0 + 4))
                    pe.wait_ge(item_p, count(g + 1))
                    pe.wait_ge(item_pt, count(g))
                    for t in range(tiles(k)):
                        to = ps[:, T0 + t // 4, (t % 4) * P:(t % 4 + 1) * P]
                        last = nc.tensor.transpose(to, pb2[:, t * P:(t + 1) * P], ident)
                    last.then_inc(own(item_t), 1)

                def outputs(k):
                    kind, i = ITEMS2[k]
                    g = NI * l + k
                    pe.wait_ge(item_pt, count(g + 1))
                    pe.wait_ge(out_free, count(outs[0]))
                    if kind == "dil":
                        hh, r = divmod(i, NT)
                        pp, half = hh // 2, 64 * (hh % 2)
                        pe.wait_ge(vtok_ready, count(6 * DEPTH + 8 * l + (3 if pp == 0 else 6)))
                        vs = [(half, [(t, pp) for t in range(NT)] + [(r, 2 + pp), (r, 4 + pp)])]
                    else:
                        pp, i = divmod(i, NT)
                        pe.wait_ge(vtok_ready, count(6 * DEPTH + 8 * l + 8))
                        vs = [(half, [(NT - 1 - i + t, 6 + pp) for t in range(i + 1)]) for half in (0, 64)]
                    at = 0
                    for half, tiles_of_values in vs:
                        for t, (tile, blk) in enumerate(tiles_of_values):
                            last = mm(ps[half:half + 64, OB, 0:P], vtok2[:, tile, blk, half:half + 64],
                                      pt2[:, at * P:(at + 1) * P], start=t == 0, stop=t == len(tiles_of_values) - 1)
                            at += 1
                    last.then_inc(own(item_o), 1)
                    outs[0] += 1

                for what, k in STEPS2:
                    if what == "unit":
                        if k == 0:
                            opening_units(n0, mixer_bank, "early")
                        elif k >= 4:
                            pe.wait_ge(unit_evac, count(c0 + k - 1 if k > 5 else c0 + k - 3))
                            half_unit(n0 + k, mixer_bank(k), 0)
                    elif what == "rest":
                        if k >= 4:
                            half_unit(n0 + k, mixer_bank(k), 1)
                    elif what == "vT":
                        kind, g, b = IN2[k]
                        value_transposes(vtmp2, kind == "v" and g > 0, c0 + k + 1)
                    elif what in "STO":
                        {"S": scores, "T": transposes, "O": outputs}[what](k)
                nu = n0 + len(IN2)
                for u in range(4):
                    unit_ready(nu + u, nu + u)
                    pe.wait_ge(unit_evac, count(c0 + len(IN2) + max(u - 1, 0)))
                    if u == 0:
                        misc_wait()
                        pe.wait_ge(out_free, count(outs[0]))
                        pe.wait_ge(sb_s_read, count(8 * (l + 1)))
                    for j in range(4):
                        for k in range(2):
                            src = 2 * (j % 2) + k
                            if u == 0 and j < 2:
                                pe.wait_ge(s_lo_ready, count(chunks[0] + src + 1))
                            last = three(ps[:, 4 * (u % 2) + j, :], (nu + u) % RING, 2 * j + k,
                                         s_hi[:, src, :], s_lo[:, src, :], k == 0, k == 1)
                    last.then_inc(own(unit_done), 1)
                chunks[0] += 4
                n, c = nu + 4, c0 + len(IN2) + 4
                pe.wait_ge(unit_evac, count(c - 1))
                opening_units(n, out_bank2, None)
                for u in range(4, KD):
                    pe.wait_ge(unit_evac, count(c + u - 2))
                    inner_unit(n + u, n + u, out_bank2(u))

            for l in range(DEPTH):
                mixer1(l)
                n, c = base1(l) + len(IN1) + KD, inner1(l) + len(IN1) + KD
                mlp_up(n, c, "late")
                mlp_down(n + 2 * KF, c + 2 * KF)
                sums_by_token()
                spread_factor()
            for l in range(DEPTH):
                mlp_up(base2(l), inner2(l), "early" if l else "late")
                mlp_down(base2(l) + 2 * KF, inner2(l) + 2 * KF)
                mixer2(l)
                n, c = base2(l) + 3 * KF + len(IN2) + 4 + KD, inner2(l) + 2 * KF + len(IN2) + 4 + KD
                mlp_up(n, c, "early")
                mlp_down(n + 2 * KF, c + 2 * KF)
            sums_by_token()
            spread_factor()

        @block.scalar
        def _(act):
            own = Own(act, (gains_loaded, 16))
            fn = nc.scalar.activation
            ahead = [0]
            sums = [0]
            misc = [0]
            roots = [0]

            def next_w(i=None, at=None):
                if i is None:
                    m = ahead[0]
                    if m < UNITS:
                        act.wait_ge(w_loaded[m % RAW], count((m // RAW + 1) * 16))
                        act.wait_ge(unit_done, count(m - RING + 1))
                        fn(w_hi[:, m % RING, :], w_raw[:, m % RAW, :], ACT.Copy).then_inc(own(w_hi_ready), 1)
                        ahead[0] += 1
                else:
                    act.wait_ge(w_loaded[at % RAW], count(i * (4 // RAW * 16) + (at // RAW + 1) * 16))
                    act.wait_ge(unit_done, count(i * 4 + (at - RING + 1)))
                    fn(w_hi[:, at % RING, :], w_raw[:, at % RAW, :], ACT.Copy).then_inc(own(w_hi_ready), 1)

            def square(c, source):
                if c < 2:
                    act.wait_ge(acc_ready, count(sums[0]))
                else:
                    act.wait_ge(sq_used, count(6 * sums[0] + max(1, c - 2)))
                fn(sq[:, c % 2, :], source, ACT.Square).then_inc(own(sq_ready), 1)
                if c == KD - 1:
                    sums[0] += 1

            def load_root():
                fn(small[:, 40:41], eps, ACT.Sqrt).then_inc(own(sb_step), 1)

            def root_of_sums():
                misc[0] += 1
                roots[0] += 1
                act.wait_ge(token_sums, count(roots[0]))
                fn(root, ps[:, MB, 0:NT], ACT.Sqrt, bias=eps, scale=1.0 / D).then_inc(own(root_ready), 1)

            xb = lambda c: x[:, c, :]

            def first_chunks(produced, name):
                for k in range(2):
                    act.wait_ge(name, count(produced + k + 1))
                    fn(s_hi[:, k, :], prod[:, k, :], ACT.Copy).then_inc(own(s_hi_ready), 1)

            def mlp_up1(n0, c0, l):
                def unit(i, u, at, prod0):
                    k = u if i is None else i * 4 + u
                    if i is not None or u % 2 == 0:
                        next_w(i, at)
                    act.wait_ge(unit_evac, count(c0 + k + 1))
                    act.wait_ge(mlp_prod, count(prod0 + (u // 2) if i is None else i * 2 + (prod0 + u // 2)))
                    if i is None:
                        blk = u // 2 + KF * (u % 2)
                    else:
                        blk = i * 2 + (u // 2 + KF * (u % 2))
                    w2 = vec1[:, l, bass.ds(V1["conv_w"] + 2 * 2 * KF + blk, 1)]
                    bias = vec1[:, l, bass.ds(V1["conv_b"] + blk, 1)]
                    fn(taps[:, u % 2, :], upads[:, u % 2, 2:], ACT.Identity, bias=bias, scale=w2)\
                        .then_inc(own(tap_ready), 1)
                    if u % 2:
                        act.wait_ge(conv_done, count(conv0 + k))
                        fn(taps[:, 0, :], taps[:, 0, :], ACT.Gelu_apprx_tanh).then_inc(own(gelu_ready), 1)

                conv0 = 2 * KF * l
                p0 = KF * l
                for u in range(4):
                    unit(None, u, n0 + u + AHEAD, p0)
                first_chunks(p0, mlp_prod)
                with own.loop(KF // 2 - 1, {w_hi_ready: 4, tap_ready: 4, gelu_ready: 2}) as i:
                    for u in range(4, 8):
                        unit(i, u, n0 + u + AHEAD, p0)
                ahead[0] += 4 * (KF // 2 - 1)

            def mlp_up2(n0, c0, d):
                def unit(i, u, at):
                    if i is not None or u % 2 == 0:
                        next_w(i, at)
                    if u % 2 == 0:
                        j = d * KF + u // 2
                        j = j if i is None else i * 2 + j
                        act.wait_ge(unit_evac, count(c0 + u + 1 if i is None else i * 4 + (c0 + u + 1)))
                        act.wait_ge(mlp_prod2, count(j))
                        fn(gate_s[:, 1, :], gate_s[:, 0, :], ACT.Silu).then_inc(own(silu_ready), 1)

                unit(None, 0, n0)
                unit(None, 1, n0)
                unit(None, 2, n0 + AHEAD)
                unit(None, 3, n0 + AHEAD)
                first_chunks(KF * d, mlp_prod2)
                with own.loop(KF // 2 - 1, {w_hi_ready: 4, silu_ready: 2}) as i:
                    for u in range(4, 8):
                        unit(i, u, n0 + u + AHEAD)
                ahead[0] += 4 * (KF // 2 - 1)

            def mlp_down(n0, produced, name):
                def chunk(i, k):
                    kk = k if i is None else i * 4 + k
                    if i is None:
                        act.wait_ge(name, count(produced + min(k + 1, KF)))
                        act.wait_ge(unit_done, count(n0 + k - 3))
                    else:
                        act.wait_ge(name, count(i * 4 + (produced + k + 1)))
                        act.wait_ge(unit_done, count(i * 4 + (n0 + k - 3)))
                    fn(s_hi[:, k % 4, :], prod[:, kk, :], ACT.Copy).then_inc(own(s_hi_ready), 1)

                for k in range(2):
                    next_w()
                    chunk(None, k + 2)
                with own.loop(4, {w_hi_ready: 4, s_hi_ready: 4}) as i:
                    for k in range(2, 6):
                        next_w(i, n0 + k + AHEAD)
                        chunk(i, k + 2)
                ahead[0] += 16
                for k in range(18, 22):
                    next_w()
                    if k + 2 < KF:
                        chunk(None, k + 2)

            def mixer1(l):
                n0, c0 = base1(l), inner1(l)
                lam = 8 * l

                def exps(k):
                    h, i = divmod(k, 4)
                    w = (i + 1) * P
                    act.wait_ge(da_max, count(16 * l + k + 1))
                    act.wait_ge(da_comb, count(16 * l + k))
                    for m in range(2):
                        fn(probs1[:, m, 0:w], ps[:, S0 + m, 0:w], ACT.Exp, scale=DA_SCALE,
                           bias=small[:, 2 + m:3 + m], accum_out=small[:, 4 + m:5 + m])\
                            .then_inc(own(da_exp), 1)

                def second_map(k):
                    w = (k % 4 + 1) * P
                    act.wait_ge(da_coef, count(16 * l + k + 1))
                    fn(probs1[:, 1, 0:w], probs1[:, 1, 0:w], ACT.Copy, scale=small[:, 9:10])\
                        .then_inc(own(da_second), 1)

                def evac_t(k):
                    w = (k % 4 + 1) * P
                    act.wait_ge(da_transposed, count(16 * l + k + 1))
                    if k:
                        act.wait_ge(da_out, count(16 * l + k))
                    fn(pt1[:, 0:w], ps[:, T0, 0:w], ACT.Copy).then_inc(own(da_pt), 1)

                made = {}
                for what, k in STEPS1:
                    if what == "unit":
                        if k >= 2:
                            next_w()
                    elif what == "S":
                        exps(k)
                    elif what == "T":
                        evac_t(k)
                    elif what == "N":
                        second_map(k)
                    elif what == "poolmm":
                        misc[0] += 1
                        made[6 + k] = (misc_free, misc[0])
                    elif what == "mean":
                        misc[0] += 1
                        centred = misc[0]
                    elif what == "squares":
                        if k == 0:
                            act.wait_ge(misc_free, count(centred))
                            act.wait_ge(ret_o, count(8 * (l + 1)))
                        act.wait_ge(out_free, count(18 * l + (10 if k == 0 else 18)))
                        for c in HEAD_NORMS[k]:
                            fn(square_at[c], mix[:, c, :], ACT.Square)\
                                .then_inc(own(mix_sq if c == HEAD_NORMS[k][-1] else sb_step), 1)
                    elif what == "roots":
                        act.wait_ge(mix_sums, count(2 * l + k + 1))
                        at = slice(0, 8) if k == 0 else slice(8, 16)
                        fn(mix_roots[:, at], ps[:, MB, at], ACT.Sqrt, bias=eps, scale=1.0 / P)\
                            .then_inc(own(sb_step if k == 0 else mix_root), 1)
                        if k == 0:
                            fn(mix_roots[:, 16:32], ps[:, MB, 16:32], ACT.Sqrt, bias=eps).then_inc(own(mix_root), 1)
                    elif what == "spread":
                        misc[0] += 1
                        if k != 1:
                            c = 0 if k == 0 else 2
                            made[c] = (mixed, 4 * l + (1 if k == 0 else 4))
                            made[c + 1] = (misc_free, misc[0])
                    elif what == "silu":
                        act.wait_ge(unit_evac, count(c0 + len(IN1)))
                        for b in range(2):
                            fn(gr[:, b, :], gr[:, b, :], ACT.Silu).then_inc(own(ret_gate), 1)
                            made[4 + b] = (mixed, 4 * l + 2 + b)
                    elif what == "split":
                        if k == 0:
                            act.wait_ge(unit_done, count(n0 + len(IN1)))
                        c = OUT1[k]
                        act.wait_ge(*made[c])
                        fn(h_hi[:, c, :], mix[:, c, :], ACT.Copy).then_inc(own(h_hi_ready), 1)
                load_root()
                for u in range(KD):
                    next_w()
                    act.wait_ge(unit_evac, count(c0 + len(IN1) + u + 1))
                    square(u, yf[:, u, :])
                root_of_sums()

            def mixer2(l):
                n0, c0 = base2(l) + 3 * KF, inner2(l) + 2 * KF
                g0 = NI * l

                def scores(k):
                    kind, i = ITEMS2[k]
                    g = g0 + k
                    if kind == "dil":
                        act.wait_ge(dil_max, count(16 * l + k + 1))
                        act.wait_ge(item_t, count(g))
                        fn(pb2[:, 0:768], ps[:, S0:S0 + 2, :].rearrange("p a b -> p (a b)")[:, 0:768], ACT.Exp,
                           scale=DA_SCALE, bias=small[:, 11:12], accum_out=small[:, 12:13])\
                            .then_inc(own(dil_s_read), 1)
                    else:
                        j = 8 * l + k - 16
                        w = (i % NT + 1) * P
                        act.wait_ge(sb_s_read, count(j + 1))
                        act.wait_ge(sb_arg, count(j))
                        fn(sb_log[:, :, 0:w], sb_z[:, :, 0:w], ACT.Abs).then_inc(own(sb_step), 1)
                        act.wait_ge(*own.last())
                        fn(sb_log[:, :, 0:w], sb_log[:, :, 0:w], ACT.Exp, scale=-1.0).then_inc(own(sb_step), 1)
                        last = own.last()
                        if k > 16:
                            weights(k - 1)
                        act.wait_ge(*last)
                        fn(sb_log[:, :, 0:w], sb_log[:, :, 0:w], ACT.Ln, bias=one).then_inc(own(sb_ln), 1)

                def weights(k):
                    kind, i = ITEMS2[k]
                    w = (i % NT + 1) * P
                    act.wait_ge(sb_arg, count(8 * l + k - 15))
                    act.wait_ge(item_t, count(g0 + k))
                    fn(pb2[:, 0:2 * w].rearrange("p (a b) -> p a b", a=2), sb_sum[:, :, 0:w], ACT.Exp)\
                        .then_inc(own(item_p), 1)

                def normal(k):
                    act.wait_ge(dil_coef, count(16 * l + k + 1))
                    fn(pb2[:, 0:768], pb2[:, 0:768], ACT.Copy, scale=small[:, 13:14]).then_inc(own(item_p), 1)

                def evac_t(k):
                    kind, i = ITEMS2[k]
                    w = 768 if kind == "dil" else 2 * (i % NT + 1) * P
                    act.wait_ge(item_t, count(g0 + k + 1))
                    act.wait_ge(item_o, count(g0 + k))
                    fn(pt2[:, 0:w], ps[:, T0:T0 + 2, :].rearrange("p a b -> p (a b)")[:, 0:w], ACT.Copy)\
                        .then_inc(own(item_pt), 1)

                for what, k in STEPS2:
                    if what == "unit":
                        if k >= 2:
                            next_w()
                    elif what in "STNE":
                        {"S": scores, "T": evac_t, "N": normal, "E": weights}[what](k)
                act.wait_ge(out_free, count(18 * DEPTH + NI * (l + 1)))
                for c in range(4):
                    src = qk2[:, c, :] if c < 2 else qk2[:, 12 + c - 2, :]
                    fn(s_hi[:, c, :], src, ACT.Copy).then_inc(own(s_hi_ready), 1)
                act.wait_ge(unit_evac, count(c0 + len(IN2)))
                for u in range(4):
                    for c in (2 * u, 2 * u + 8, 2 * u + 1, 2 * u + 9):
                        fn(gate_at(c), gate_at(c), ACT.Sigmoid).then_inc(own(gate2_ready), 1)
                    next_w()
                    if u == 1:
                        act.wait_ge(unit_done, count(n0 + len(IN2)))
                    for c in (2 * u - 2, 2 * u - 1) if u else ():
                        act.wait_ge(mixed2, count(8 * l + c + 1))
                        fn(h_hi[:, c, :], gate_at(c), ACT.Copy).then_inc(own(h_hi_ready), 1)
                for c in (KD - 2, KD - 1):
                    act.wait_ge(mixed2, count(8 * l + c + 1))
                    fn(h_hi[:, c, :], gate_at(c), ACT.Copy).then_inc(own(h_hi_ready), 1)
                for u in range(KD):
                    next_w()

            rtab_in_dram = aps["rtab"].rearrange("p (a b) -> p a b", a=6)

            def retention_turns():
                act.dma_start(rtab[:, 0:2, :], rtab_in_dram[:, 0:2, :]).then_inc(turns_loaded, 16)

            def retention_decays():
                act.dma_start(rtab[:, 2:6, :], rtab_in_dram[:, 2:6, :]).then_inc(rtab_loaded, 16)

            for i in range(4):
                act.dma_start(x[:, 2 * i:2 * i + 2, :], aps["x"][:, 2 * i:2 * i + 2, :]).then_inc(x_loaded[i], 16)
            act.dma_start(tab[:, :], aps["tab"]).then_inc(tab_loaded, 16)
            g1 = lambda l, name: vec1[:, l, V1[name]:V1[name] + KD]
            g2 = lambda l, name: vec2[:, l, V2[name]:V2[name] + KD]

            def other_loads():
                retention_turns()
                act.dma_start(vec1[:, :, 4 * KD:], aps["vec1"][:, :, 4 * KD:]).then_inc(vec_loaded, 16)
                act.dma_start(bmask[:, :], aps["bmask"]).then_inc(rest_loaded, 16)
                act.dma_start(vec2[:, :, :], aps["vec2"]).then_inc(rest_loaded, 16)
                act.dma_start(pool_w[:, :, :, :], aps["pool_w"]).then_inc(rest_loaded, 16)
                retention_decays()

            def lambdas(l):
                act.wait_ge(lam_dots, count(l + 1))
                fn(small[:, 16 + 2 * l:18 + 2 * l], small[:, 16 + 2 * l:18 + 2 * l], ACT.Exp)\
                    .then_inc(own(lam_exp), 1)

            def split_x(gain, n_done, name, value):
                act.wait_ge(unit_done, count(n_done))
                for c in range(KD):
                    if name is None and c == 0:
                        act.wait_ge(gains_loaded, 16)
                    if name is None and c % 2 == 0:
                        act.wait_ge(x_loaded[c // 2], 16)
                    if name is not None:
                        act.wait_ge(name, count(value + c + 1))
                    fn(h_hi[:, c, :], x[:, c, :], ACT.Copy, scale=gain[:, c:c + 1]).then_inc(own(h_hi_ready), 1)
                    square(c, xb(c))
                    if c == 3 or name is None and c == 1:
                        next_w()
                    if name is None and c == 1:
                        other_loads()
                if name is None:
                    act.wait_ge(tab_loaded, 16)
                next_w()
                root_of_sums()

            for _ in range(AHEAD - 1):
                next_w()
            for l in range(DEPTH):
                n0 = base1(l)
                split_x(g1(l, "mix_pre"), n0 - KF, x_ready if l else None, 16 * l - 8)
                if l == 0:
                    for layer in range(DEPTH):
                        lambdas(layer)
                mixer1(l)
                n, c = n0 + len(IN1) + KD, inner1(l) + len(IN1) + KD
                split_x(g1(l, "mlp_pre"), n, x_ready, 16 * l)
                mlp_up1(n, c, l)
                mlp_down(n + 2 * KF, KF * l, mlp_prod)
                if l + 1 < DEPTH:
                    act.wait_ge(s_lo_ready, count(KF * (l + 1)))
                    act.wait_ge(*own.last())
                    retention_turns()
                    retention_decays()
                load_root()
                for b in range(KD):
                    act.wait_ge(down_evac, count(8 * l + b + 1))
                    square(b, yf[:, b, :])
                root_of_sums()
            for l in range(DEPTH):
                n0 = base2(l)
                split_x(g2(l, "ffn1"), n0 - KF, down_evac if l else x_ready, 8 * (DEPTH + 2 * l - 1) if l else 8 * 3)
                mlp_up2(n0, inner2(l), 2 * l)
                mlp_down(n0 + 2 * KF, KF * 2 * l, mlp_prod2)
                split_x(g2(l, "mix"), n0 + 2 * KF, down_evac, 8 * (DEPTH + 2 * l))
                mixer2(l)
                n = n0 + 3 * KF + len(IN2) + 4 + KD
                split_x(g2(l, "ffn2"), n, unit_evac, inner2(l) + 2 * KF + len(IN2) + 4)
                mlp_up2(n, inner2(l) + 2 * KF + len(IN2) + 4 + KD, 2 * l + 1)
                mlp_down(n + 2 * KF, KF * (2 * l + 1), mlp_prod2)
            load_root()
            for c in range(KD):
                act.wait_ge(down_evac, count(8 * (3 * DEPTH - 1) + c + 1))
                square(c, xb(c))
            root_of_sums()

        @block.vector
        def _(dve):
            own = Own(dve, (gains_loaded, 16))
            v = nc.vector
            misc, outs, sums, splits, roots = [0], [0], [0], [0], [0]

            def low_h(c, source, gain=None, i=None):
                i = c if i is None else i
                dve.wait_ge(h_hi_ready, count(8 * splits[0] + i + 1))
                hi = h_hi[:, c, :].bitcast(F32)
                if gain is None:
                    dve.wait_ge(*own.last())
                    v.tensor_tensor(h_lo[:, c, :], source, hi, ALU.subtract).then_inc(own(h_lo_ready), 1)
                else:
                    dve.wait_ge(*own.last())
                    v.scalar_tensor_tensor(h_lo[:, c, :], source, gain[:, c:c + 1], hi, ALU.mult, ALU.subtract)\
                        .then_inc(own(h_lo_ready), 1)
                if i == KD - 1:
                    splits[0] += 1

            def add_square(c):
                if c == 0:
                    return
                dve.wait_ge(sq_ready, count(8 * sums[0] + c + 1))
                dve.wait_ge(*own.last())
                v.tensor_tensor(acc[:, :], sq[:, 0, :] if c == 1 else acc[:, :], sq[:, c % 2, :], ALU.add)\
                    .then_inc(own(acc_ready if c == KD - 1 else sq_used), 1)
                if c == KD - 1:
                    sums[0] += 1

            def factor_in_psum():
                roots[0] += 1
                dve.wait_ge(root_ready, count(roots[0]))
                dve.wait_ge(*own.last())
                v.reciprocal(factor, root).then_inc(own(factor_ready), 1)
                misc[0] += 1
                dve.wait_ge(misc_ready, count(misc[0]))

            def norm_factor():
                factor_in_psum()
                dve.wait_ge(*own.last())
                v.tensor_copy(rstd[:, :], ps[:, MB, :]).then_inc(own(misc_free), 1)

            def prenorm(gain, update=None, lead=0, meanwhile=None):
                for c in range(KD + lead + 1):
                    if update is not None and c < KD:
                        update(c)
                    if 0 <= c - lead < KD:
                        low_h(c - lead, x[:, c - lead, :], gain)
                    if 0 <= c - lead - 1:
                        add_square(c - lead - 1)
                if meanwhile is not None:
                    meanwhile()
                norm_factor()

            def add_normed(gain):
                def update(c):
                    dve.wait_ge(*own.last())
                    v.scalar_tensor_tensor(yf[:, c, :], yf[:, c, :], gain[:, c:c + 1], ps[:, MB, :], ALU.mult,
                                           ALU.mult).then_inc(own(misc_free if c == KD - 1 else vector_step), 1)
                    dve.wait_ge(*own.last())
                    v.tensor_tensor(x[:, c, :], x[:, c, :], yf[:, c, :], ALU.add).then_inc(own(x_ready), 1)
                return update

            down_end = [0]

            def down_block_done(b):
                return (down_done, 7 * downs[0] - 6 + b) if b < KD - 1 else (unit_done, down_end[0])

            def add_half(b):
                dve.wait_ge(*down_block_done(b))
                dve.wait_ge(*own.last())
                v.scalar_tensor_tensor(x[:, b, :], ps[:, b, :], 0.5, x[:, b, :], ALU.mult, ALU.add)\
                    .then_inc(own(down_evac), 1)

            def evac(u_done, bank, dst, by=None, to=unit_evac):
                dve.wait_ge(unit_done, count(u_done))
                dve.wait_ge(*own.last())
                v.tensor_tensor(dst, ps[:, bank, :], rstd[:, :] if by is None else by, ALU.mult).then_inc(own(to), 1)

            def rope(n, bank, dst, ready):
                dve.wait_ge(unit_done, count(n + 1))
                dve.wait_ge(*own.last())
                v.stream_shuffle(shuf[:, :], ps[:, bank, :], [(i + 8) % 16 if i < 16 else i for i in range(32)])\
                    .then_inc(own(vector_step), 1)
                dve.wait_ge(*own.last())
                v.tensor_tensor(dst, ps[:, bank, :], rope_cr[:, :], ALU.mult).then_inc(own(unit_evac), 1)
                dve.wait_ge(*own.last())
                v.tensor_tensor(shuf[:, :], shuf[:, :], rope_sr[:, :], ALU.mult).then_inc(own(vector_step), 1)
                dve.wait_ge(*own.last())
                v.tensor_tensor(dst, dst, shuf[:, :], ALU.add).then_inc(own(ready), 1)

            def rope_tables():
                dve.wait_ge(*own.last())
                v.tensor_tensor(rope_cr[:, :], rope_c, rstd[:, :], ALU.mult).then_inc(own(vector_step), 1)
                dve.wait_ge(*own.last())
                v.tensor_tensor(rope_sr[:, :], rope_s, rstd[:, :], ALU.mult).then_inc(own(vector_step), 1)

            vts = [0]

            def values(n, bank, tmp, dst, backward=False):
                dve.wait_ge(v_done, count(vts[0]))
                evac(n + 1, bank, tmp[:, ::-1] if backward else tmp, to=unit_evac)

            def values_by_token(dst):
                vts[0] += 1
                dve.wait_ge(v_done, count(vts[0]))
                dve.wait_ge(*own.last())
                v.tensor_copy(dst, ps[:, MB, :].rearrange("p (t d) -> p t d", t=NT)).then_inc(own(vtok_ready), 1)

            chunks = [0]

            def low_chunk(i, k):
                kk = k if i is None else i * 4 + k
                dve.wait_ge(s_hi_ready, count(chunks[0] + 1 + kk))
                dve.wait_ge(*own.last())
                v.tensor_tensor(s_lo[:, k % 4, :], prod[:, kk, :], s_hi[:, k % 4, :].bitcast(F32),
                                ALU.subtract).then_inc(own(s_lo_ready), 1)

            def mlp_up1(n0, c0, l):
                dve.wait_ge(*own.last())
                v.memset(upads[:, :, 0:2], 0.0).then_inc(own(vector_step), 1)

                def unit(i, u):
                    k = u if i is None else i * 4 + u
                    up, tp = upads[:, u % 2, :], taps[:, u % 2, :]
                    blk = u // 2 + KF * (u % 2)
                    if i is not None:
                        blk = i * 2 + blk
                    tap = lambda j: vec1[:, l, bass.ds(V1["conv_w"] + j * 2 * KF + blk, 1)]
                    evac(n0 + 1 + k, u % 4, up[:, 2:])
                    dve.wait_ge(tap_ready, count(2 * KF * l + k + 1))
                    dve.wait_ge(*own.last())
                    v.scalar_tensor_tensor(tp, up[:, 1:T + 1], tap(1), tp, ALU.mult, ALU.add)\
                        .then_inc(own(vector_step), 1)
                    dve.wait_ge(*own.last())
                    v.scalar_tensor_tensor(tp, up[:, 0:T], tap(0), tp, ALU.mult, ALU.add).then_inc(own(conv_done), 1)
                    if u % 2:
                        j = u // 2 if i is None else i * 2 + u // 2
                        dve.wait_ge(gelu_ready, count(KF * l + j + 1))
                        dve.wait_ge(*own.last())
                        v.tensor_tensor(prod[:, j, :], taps[:, 0, :], taps[:, 1, :], ALU.mult)\
                            .then_inc(own(mlp_prod), 1)

                for u in range(4):
                    unit(None, u)
                low_chunk(None, 0)
                low_chunk(None, 1)
                with own.loop(KF // 2 - 1, {vector_step: 4, unit_evac: 4, conv_done: 4, mlp_prod: 2}) as i:
                    for u in range(4, 8):
                        unit(i, u)

            def mlp_up2(n0, c0, d):
                def unit(i, u):
                    k = u if i is None else i * 4 + u
                    j = u // 2 if i is None else i * 2 + u // 2
                    if u % 2 == 0:
                        dve.wait_ge(silu_ready, count(KF * d + j))
                        dve.wait_ge(unit_done, count(n0 + 1 + k))
                        dve.wait_ge(*own.last())
                        v.tensor_tensor(gate_s[:, 0, :], ps[:, u % 4, :], rstd[:, :], ALU.mult)\
                            .then_inc(own(unit_evac), 1)
                    else:
                        evac(n0 + 1 + k, u % 4, prod[:, j, :])
                        dve.wait_ge(silu_ready, count(KF * d + j + 1))
                        dve.wait_ge(*own.last())
                        v.tensor_tensor(prod[:, j, :], prod[:, j, :], gate_s[:, 1, :], ALU.mult)\
                            .then_inc(own(mlp_prod2), 1)

                for u in range(4):
                    unit(None, u)
                low_chunk(None, 0)
                low_chunk(None, 1)
                with own.loop(KF // 2 - 1, {unit_evac: 4, mlp_prod2: 2}) as i:
                    for u in range(4, 8):
                        unit(i, u)

            downs = [0]

            def mlp_down(n0):
                for k in range(2, 4):
                    low_chunk(None, k)
                with own.loop(4, {s_lo_ready: 4}) as i:
                    for k in range(4, 8):
                        low_chunk(i, k)
                for k in range(20, 22):
                    low_chunk(None, k)
                chunks[0] += KF
                downs[0] += 1
                down_end[0] = n0 + KF

            def outputs(signal, value, dst, src):
                dve.wait_ge(signal, count(value))
                dve.wait_ge(*own.last())
                v.tensor_copy(dst, src).then_inc(own(out_free), 1)
                outs[0] += 1

            def mixer1(l):
                n0, c0 = base1(l), inner1(l)
                g = vec1[:, l, :]
                neglam, gain = small[:, 20 + l:21 + l], small[:, 24 + l:25 + l]

                def scores(k):
                    w = (k % 4 + 1) * P
                    dve.wait_ge(da_scores, count(16 * l + k + 1))
                    dve.wait_ge(*own.last())
                    v.tensor_reduce(small[:, 0:2], ps[:, S0:S0 + 2, 0:w], AX_X, ALU.max).then_inc(own(vector_step), 1)
                    dve.wait_ge(*own.last())
                    v.tensor_scalar(small[:, 2:4], small[:, 0:2], -DA_SCALE, None, ALU.mult).then_inc(own(da_max), 1)

                def normal(k):
                    w = (k % 4 + 1) * P
                    dve.wait_ge(da_exp, count(2 * (16 * l + k + 1)))
                    dve.wait_ge(*own.last())
                    v.reciprocal(small[:, 6:8], small[:, 4:6]).then_inc(own(vector_step), 1)
                    dve.wait_ge(*own.last())
                    v.tensor_tensor(small[:, 9:10], small[:, 7:8], neglam, ALU.mult).then_inc(own(da_coef), 1)
                    dve.wait_ge(da_second, count(16 * l + k + 1))
                    dve.wait_ge(da_transposed, count(16 * l + k))
                    dve.wait_ge(*own.last())
                    v.scalar_tensor_tensor(comb1[:, 0:w], probs1[:, 0, 0:w], small[:, 6:7], probs1[:, 1, 0:w],
                                           ALU.mult, ALU.add).then_inc(own(da_comb), 1)

                def retention(n):
                    if n in (4, 8):
                        outputs(ret_o, 8 * l + n, mix[:, 4 + n // 4 - 1, :], ps[:, RB, :])
                    if n < 8:
                        hh = n // 2
                        dve.wait_ge(rtab_loaded, 16 * (l + 1))
                        dve.wait_ge(ret_s, count(8 * l + n + 1))
                        dve.wait_ge(ret_o, count(8 * l + n))
                        for j in (2 * (n % 2), 2 * (n % 2) + 1):
                            w = T - j * P
                            dve.wait_ge(*own.last())
                            v.tensor_tensor(sq[:, j % 2, 0:w], ps[:, S0 + j % 2, 0:w], rtab[:, 2 + hh, 0:w],
                                            ALU.mult).then_inc(own(ret_p if j % 2 else vector_step), 1)

                for what, k in STEPS1:
                    if what == "rest":
                        kind, i = IN1[k]
                        bank, n = mixer_bank(k), n0 + k
                        if k == 0:
                            if l == 0:
                                dve.wait_ge(tab_loaded, 16)
                            rope_tables()
                            dve.wait_ge(*own.last())
                            v.memset(upad[:, :, 0:16], 0.0).then_inc(own(vector_step), 1)
                        if kind in ("q", "k"):
                            rope(n, bank, mix[:, i, :] if kind == "q" else k_at(i), rope_ready)
                        elif kind in ("v", "vr"):
                            values(n, bank, vtmp1, None)
                        elif kind in ("qr", "kr"):
                            dst = qkr[:, kind == "kr", :]
                            evac(n + 1, bank, dst)
                            dve.wait_ge(*own.last())
                            v.stream_shuffle(shuf[:, :], dst, [(i + 16) % 32 for i in range(32)])\
                                .then_inc(own(vector_step), 1)
                            dve.wait_ge(turns_loaded, count(16 * (l + 1)))
                            dve.wait_ge(*own.last())
                            v.tensor_tensor(shuf[:, :], shuf[:, :], rtab[:, 1, :], ALU.mult)\
                                .then_inc(own(vector_step), 1)
                            dve.wait_ge(*own.last())
                            v.tensor_tensor(dst, dst, rtab[:, 0, :], ALU.mult).then_inc(own(vector_step), 1)
                            dve.wait_ge(*own.last())
                            v.tensor_tensor(dst, dst, shuf[:, :], ALU.add).then_inc(own(rope_ready), 1)
                        elif kind == "g":
                            evac(n + 1, bank, gr[:, i, :])
                        else:
                            evac(n + 1, bank, upad[:, i, 16:])
                        if l == 0 and k == 4:
                            lambdas()
                    elif what == "vT":
                        kind, i = IN1[k]
                        values_by_token(vtok1[:, :, i + 4 * (kind == "vr"), :])
                    elif what == "S":
                        scores(k)
                    elif what == "N":
                        normal(k)
                    elif what == "O":
                        h, i = divmod(k, 4)
                        outputs(da_out, 16 * l + k + 1, mix[:, h, i * P:(i + 1) * P], ps[:, OB, 0:P])
                    elif what == "R":
                        retention(k)
                    elif what == "pool":
                        b = k
                        u, t0, t1 = upad[:, b, :], ptmp[:, 0, :], ptmp[:, 1, :]
                        dve.wait_ge(*own.last())
                        v.tensor_tensor(t0[:, 1:], u[:, 1:], u[:, :-1], ALU.add).then_inc(own(vector_step), 1)
                        if b == 0:
                            dve.wait_ge(*own.last())
                            v.tensor_tensor(t1[64:, 3:], t0[64:, 3:], t0[64:, 1:-2], ALU.add)\
                                .then_inc(own(vector_step), 1)
                        else:
                            dve.wait_ge(*own.last())
                            v.tensor_tensor(t1[:, 3:], t0[:, 3:], t0[:, 1:-2], ALU.add)\
                                .then_inc(own(vector_step), 1)
                            dve.wait_ge(*own.last())
                            v.tensor_tensor(t0[:, 7:], t1[:, 7:], t1[:, 3:-4], ALU.add)\
                                .then_inc(own(vector_step), 1)
                            dve.wait_ge(*own.last())
                            v.tensor_tensor(t1[64:, 15:], t0[64:, 15:], t0[64:, 7:-8], ALU.add)\
                                .then_inc(own(vector_step), 1)
                        for rows, t in ((slice(0, 64), t0), (slice(64, 128), t1)):
                            dve.wait_ge(*own.last())
                            v.tensor_tensor(t[rows, 16:32], t[rows, 16:32], inv_head[rows, b, :], ALU.mult)\
                                .then_inc(own(vector_step), 1)
                            dve.wait_ge(*own.last())
                            v.tensor_tensor(u[rows, 16:32], t[rows, 16:32], u[rows, 16:32], ALU.subtract)\
                                .then_inc(own(vector_step), 1)
                            inv = tab[rows, TAB["inv_w"][0] + b:TAB["inv_w"][0] + b + 1]
                            dve.wait_ge(*own.last())
                            v.scalar_tensor_tensor(u[rows, 32:], t[rows, 32:], inv, u[rows, 32:], ALU.mult,
                                                   ALU.subtract)\
                                .then_inc(own(vector_step if rows.start == 0 else pooled), 1)
                    elif what == "poolmm":
                        misc[0] += 1
                        dve.wait_ge(misc_ready, count(misc[0]))
                        scale = g[:, V1["pool_scale"] + k:V1["pool_scale"] + k + 1]
                        dve.wait_ge(*own.last())
                        v.tensor_scalar(mix[:, 6 + k, :], ps[:, MB, :], scale, None, ALU.mult)\
                            .then_inc(own(misc_free), 1)
                    elif what == "mean":
                        misc[0] += 1
                        dve.wait_ge(misc_ready, count(misc[0]))
                        dve.wait_ge(*own.last())
                        v.tensor_tensor(mix[:, 4 + k, :], mix[:, 4 + k, :], ps[:, MB, :], ALU.subtract)\
                            .then_inc(own(misc_free), 1)
                    elif what == "roots":
                        dve.wait_ge(mix_root, count(2 * l + k + 1))
                        at = slice(0, 8) if k == 0 else slice(8, 16)
                        dve.wait_ge(*own.last())
                        v.reciprocal(mix_factors[:, at], mix_roots[:, at])\
                            .then_inc(own(vector_step if k == 0 else mix_factor), 1)
                        if k == 0:
                            dve.wait_ge(*own.last())
                            v.reciprocal(mix_factors[:, 16:32], mix_roots[:, 16:32]).then_inc(own(mix_factor), 1)
                    elif what == "spread":
                        misc[0] += 1
                        dve.wait_ge(misc_ready, count(misc[0]))
                        first = (0, 4, 2)[k]
                        for c, bank in ((first, MB), (first + 1, RB if k < 2 else S0 + 1)):
                            by = gain if c < 4 else g[:, V1["ret"] + c - 4:V1["ret"] + c - 3]
                            dve.wait_ge(*own.last())
                            v.scalar_tensor_tensor(mix[:, c, :], mix[:, c, :], by, ps[:, bank, :], ALU.mult,
                                                   ALU.mult)\
                                .then_inc(own(misc_free if bank != MB else vector_step if k == 1 else mixed), 1)
                    elif what == "gated":
                        for b in range(2):
                            dve.wait_ge(ret_gate, count(2 * l + b + 1))
                            dve.wait_ge(*own.last())
                            v.tensor_tensor(mix[:, 4 + b, :], mix[:, 4 + b, :], gr[:, b, :], ALU.mult)\
                                .then_inc(own(mixed), 1)
                    elif what == "split":
                        low_h(OUT1[k], mix[:, OUT1[k], :], None, k)
                for u in range(KD):
                    dve.wait_ge(unit_done, count(n0 + len(IN1) + u + 1))
                    dve.wait_ge(*own.last())
                    v.tensor_copy(yf[:, u, :], ps[:, out_bank(u), :]).then_inc(own(unit_evac), 1)
                    if u:
                        add_square(u - 1)
                add_square(KD - 1)
                factor_in_psum()

            def mixer2(l):
                n0, c0 = base2(l) + 3 * KF, inner2(l) + 2 * KF
                g0 = NI * l
                wide = ps[:, S0:S0 + 2, :].rearrange("p a b -> p (a b)")[:, 0:768]

                def scores(k):
                    kind, i = ITEMS2[k]
                    dve.wait_ge(item_s, count(g0 + k + 1))
                    if kind == "dil":
                        dve.wait_ge(*own.last())
                        v.tensor_reduce(small[:, 10:11], wide, AX_X, ALU.max).then_inc(own(vector_step), 1)
                        dve.wait_ge(*own.last())
                        v.tensor_scalar(small[:, 11:12], small[:, 10:11], -DA_SCALE, None, ALU.mult)\
                            .then_inc(own(dil_max), 1)
                    else:
                        w = (i % NT + 1) * P
                        z, total = sb_z[:, :, 0:w], sb_sum[:, :, 0:w]
                        dve.wait_ge(sb_ln, count(8 * l + k - 16))
                        dve.wait_ge(*own.last())
                        v.tensor_scalar(z, ps[:, S0:S0 + 2, 0:w], DA_SCALE, None, ALU.mult).then_inc(own(sb_s_read), 1)
                        dve.wait_ge(item_p, count(g0 + k))
                        dve.wait_ge(*own.last())
                        v.tensor_scalar(total, z, 0.0, None, ALU.max).then_inc(own(vector_step), 1)
                        dve.wait_ge(sb_ln, count(8 * l + k - 15))
                        for hh in range(2):
                            dve.wait_ge(*own.last())
                            v.tensor_tensor_scan(total[:, hh, :], total[:, hh, :], sb_log[:, hh, 0:w], 0.0, ALU.add,
                                                 ALU.add).then_inc(own(vector_step), 1)
                        dve.wait_ge(*own.last())
                        v.tensor_tensor(total, z, total, ALU.subtract).then_inc(own(sb_arg), 1)

                def normal(k):
                    kind, i = ITEMS2[k]
                    if kind == "dil":
                        dve.wait_ge(dil_s_read, count(16 * l + k + 1))
                        dve.wait_ge(*own.last())
                        v.reciprocal(small[:, 13:14], small[:, 12:13]).then_inc(own(dil_coef), 1)

                def output(k):
                    kind, i = ITEMS2[k]
                    h, r = divmod(i, NT)
                    half = slice(64 * (h % 2), 64 * (h % 2) + 64) if kind == "dil" else slice(0, P)
                    dst = qk2[half, h // 2, r:T:NT] if kind == "dil" else qk2[:, 12 + h, r * P:(r + 1) * P]
                    outputs(item_o, g0 + k + 1, dst, ps[half, OB, 0:P])

                for what, k in STEPS2:
                    if what == "rest":
                        kind, g, b = IN2[k]
                        bank, n = mixer_bank(k), n0 + k
                        if k == 0:
                            rope_tables()
                        if kind in ("q", "k"):
                            rope(n, bank, qk2[:, 2 * g + b + 6 * (kind == "k"), :], rope_ready)
                        elif kind == "v":
                            values(n, bank, vtmp2, None)
                        elif kind == "vs":
                            values(n, bank, vtmp2, None, backward=True)
                        elif kind == "qs":
                            evac(n + 1, bank, qk2[:, 12 + b, :])
                        elif kind == "ks":
                            evac(n + 1, bank, qk2[:, 14 + b, ::-1])
                        else:
                            if b == 14:
                                dve.wait_ge(item_s, count(g0 + NI))
                            evac(n + 1, bank, gate_at(b))
                    elif what == "vT":
                        kind, g, b = IN2[k]
                        values_by_token(vtok2[:, :, 6 + b if kind == "vs" else 2 * g + b, :])
                    elif what in "SNO":
                        {"S": scores, "N": normal, "O": output}[what](k)
                for c in range(4):
                    src = qk2[:, c, :] if c < 2 else qk2[:, 12 + c - 2, :]
                    dve.wait_ge(s_hi_ready, count(chunks[0] + c + 1))
                    dve.wait_ge(*own.last())
                    v.tensor_tensor(s_lo[:, c, :], src, s_hi[:, c, :].bitcast(F32), ALU.subtract)\
                        .then_inc(own(s_lo_ready), 1)
                chunks[0] += 4
                for u in range(4):
                    dve.wait_ge(unit_done, count(n0 + len(IN2) + u + 1))
                    for j in range(4):
                        c = 2 * u + j // 2
                        gate = gate_at(c + 8 * (j % 2))
                        dve.wait_ge(gate2_ready, count(16 * l + 4 * u + j + 1))
                        dve.wait_ge(*own.last())
                        v.tensor_tensor(gate, ps[:, 4 * (u % 2) + j, :], gate, ALU.mult)\
                            .then_inc(own(unit_evac if j == 3 else vector_step), 1)
                    for c in (2 * u, 2 * u + 1):
                        dve.wait_ge(*own.last())
                        v.tensor_tensor(gate_at(c), gate_at(c), gate_at(c + 8), ALU.add).then_inc(own(mixed2), 1)
                    for c in (2 * u - 2, 2 * u - 1) if u else ():
                        low_h(c, gate_at(c))
                for c in (KD - 2, KD - 1):
                    low_h(c, gate_at(c))
                for c in range(KD):
                    dve.wait_ge(unit_done, count(n0 + len(IN2) + 4 + c + 1))
                    dve.wait_ge(*own.last())
                    v.tensor_tensor(x[:, c, :], x[:, c, :], ps[:, out_bank2(c), :], ALU.add).then_inc(own(unit_evac), 1)

            def lambda_dots():
                dve.wait_ge(vec_loaded, 16)
                for layer in range(DEPTH):
                    g = vec1[:, layer, :]
                    for m in range(2):
                        at = V1["lq1"] + 128 * m
                        dve.wait_ge(*own.last())
                        v.tensor_tensor(shuf[:, 0:64], g[:, at:at + 64], g[:, at + 64:at + 128], ALU.mult)\
                            .then_inc(own(vector_step), 1)
                        dve.wait_ge(*own.last())
                        v.reduce_sum(small[:, 16 + 2 * layer + m:17 + 2 * layer + m], shuf[:, 0:64], axis=AX_X)\
                            .then_inc(own(lam_dots if m else vector_step), 1)

            def lambdas():
                dve.wait_ge(rest_loaded, 48)
                for layer in range(DEPTH):
                    g = vec1[:, layer, :]
                    dve.wait_ge(lam_exp, count(layer + 1))
                    dve.wait_ge(*own.last())
                    v.tensor_tensor(small[:, 20 + layer:21 + layer], small[:, 17 + 2 * layer:18 + 2 * layer],
                                    small[:, 16 + 2 * layer:17 + 2 * layer], ALU.subtract).then_inc(own(vector_step), 1)
                    dve.wait_ge(*own.last())
                    v.tensor_scalar(small[:, 20 + layer:21 + layer], small[:, 20 + layer:21 + layer], LAM_INIT[layer], None,
                                    ALU.subtract).then_inc(own(vector_step), 1)
                    dve.wait_ge(*own.last())
                    v.tensor_scalar(small[:, 24 + layer:25 + layer], g[:, V1["subln"]:V1["subln"] + 1], 1.0 - LAM_INIT[layer],
                                    None, ALU.mult).then_inc(own(vector_step), 1)

            def gains(vectors, at):
                return vectors[:, at:at + KD]

            prenorm(gains(vec1[:, 0, :], V1["mix_pre"]), meanwhile=lambda_dots)
            for l in range(DEPTH):
                g = vec1[:, l, :]
                mixer1(l)
                n, c = base1(l) + len(IN1) + KD, inner1(l) + len(IN1) + KD
                prenorm(gains(g, V1["mlp_pre"]), add_normed(gains(g, V1["mix_post"])), 1)
                mlp_up1(n, c, l)
                mlp_down(n + 2 * KF)
                for b in range(KD):
                    dve.wait_ge(*down_block_done(b))
                    dve.wait_ge(*own.last())
                    v.tensor_copy(yf[:, b, :], ps[:, b, :]).then_inc(own(down_evac), 1)
                    if b:
                        add_square(b - 1)
                add_square(KD - 1)
                factor_in_psum()
                following = gains(vec1[:, l + 1, :], V1["mix_pre"]) if l + 1 < DEPTH else gains(vec2[:, 0, :], V2["ffn1"])
                prenorm(following, add_normed(gains(g, V1["mlp_post"])), 1)
            for l in range(DEPTH):
                n = base2(l)
                mlp_up2(n, 0, 2 * l)
                mlp_down(n + 2 * KF)
                prenorm(gains(vec2[:, l, :], V2["mix"]), add_half, 2)
                mixer2(l)
                n = n + 3 * KF + len(IN2) + 4 + KD
                prenorm(gains(vec2[:, l, :], V2["ffn2"]))
                mlp_up2(n, 0, 2 * l + 1)
                mlp_down(n + 2 * KF)
                if l + 1 < DEPTH:
                    prenorm(gains(vec2[:, l + 1, :], V2["ffn1"]), add_half, 2)
            for b in range(KD):
                add_half(b)
                if b:
                    add_square(b - 1)
            add_square(KD - 1)
            norm_factor()
            final = vec2[:, 0, V2["final"]:V2["final"] + KD]
            for c in range(KD):
                dve.wait_ge(*own.last())
                v.scalar_tensor_tensor(x[:, c, :], x[:, c, :], final[:, c:c + 1], rstd[:, :], ALU.mult, ALU.mult)\
                    .then_inc(own(y_ready), 1)


def kernel(**inputs):
    import concourse.bacc as bacc
    from concourse.bass_utils import run_bass_kernel_spmd

    a = {k: np.ascontiguousarray(v) for k, v in inputs.items()}

    def blocks(w, order=None):
        k, f = w.shape
        tiles = w.reshape(k // P, P, f // P, P).transpose(2, 1, 0, 3).reshape(f // P, P, (k // P) * P)
        return tiles if order is None else tiles[order]

    def paired(w0, w1):
        return np.stack([blocks(w0), blocks(w1)], 1).reshape(-1, P, UW)

    def rows(w):
        return w.reshape(-1, P, UW)

    units = []
    for l in range(DEPTH):
        units.append(blocks(a["w_in"][l], [IN1_COLUMN[k] + i for k, i in IN1]))
        units.append(blocks(a["w_out"][l]))
        units.append(paired(a["w_up"][l][:, :FF], a["w_up"][l][:, FF:]))
        units.append(rows(a["w_down"][l]))
    for l in range(DEPTH):
        units.append(paired(a["ffn1_w_gate_2"][l], a["ffn1_w_up_2"][l]))
        units.append(rows(a["ffn1_w_down_2"][l]))
        units.append(blocks(a["w_in_2"][l], [IN2_COLUMN[k] + 2 * g + b for k, g, b in IN2]))
        both = np.stack([blocks(a["w_proj_dil_2"][l]), blocks(a["w_proj_sb_2"][l])], 2)
        units.append(both.reshape(4, 2, P, 2 * 2 * P).transpose(0, 2, 1, 3).reshape(4, P, UW))
        units.append(blocks(a["w_out_2"][l]))
        units.append(paired(a["ffn2_w_gate_2"][l], a["ffn2_w_up_2"][l]))
        units.append(rows(a["ffn2_w_down_2"][l]))
    w = np.concatenate(units)
    assert w.shape == (UNITS, P, UW)

    def columns(v):
        return v.reshape(-1, P).T

    def everywhere(v):
        return np.broadcast_to(v[None, :], (P, v.shape[0]))

    vec1 = np.stack([np.concatenate(
        [columns(a[n][l]) for n in ("norm_mix_pre", "norm_mix_post", "norm_mlp_pre", "norm_mlp_post", "diff_subln",
                                    "ret_norm", "pool_scale", "conv_b")]
        + [columns(a["conv_w"][l].reshape(-1))]
        + [everywhere(a[n][l]) for n in ("lambda_q1", "lambda_k1", "lambda_q2", "lambda_k2")], 1)
        for l in range(DEPTH)], 1)
    vec2 = np.stack([np.concatenate(
        [columns(a[n][l]) for n in ("norm_ffn1_2", "norm_mix_2", "norm_ffn2_2")] + [columns(a["norm_final_2"])], 1)
        for l in range(DEPTH)], 1)
    pool_w = a["pool_w"].reshape(DEPTH, 2, P, 64).transpose(2, 0, 1, 3)
    tab, rtab, bmask = constants()
    arrays = {
        "x": a["x"][0].T.reshape(KD, P, T).transpose(1, 0, 2), "w": w, "vec1": vec1, "vec2": vec2,
        "pool_w": pool_w, "tab": tab, "rtab": rtab, "bmask": bmask.astype(mybir.dt.np(BF16)),
    }
    nc = bacc.Bacc("TRN2", target_bir_lowering=False, num_devices=1)
    aps, ins = {}, {}
    for name, v in arrays.items():
        ins["in_" + name] = np.ascontiguousarray(v)
        aps[name] = nc.dram_tensor("in_" + name, v.shape, mybir.dt.from_np(v.dtype), kind="ExternalInput").ap()
    aps["out"] = nc.dram_tensor("out", (P, KD, T), F32, kind="ExternalOutput").ap()
    program(nc, aps)
    got = run_bass_kernel_spmd(nc, [ins], core_ids=[0]).results[0]["out"]
    return np.ascontiguousarray(got.transpose(2, 1, 0).reshape(1, T, D))
```
